# Optimizing a Trainium2 kernel written in Bass

```python
import jax, jax.numpy as jnp
from jax import lax
import numpy as np

D_MODEL = 1024
BATCH = 1
SEQ = 1024
DEPTH = 1

HEAD_DIM = 64
FOX_HEADS = 8
SWA_HEADS = 8
SWA_KV_HEADS = 2
SWA_GROUP = SWA_HEADS // SWA_KV_HEADS
MIX_WIDTH = (FOX_HEADS + SWA_HEADS) * HEAD_DIM
Q_BLOCK = 128
WINDOW = 128
FOX_Q_W = FOX_HEADS * HEAD_DIM
FOX_K_W = FOX_HEADS * HEAD_DIM
FOX_V_W = FOX_HEADS * HEAD_DIM
FOX_F_W = FOX_HEADS
SWA_Q_W = SWA_HEADS * HEAD_DIM
SWA_K_W = SWA_KV_HEADS * HEAD_DIM
SWA_V_W = SWA_KV_HEADS * HEAD_DIM
IN_WIDTH = FOX_Q_W + FOX_K_W + FOX_V_W + FOX_F_W + SWA_Q_W + SWA_K_W + SWA_V_W
PEER_HEADS = 8
PEER_QUERY_DIM = 256
PEER_HALF = PEER_QUERY_DIM // 2
N_KEYS = 128
N_EXPERTS = N_KEYS * N_KEYS
PEER_TOPK = 16
PEER_CHUNK = 128
N_MOD = 6
RMS_EPS = 1e-6
NEG_INF = -1e30

kernel_name = "hymba_fox_swa_peer_block"

def rmsnorm(x, g):
    xf = x.astype(jnp.float32)
    y = xf * lax.rsqrt(jnp.mean(xf * xf, axis=-1, keepdims=True) + RMS_EPS)
    return y.astype(x.dtype) * g

def alibi_slopes(n):
    return jnp.exp2(-8.0 * jnp.arange(1, n + 1, dtype=jnp.float32) / n)

def fox_attention(q, k, v, f_logit):
    B, S, H, Dh = q.shape
    nb = S // Q_BLOCK
    F = jnp.cumsum(jax.nn.log_sigmoid(f_logit.astype(jnp.float32)), axis=1)
    Fk = F.transpose(0, 2, 1)
    kpos = jnp.arange(S)
    scale = Dh ** -0.5

    def block(i):
        start = i * Q_BLOCK
        qb = lax.dynamic_slice_in_dim(q, start, Q_BLOCK, axis=1)
        Fq = lax.dynamic_slice_in_dim(Fk, start, Q_BLOCK, axis=2)
        s = jnp.einsum('bqhd,bkhd->bhqk', qb, k).astype(jnp.float32) * scale
        s = s + Fq[..., :, None] - Fk[..., None, :]
        qpos = start + jnp.arange(Q_BLOCK)
        s = jnp.where(kpos[None, :] <= qpos[:, None], s, NEG_INF)
        p = jax.nn.softmax(s, axis=-1).astype(v.dtype)
        return jnp.einsum('bhqk,bkhd->bqhd', p, v)

    out = lax.map(block, jnp.arange(nb))
    return out.transpose(1, 0, 2, 3, 4).reshape(B, S, H * Dh)

def swa_attention(q, k, v, sinks):
    B, S = q.shape[0], q.shape[1]
    nb = S // WINDOW
    scale = HEAD_DIM ** -0.5
    qb = q.reshape(B, nb, WINDOW, SWA_KV_HEADS, SWA_GROUP, HEAD_DIM)

    def band(t):
        tp = jnp.pad(t, ((0, 0), (WINDOW, 0), (0, 0), (0, 0)))
        prev = tp[:, :S].reshape(B, nb, WINDOW, SWA_KV_HEADS, HEAD_DIM)
        cur = t.reshape(B, nb, WINDOW, SWA_KV_HEADS, HEAD_DIM)
        return jnp.concatenate([prev, cur], axis=2)

    kb, vb = band(k), band(v)
    s = jnp.einsum('bnqkgd,bnjkd->bnkgqj', qb, kb).astype(jnp.float32) * scale
    r = jnp.arange(WINDOW)[:, None]
    j = jnp.arange(2 * WINDOW)[None, :]
    dist = r + WINDOW - j
    valid = (dist >= 0) & (dist < WINDOW)
    not_pad = (jnp.arange(nb)[:, None] * WINDOW - WINDOW + jnp.arange(2 * WINDOW)[None, :]) >= 0
    mask = valid[None] & not_pad[:, None, :]
    slopes = alibi_slopes(SWA_HEADS).reshape(SWA_KV_HEADS, SWA_GROUP)
    s = s - slopes[:, :, None, None] * dist.astype(jnp.float32)
    s = jnp.where(mask[None, :, None, None], s, NEG_INF)
    sink = jnp.broadcast_to(sinks.astype(jnp.float32).reshape(SWA_KV_HEADS, SWA_GROUP, 1, 1),
                            s.shape[:-1] + (1,))
    p = jax.nn.softmax(jnp.concatenate([s, sink], axis=-1), axis=-1)[..., :-1]
    out = jnp.einsum('bnkgqj,bnjkd->bnqkgd', p.astype(v.dtype), vb)
    return out.reshape(B, S, SWA_HEADS * HEAD_DIM)

def peer_ffn(h, w_query, sub_keys, w_u, w_v):
    B, S, D = h.shape
    T = B * S
    hf = h.reshape(T, D)
    q = (hf @ w_query).reshape(T, PEER_HEADS, 2, PEER_HALF)
    sc = jnp.einsum('thpd,hpkd->thpk', q, sub_keys).astype(jnp.float32)
    sv, si = lax.top_k(sc, PEER_TOPK)
    cand = sv[:, :, 0, :, None] + sv[:, :, 1, None, :]
    cv, ci = lax.top_k(cand.reshape(T, PEER_HEADS, PEER_TOPK * PEER_TOPK), PEER_TOPK)
    i1 = jnp.take_along_axis(si[:, :, 0, :], ci // PEER_TOPK, axis=-1)
    i2 = jnp.take_along_axis(si[:, :, 1, :], ci % PEER_TOPK, axis=-1)
    experts = i1 * N_KEYS + i2
    gates = jax.nn.softmax(cv, axis=-1)
    nc = T // PEER_CHUNK
    experts = experts.reshape(nc, PEER_CHUNK, PEER_HEADS * PEER_TOPK)
    gates = gates.reshape(nc, PEER_CHUNK, PEER_HEADS * PEER_TOPK).astype(h.dtype)

    def chunk(args):
        hc, ec, gc = args
        u = jnp.take(w_u, ec, axis=0)
        a = jax.nn.gelu(jnp.einsum('cd,ced->ce', hc, u)) * gc
        vv = jnp.take(w_v, ec, axis=0)
        return jnp.einsum('ce,ced->cd', a, vv)

    out = lax.map(chunk, (hf.reshape(nc, PEER_CHUNK, D), experts, gates))
    return out.reshape(B, S, D)

def setup_inputs(seed: int = 0) -> dict:
    key = jax.random.key(seed)
    ks = jax.random.split(key, 16)
    D = D_MODEL
    nrm = jax.random.normal
    f32 = jnp.float32
    return {
        "x": nrm(ks[0], (BATCH, SEQ, D), f32),
        "c": nrm(ks[1], (BATCH, D), f32),
        "w_ada": nrm(ks[2], (DEPTH, D, N_MOD * D), f32) * (0.5 * D ** -0.5),
        "b_ada": nrm(ks[3], (DEPTH, N_MOD * D), f32) * 0.1,
        "g_pre_mix": 1.0 + 0.05 * nrm(ks[4], (DEPTH, D), f32),
        "g_post_mix": 1.0 + 0.05 * nrm(ks[5], (DEPTH, D), f32),
        "g_pre_ffn": 1.0 + 0.05 * nrm(ks[6], (DEPTH, D), f32),
        "g_post_ffn": 1.0 + 0.05 * nrm(ks[7], (DEPTH, D), f32),
        "w_in": nrm(ks[8], (DEPTH, D, IN_WIDTH), f32) * D ** -0.5,
        "b_fgate": 3.0 + 0.5 * nrm(ks[9], (DEPTH, FOX_HEADS), f32),
        "swa_sinks": 0.5 * nrm(ks[10], (DEPTH, SWA_HEADS), f32),
        "w_out": nrm(ks[11], (DEPTH, MIX_WIDTH, D), f32) * MIX_WIDTH ** -0.5,
        "w_query": nrm(ks[12], (DEPTH, D, PEER_HEADS * PEER_QUERY_DIM), f32) * D ** -0.5,
        "sub_keys": nrm(ks[13], (DEPTH, PEER_HEADS, 2, N_KEYS, PEER_HALF), f32) * PEER_HALF ** -0.5,
        "w_u": nrm(ks[14], (DEPTH, N_EXPERTS, D), f32) * D ** -0.5,
        "w_v": nrm(ks[15], (DEPTH, N_EXPERTS, D), f32) * D ** -0.5,
    }

def reference(x, c, w_ada, b_ada, g_pre_mix, g_post_mix, g_pre_ffn, g_post_ffn,
              w_in, b_fgate, swa_sinks, w_out, w_query, sub_keys, w_u, w_v):
    B, S, _ = x.shape
    s1 = FOX_Q_W
    s2 = s1 + FOX_K_W
    s3 = s2 + FOX_V_W
    s4 = s3 + FOX_F_W
    s5 = s4 + SWA_Q_W
    s6 = s5 + SWA_K_W
    for l in range(DEPTH):
        mod = jax.nn.silu(c) @ w_ada[l] + b_ada[l]
        sh1, sc1, gt1, sh2, sc2, gt2 = [m[:, None, :] for m in jnp.split(mod, N_MOD, axis=-1)]

        h = rmsnorm(x, g_pre_mix[l]) * (1 + sc1) + sh1
        proj = h @ w_in[l]
        fq, fk, fv, ff, sq, sk, sv = jnp.split(proj, [s1, s2, s3, s4, s5, s6], axis=-1)
        fox = fox_attention(fq.reshape(B, S, FOX_HEADS, HEAD_DIM),
                            fk.reshape(B, S, FOX_HEADS, HEAD_DIM),
                            fv.reshape(B, S, FOX_HEADS, HEAD_DIM),
                            ff + b_fgate[l])
        swa = swa_attention(sq.reshape(B, S, SWA_HEADS, HEAD_DIM),
                            sk.reshape(B, S, SWA_KV_HEADS, HEAD_DIM),
                            sv.reshape(B, S, SWA_KV_HEADS, HEAD_DIM),
                            swa_sinks[l])
        y = jnp.concatenate([fox, swa], axis=-1) @ w_out[l]
        x = x + gt1 * rmsnorm(y, g_post_mix[l])

        h = rmsnorm(x, g_pre_ffn[l]) * (1 + sc2) + sh2
        y = peer_ffn(h, w_query[l], sub_keys[l], w_u[l], w_v[l])
        x = x + gt2 * rmsnorm(y, g_post_ffn[l])
    return x


_drawn_inputs = setup_inputs


def setup_inputs(seed=0):
    import zlib

    import numpy as np

    out = dict(_drawn_inputs(seed))
    spreads = {}
    factors = {'g_post_ffn': 4.009}
    for name, (base, spread) in spreads.items():
        noise = np.random.default_rng([zlib.crc32(name.encode()), seed]).standard_normal(out[name].shape)
        drawn = base * np.exp(spread * noise) if base else spread * noise
        out[name] = __import__('jax').numpy.asarray(drawn.astype(out[name].dtype))
    for name, factor in factors.items():
        out[name] = (out[name] * factor).astype(out[name].dtype)
    return out
```

```python
from contextlib import ExitStack

import numpy as np

import concourse.bass as bass
from concourse import mybir

F32 = mybir.dt.float32
F16 = mybir.dt.float16
U32 = mybir.dt.uint32
ALU = mybir.AluOpType
ACT = mybir.ActivationFunctionType
AX_X = mybir.AxisListType.X

P = 128
BANK = 512
D = 1024
T = 1024
KD = D // P
TT = T // P
N_MOD = 6
HD = 64
FOX_H, SWA_H, SWA_KV = 8, 8, 2
SWA_GROUP = SWA_H // SWA_KV
AUG = HD + 2
COL_FV = 2 * FOX_H * HD
COL_FF = 3 * FOX_H * HD
COL_SQ = COL_FF + FOX_H
COL_SK = COL_SQ + SWA_H * HD
COL_SV = COL_SK + SWA_KV * HD
IN_W = COL_SV + SWA_KV * HD
V_W = (FOX_H + SWA_KV) * HD
PH = 8
NG = 2 * PH
NK = 128
TOPK = 16
SLOTS = PH * TOPK
N_EXP = NK * NK
EPS = 1e-6
NEG = -1e30
TAKEN = -3.0e38
SCALE = HD ** -0.5

S_H = 16.0
S_U = 64.0
S_A = 64.0
S_V = 64.0


def ctx_tools(nc, ctx):
    def sb(name, shape, dt=F32):
        return ctx.enter_context(nc.sbuf_tensor(name, shape, dt))

    def ps(name, shape, dt=F32):
        return ctx.enter_context(nc.psum_tensor(name, shape, dt))

    def sem(name):
        return ctx.enter_context(nc.semaphore(name))

    return sb, ps, sem


def turns(eng, count, body):
    body(0)
    with eng.Fori(1, count) as i:
        body(i)


def behind(eng, sem, value):
    if not isinstance(value, int) or value > 0:
        eng.wait_ge(sem, value)


class Chain:

    def __init__(self, eng, sem, start=0, waited=None):
        self.eng, self.sem, self.n, self.start, self.waited = eng, sem, 0, start, waited

    def wait(self, ins):
        ins.then_inc(self.sem, 1)
        self.n += 1
        self.eng.wait_ge(self.sem, self.start + self.n)

    def wait_alone(self, ins):
        self.wait(ins)
        self.eng.sem_inc(self.waited, 1)


def modulation(nc, dram, kept):
    SLICE = BANK
    NS = N_MOD * D // SLICE
    RING = 2
    with ExitStack() as ctx:
        sb, ps, sem = ctx_tools(nc, ctx)
        c_raw = sb("c_raw", [P, KD])
        c_silu = sb("c_silu", [P, KD])
        c_wide = sb("c_wide", [P, KD, P])
        w = sb("w_ada_ring", [P, RING, KD, SLICE])
        gains = sb("gains", [P, 4, D])
        mod = kept["mod"]
        out = [ps(f"mod_ps{i}", [P, BANK]) for i in range(RING)]
        small_in, silu_done, wide_done = sem("m_small_in"), sem("m_silu"), sem("m_wide")
        w_in = [sem(f"m_w_in{i}") for i in range(RING)]
        slice_made, slice_kept, rows = sem("m_slice_made"), sem("m_slice_kept"), sem("m_rows")
        block = ctx.enter_context(nc.Block())
        w_view = dram["w_ada"][0].rearrange("(p k) n -> p k n", k=KD)

        @block.sync
        def _(sp):
            sp.dma_start(c_raw[:, :], dram["c"].rearrange("b (p k) -> (b p) k", k=KD)).then_inc(small_in, 16)
            sp.dma_start(mod[:, :], dram["b_ada"][0:1, :].broadcast_to([P, N_MOD * D])).then_inc(small_in, 16)
            for i, name in enumerate(("g_pre_mix", "g_post_mix", "g_pre_ffn", "g_post_ffn")):
                sp.dma_start(gains[:, i, :], dram[name][0:1, :].broadcast_to([P, D])).then_inc(small_in, 16)
            for n in range(RING):
                sp.dma_start(w[:, n], w_view[:, :, n * SLICE:(n + 1) * SLICE]).then_inc(w_in[n], 16)
            with sp.Fori(0, NS // RING - 1) as it:
                for n in range(RING):
                    sp.wait_ge(slice_made, it * RING + n + 1)
                    sp.dma_start(w[:, n], w_view[:, :, bass.ds((it * RING + RING + n) * SLICE, SLICE)]) \
                        .then_inc(w_in[n], 16)

        @block.scalar
        def _(act):
            act.wait_ge(small_in, 96)
            nc.scalar.activation(c_silu[:, :], c_raw[:, :], ACT.Silu).then_inc(silu_done, 1)

        @block.tensor
        def _(pe):
            pe.wait_ge(wide_done, 1)
            with pe.Fori(0, NS // RING) as it:
                for n in range(RING):
                    pe.wait_ge(w_in[n], 16 * it + 16)
                    pe.wait_ge(slice_kept, it * RING + n + 1)
                    for k in range(KD):
                        mm = nc.tensor.matmul(out[n][:, :], c_wide[:, k, :], w[:, n, k, :],
                                              start=(k == 0), stop=(k == KD - 1))
                    mm.then_inc(slice_made, 1)

        @block.vector
        def _(dve):
            dve.wait_ge(silu_done, 1)
            nc.vector.tensor_copy(c_wide[:, :, :], c_silu[:, :, None].broadcast_to([P, KD, P])) \
                .then_inc(wide_done, 1)
            dve.sem_inc(slice_kept, RING)
            dve.wait_ge(small_in, 96)
            with dve.Fori(0, NS // RING) as it:
                for n in range(RING):
                    dve.wait_ge(slice_made, it * RING + n + 1)
                    col = bass.ds((it * RING + n) * SLICE, SLICE)
                    nc.vector.tensor_tensor(mod[:, col], out[n][:, :], mod[:, col], ALU.add) \
                        .then_inc(slice_kept, 1)
            dve.wait_ge(slice_kept, RING + NS)
            for i, (m, g) in enumerate(((1, 0), (4, 2))):
                row = mod[:, m * D:(m + 1) * D]
                nc.vector.scalar_tensor_tensor(row, row, 1.0, gains[:, g, :], ALU.add, ALU.mult).then_inc(rows, 1)
            for i, (m, g) in enumerate(((2, 1), (5, 3))):
                row = mod[:, m * D:(m + 1) * D]
                nc.vector.tensor_tensor(row, row, gains[:, g, :], ALU.mult).then_inc(rows, 1)
            dve.wait_ge(rows, 4)


def norm_and_turn(nc, kept, tag, scale_row, shift_row, outputs):
    x, ident = kept["x"], kept["ident"]
    h_turned, h_hi, h_lo = outputs
    with ExitStack() as ctx:
        sb, ps, sem = ctx_tools(nc, ctx)
        squares = sb(f"{tag}_sq", [P, D])
        sums, var, root, inv, tmp = (sb(f"{tag}_{n}", [P, TT]) for n in ("sum", "var", "root", "inv", "tmp"))
        h = sb(f"{tag}_h", [P, 2, D])
        turned = [ps(f"{tag}_ps{i}", [P, 2, BANK]) for i in range(2)]
        squared, var_made, root_made, steps = (sem(f"{tag}_{n}") for n in ("s_sq", "s_var", "s_root", "s_step"))
        h_made, h_turned_sem, hi_made, kept_sem = (sem(f"{tag}_{n}") for n in ("s_h", "s_t", "s_hi", "s_k"))
        block = ctx.enter_context(nc.Block())

        @block.scalar
        def _(act):
            for t in range(TT):
                if t:
                    act.wait_ge(squared, t)
                nc.scalar.activation(squares[:, :], x[:, t, :], ACT.Square,
                                     accum_out=sums[:, t:t + 1]).then_inc(squared, 1)
            act.wait_ge(var_made, 1)
            nc.scalar.activation(root[:, :], var[:, :], ACT.Sqrt).then_inc(root_made, 1)
            for t in range(TT):
                act.wait_ge(h_turned_sem, t + 1)
                src = turned[t % 2][:, :, :].rearrange("p a (k c) -> p (a k) c", c=P)
                if h_hi is None:
                    nc.scalar.copy(h_turned[:, :, t * P:(t + 1) * P], src).then_inc(kept_sem, 1)
                else:
                    nc.scalar.activation(h_hi[:, :, t * P:(t + 1) * P], src, ACT.Copy, scale=S_H) \
                        .then_inc(hi_made, 1)

        @block.vector
        def _(dve):
            ch = Chain(dve, steps)
            dve.wait_ge(squared, TT)
            nc.vector.tensor_scalar(var[:, :], sums[:, :], 1.0 / D, EPS, ALU.mult, ALU.add).then_inc(var_made, 1)
            dve.wait_ge(root_made, 1)
            ch.wait(nc.vector.reciprocal(inv[:, :], root[:, :]))
            dve.wait_ge(var_made, 1)
            ch.wait(nc.vector.tensor_tensor(tmp[:, :], inv[:, :], inv[:, :], ALU.mult))
            ch.wait(nc.vector.tensor_tensor(tmp[:, :], tmp[:, :], var[:, :], ALU.mult))
            ch.wait(nc.vector.tensor_scalar(tmp[:, :], tmp[:, :], -0.5, 1.5, ALU.mult, ALU.add))
            ch.wait(nc.vector.tensor_tensor(inv[:, :], inv[:, :], tmp[:, :], ALU.mult))

            def keep(t):
                src = turned[t % 2][:, :, :].rearrange("p a (k c) -> p (a k) c", c=P)
                if h_hi is not None:
                    dve.wait_ge(hi_made, t + 1)
                    if h_turned is not None:
                        nc.vector.tensor_copy(h_turned[:, :, t * P:(t + 1) * P], src)
                    nc.vector.scalar_tensor_tensor(h_lo[:, :, t * P:(t + 1) * P], src, S_H,
                                                   h_hi[:, :, t * P:(t + 1) * P], ALU.mult, ALU.subtract) \
                        .then_inc(kept_sem, 1)

            for t in range(TT):
                if t >= 2:
                    dve.wait_ge(h_turned_sem, t - 1)
                ch.wait(nc.vector.scalar_tensor_tensor(h[:, t % 2, :], x[:, t, :], inv[:, t:t + 1], scale_row,
                                                       ALU.mult, ALU.mult))
                nc.vector.tensor_tensor(h[:, t % 2, :], h[:, t % 2, :], shift_row, ALU.add).then_inc(h_made, 1)
                if t >= 1:
                    keep(t - 1)
            keep(TT - 1)

        @block.tensor
        def _(pe):
            for t in range(TT):
                pe.wait_ge(h_made, t + 1)
                if t >= 2:
                    pe.wait_ge(kept_sem, t - 1)
                for k in range(KD):
                    tr = nc.tensor.transpose(turned[t % 2][:, k // 4, (k % 4) * P:(k % 4 + 1) * P],
                                             h[:, t % 2, k * P:(k + 1) * P], ident[:, :])
                tr.then_inc(h_turned_sem, 1)


def project_in(nc, dram, scratch, kept, h_t):
    with ExitStack() as ctx:
        sb, ps, sem = ctx_tools(nc, ctx)
        RING = 3
        w = sb("w_ring", [P, RING, KD, P])
        w_v = sb("w_v", [P, KD, V_W])
        w_f = sb("w_f", [P, KD, FOX_H])
        wide = sb("qk_rows", [P, 2, T])
        vals = sb("v_rows", [P, 2, V_W])
        bias_f = sb("bias_f", [FOX_H, 1])
        f_logit, f_abs, f_exp, f_min, f_sum, f_neg, f_one = (
            sb(f"f_{n}", [FOX_H, T]) for n in ("logit", "abs", "exp", "min", "sum", "neg", "one"))
        acc = [ps(f"in_ps{i}", [P, 2, BANK]) for i in range(2)]
        acc_v = [ps(f"in_psv{i}", [P, 2, BANK]) for i in range(2)]
        w_in = [sem(f"i_w{i}") for i in range(RING)]
        wv_in, small_in, f_steps = sem("i_wv"), sem("i_small"), sem("i_f")
        made, taken, v_made, v_taken = sem("i_made"), sem("i_taken"), sem("i_vmade"), sem("i_vtaken")
        stored = [sem(f"i_st{i}") for i in range(2)]
        v_stored = [sem(f"i_vst{i}") for i in range(2)]
        f_act, f_stored = sem("i_fact"), sem("i_fst")
        block = ctx.enter_context(nc.Block())
        w_view = dram["w_in"][0].rearrange("(k p) n -> p k n", p=P)
        tiles = [(j * P, SCALE if j < 4 else 1.0, scratch["qk_fox"][2 * j:2 * j + 2, 0:HD, :]) for j in range(8)]
        tiles += [(COL_SQ + j * P, SCALE if j < 4 else 1.0, scratch["qk_swa"][2 * j:2 * j + 2]) for j in range(5)]
        NTL = len(tiles)

        @block.sync
        def _(sp):
            sp.dma_start(w_f[:, :, :], w_view[:, :, COL_FF:COL_SQ]).then_inc(small_in, 16)
            sp.dma_start(bias_f[:, :], dram["b_fgate"].rearrange("a h -> h a")).then_inc(small_in, 16)
            for j in range(NTL):
                if j >= RING:
                    sp.wait_ge(made, j - RING + 1)
                sp.dma_start(w[:, j % RING], w_view[:, :, tiles[j][0]:tiles[j][0] + P]).then_inc(w_in[j % RING], 16)
                if j == 4:
                    sp.dma_start(w_v[:, :, 0:FOX_H * HD], w_view[:, :, COL_FV:COL_FF]).then_inc(wv_in, 16)
                    sp.dma_start(w_v[:, :, FOX_H * HD:], w_view[:, :, COL_SV:IN_W]).then_inc(wv_in, 16)
            for s in range(2):
                sp.wait_ge(stored[s], 16 * 2 * ((NTL - s + 1) // 2))
                sp.wait_ge(v_stored[s], 16 * TT // 2)
            sp.wait_ge(f_stored, 16 * 4)

        @block.tensor
        def _(pe):
            pe.wait_ge(small_in, 32)
            for half in range(2):
                for k in range(KD):
                    mm = nc.tensor.matmul(acc_v[0][0:FOX_H, half, :], w_f[:, k, :], h_t[:, k, half * BANK:(half + 1) * BANK],
                                          start=(k == 0), stop=(k == KD - 1))
            mm.then_inc(v_made, 1)
            for j in range(NTL):
                pe.wait_ge(w_in[j % RING], 16 * (j // RING + 1))
                if j >= 2:
                    pe.wait_ge(taken, j - 1)
                for half in range(2):
                    for k in range(KD):
                        mm = nc.tensor.matmul(acc[j % 2][:, half, :], w[:, j % RING, k, :],
                                              h_t[:, k, half * BANK:(half + 1) * BANK],
                                              start=(k == 0), stop=(k == KD - 1))
                mm.then_inc(made, 1)
            pe.wait_ge(wv_in, 32)
            for t in range(TT):
                pe.wait_ge(v_taken, max(t, 1))
                for lo, hi, half in ((0, BANK, 0), (BANK, V_W, 1)):
                    for k in range(KD):
                        mm = nc.tensor.matmul(acc_v[t % 2][:, half, 0:hi - lo], h_t[:, k, t * P:(t + 1) * P],
                                              w_v[:, k, lo:hi], start=(k == 0), stop=(k == KD - 1))
                mm.then_inc(v_made, 1)

        @block.scalar
        def _(act):
            act.wait_ge(f_steps, 1)
            nc.scalar.activation(f_abs[:, :], f_logit[:, :], ACT.Abs).then_inc(f_act, 1)
            act.wait_ge(f_act, 1)
            nc.scalar.activation(f_exp[:, :], f_abs[:, :], ACT.Exp, scale=-1.0).then_inc(f_act, 1)
            act.wait_ge(f_act, 2)
            nc.scalar.activation(f_abs[:, :], f_exp[:, :], ACT.Ln, bias=1.0).then_inc(f_act, 1)
            for j in range(NTL):
                act.wait_ge(made, j + 1)
                if j >= 2:
                    act.wait_ge(stored[j % 2], 32 * (j // 2))
                nc.scalar.activation(wide[:, j % 2, :], acc[j % 2][:, :, :].rearrange("p a b -> p (a b)"), ACT.Copy,
                                     scale=tiles[j][1]).then_inc(taken, 1)
                act.wait_ge(taken, j + 1)
                for head in range(2):
                    act.dma_start(tiles[j][2][head], wide[head * HD:(head + 1) * HD, j % 2, :]) \
                        .then_inc(stored[j % 2], 16)

        @block.vector
        def _(dve):
            dve.wait_ge(v_made, 1)
            nc.vector.tensor_scalar(f_logit[:, :], acc_v[0][0:FOX_H, :, :].rearrange("p a b -> p (a b)"),
                                    bias_f[:, 0:1], None, ALU.add).then_inc(f_steps, 1)
            dve.wait_ge(f_steps, 1)
            nc.vector.tensor_scalar(f_min[:, :], f_logit[:, :], 0.0, None, ALU.min).then_inc(v_taken, 1)
            nc.vector.memset(f_one[:, :], 1.0).then_inc(f_steps, 1)
            dve.wait_ge(f_act, 3)
            dve.wait_ge(v_taken, 1)
            nc.vector.tensor_tensor(f_min[:, :], f_min[:, :], f_abs[:, :], ALU.subtract).then_inc(f_steps, 1)
            dve.wait_ge(f_steps, 3)
            nc.vector.tensor_tensor_scan(f_sum[:, :], f_one[:, :], f_min[:, :], 0.0, ALU.mult, ALU.add) \
                .then_inc(f_steps, 1)
            dve.wait_ge(f_steps, 4)
            nc.vector.tensor_scalar(f_neg[:, :], f_sum[:, :], -1.0, None, ALU.mult).then_inc(f_steps, 1)
            for t in range(TT):
                dve.wait_ge(v_made, t + 2)
                if t >= 2:
                    dve.wait_ge(v_stored[t % 2], 16 * (t // 2))
                nc.vector.tensor_copy(vals[:, t % 2, :],
                                      acc_v[t % 2][:, :, :].rearrange("p a b -> p (a b)")[:, 0:V_W]).then_inc(v_taken, 1)

        @block.gpsimd
        def _(pool):
            pool.wait_ge(f_steps, 5)
            rows = scratch["qk_fox"]
            pool.dma_start(rows[0:FOX_H, HD, :], f_sum[:, :]).then_inc(f_stored, 16)
            pool.dma_start(rows[0:FOX_H, HD + 1, :], f_one[:, :]).then_inc(f_stored, 16)
            pool.dma_start(rows[FOX_H:, HD, :], f_one[:, :]).then_inc(f_stored, 16)
            pool.dma_start(rows[FOX_H:, HD + 1, :], f_neg[:, :]).then_inc(f_stored, 16)
            for t in range(TT):
                pool.wait_ge(v_taken, t + 2)
                pool.dma_start(scratch["v"][t * P:(t + 1) * P, :], vals[:, t % 2, :]).then_inc(v_stored[t % 2], 16)


def fox_attention(nc, scratch, kept):
    ident, causal = kept["ident"], kept["causal"]
    with ExitStack() as ctx:
        sb, ps, sem = ctx_tools(nc, ctx)
        q, k = sb("fx_q", [AUG, 2, T]), sb("fx_k", [AUG, 2, T])
        v = sb("fx_v", [P, 2, TT, HD])
        prob, prob_t = sb("fx_p", [P, 2, T]), sb("fx_pt", [P, 2, T])
        n_max, row_sum, inv = (sb(f"fx_{n}", [P, 2 * TT]) for n in ("max", "sum", "inv"))
        out = sb("fx_out", [P, 2, TT, HD])
        score = [ps(f"fx_s{i}", [P, 2 * BANK]) for i in range(2)]
        turned = ps("fx_t", [P, 2 * BANK])
        mixed = [ps(f"fx_o{i}", [P, HD]) for i in range(2)]
        head_in = [sem(f"fx_in{i}") for i in range(2)]
        scored, masked, maxed, probed = (sem(f"fx_{n}") for n in ("scored", "masked", "maxed", "probed"))
        turn_made, turn_kept, mix_made, inv_made, mix_kept = (
            sem(f"fx_{n}") for n in ("turned", "tkept", "mixm", "invm", "mixk"))
        stored = [sem(f"fx_st{i}") for i in range(2)]
        block = ctx.enter_context(nc.Block())
        NI = FOX_H // 2
        units = [(h, i) for h in range(2) for i in range(TT)]
        NU = len(units)

        @block.sync
        def _(sp):
            def turn(it):
                for h in range(2):
                    behind(sp, mix_made, it * NU + TT * h)
                    head = it * 2 + h
                    sp.dma_start(q[:, h, :], scratch["qk_fox"][bass.ds(head, 1), :, :].rearrange("h r t -> (h r) t")) \
                        .then_inc(head_in[h], 16)
                    sp.dma_start(k[:, h, :], scratch["qk_fox"][bass.ds(head + FOX_H, 1), :, :]
                                 .rearrange("h r t -> (h r) t")).then_inc(head_in[h], 16)
                    sp.dma_start(v[:, h, :, :], scratch["v"][:, bass.ds(head * HD, HD)]
                                 .rearrange("(b p) d -> p b d", p=P)).then_inc(head_in[h], 16)

            turns(sp, NI, turn)

        @block.tensor
        def _(pe):
            pe.sem_inc(mix_made, TT)
            def turn(it):
                def scores(u):
                    h, i = units[u]
                    if i == 0:
                        pe.wait_ge(head_in[h], 48 * it + 48)
                    pe.wait_ge(probed, it * NU + u + 1)
                    for c in range(0, (i + 1) * P, BANK):
                        w = min(BANK, (i + 1) * P - c)
                        mm = nc.tensor.matmul(score[u % 2][:, c:c + w], q[:, h, i * P:(i + 1) * P],
                                              k[:, h, c:c + w], start=True, stop=True)
                    mm.then_inc(scored, 1)

                def mix(u):
                    h, i = units[u]
                    pe.wait_ge(probed, it * NU + u + 1 + 2)
                    pe.wait_ge(turn_kept, it * NU + u + 1)
                    for b in range(i + 1):
                        tr = nc.tensor.transpose(turned[:, b * P:(b + 1) * P], prob[:, u % 2, b * P:(b + 1) * P],
                                                 ident[:, :])
                    tr.then_inc(turn_made, 1)

                def weigh(u):
                    h, i = units[u]
                    pe.wait_ge(turn_kept, it * NU + u + 1 + 1)
                    pe.wait_ge(mix_kept, it * NU + u + 1)
                    for b in range(i + 1):
                        mm = nc.tensor.matmul(mixed[u % 2][:, :], prob_t[:, u % 2, b * P:(b + 1) * P], v[:, h, b, :],
                                              start=(b == 0), stop=(b == i))
                    mm.then_inc(mix_made, 1)

                scores(0)
                for u in range(NU):
                    if u + 1 < NU:
                        scores(u + 1)
                    mix(u)
                    weigh(u)

            turns(pe, NI, turn)

        @block.vector
        def _(dve):
            dve.sem_inc(turn_kept, 1)
            dve.sem_inc(mix_kept, 2)
            def turn(it):
                def stats(u):
                    h, i = units[u]
                    dve.wait_ge(scored, it * NU + u + 1)
                    diag = score[u % 2][:, i * P:(i + 1) * P]
                    nc.vector.tensor_tensor(diag, diag, causal[:, :], ALU.add).then_inc(masked, 1)
                    dve.wait_ge(masked, it * NU + u + 1)
                    nc.vector.tensor_reduce(n_max[:, u:u + 1], score[u % 2][:, 0:(i + 1) * P], AX_X, ALU.max,
                                            negate=True).then_inc(maxed, 1)

                def keep(u):
                    h, i = units[u]
                    dve.wait_ge(turn_made, it * NU + u + 1)
                    dve.wait_ge(mix_made, it * NU + u - 1 + TT)
                    nc.vector.tensor_copy(prob_t[:, u % 2, 0:(i + 1) * P], turned[:, 0:(i + 1) * P]) \
                        .then_inc(turn_kept, 1)
                    nc.vector.reciprocal(inv[:, u:u + 1], row_sum[:, u:u + 1]).then_inc(inv_made, 1)

                def norm(u):
                    h, i = units[u]
                    dve.wait_ge(mix_made, it * NU + u + 1 + TT)
                    dve.wait_ge(inv_made, it * NU + u + 1)
                    if i == 0:
                        behind(dve, stored[h], it * 16)
                    nc.vector.tensor_scalar(out[:, h, i, :], mixed[u % 2][:, :], inv[:, u:u + 1], None, ALU.mult) \
                        .then_inc(mix_kept, 1)

                stats(0)
                for u in range(NU):
                    if u + 1 < NU:
                        stats(u + 1)
                    keep(u)
                    norm(u)

            turns(dve, NI, turn)

        @block.scalar
        def _(act):
            act.sem_inc(probed, 2)
            def turn(it):
                for u, (h, i) in enumerate(units):
                    act.wait_ge(maxed, it * NU + u + 1)
                    if u >= 2:
                        behind(act, inv_made, it * NU + u - 1)
                    else:
                        behind(act, inv_made, it * NU)
                    nc.scalar.activation(prob[:, u % 2, 0:(i + 1) * P], score[u % 2][:, 0:(i + 1) * P], ACT.Exp,
                                         bias=n_max[:, u:u + 1], accum_out=row_sum[:, u:u + 1]).then_inc(probed, 1)

            turns(act, NI, turn)

        @block.gpsimd
        def _(pool):
            def turn(it):
                for h in range(2):
                    pool.wait_ge(mix_kept, it * NU + TT * (h + 1) + 2)
                    pool.dma_start(scratch["mix"][:, bass.ds((it * 2 + h) * HD, HD)].rearrange("(b p) d -> p b d", p=P),
                                   out[:, h, :, :]).then_inc(stored[h], 16)

            turns(pool, NI, turn)
            for h in range(2):
                pool.wait_ge(stored[h], 16 * NI)


def swa_attention(nc, dram, scratch, kept):
    ident = kept["ident"]
    G = SWA_GROUP
    with ExitStack() as ctx:
        sb, ps, sem = ctx_tools(nc, ctx)
        q, k = sb("sw_q", [HD, SWA_H, T]), sb("sw_k", [HD, SWA_KV, T])
        v = sb("sw_v", [P, TT, SWA_KV * HD])
        bias = sb("sw_bias", [P, SWA_H, 2 * P])
        sink = sb("sw_sink", [P, SWA_H])
        prob, prob_t = sb("sw_p", [P, 2, G, 2 * P]), sb("sw_pt", [P, 2, G, 2 * P])
        out = sb("sw_out", [P, TT, SWA_H, HD])
        NU = SWA_KV * TT
        top, n_max, less, sink_exp, row_sum, total, inv = (
            sb(f"sw_{n}", [P, NU, G]) for n in ("top", "max", "less", "sexp", "sum", "tot", "inv"))
        score = [ps(f"sw_s{i}", [P, G, 2 * P]) for i in range(2)]
        turned = ps("sw_t", [P, G, 2 * P])
        mixed = [ps(f"sw_o{i}", [P, G, HD]) for i in range(2)]
        load, scored, biased, tops, maxed, lessed, probed = (
            sem(f"sw_{n}") for n in ("load", "scored", "biased", "tops", "maxed", "lessed", "probed"))
        turn_made, turn_kept, mix_made, totaled, inv_made, mix_kept, stored = (
            sem(f"sw_{n}") for n in ("turned", "tkept", "mixm", "tot", "invm", "mixk", "stored"))
        block = ctx.enter_context(nc.Block())
        units = [(g, i) for g in range(SWA_KV) for i in range(TT)]

        def spans(i):
            return [(1, 0)] if i == 0 else [(0, i - 1), (1, i)]

        def band(i):
            return slice(P, 2 * P) if i == 0 else slice(0, 2 * P)

        @block.sync
        def _(sp):
            sp.dma_start(q[:, :, :], scratch["qk_swa"][0:SWA_H].rearrange("h r t -> r h t")).then_inc(load, 16)
            sp.dma_start(k[:, :, :], scratch["qk_swa"][SWA_H:].rearrange("h r t -> r h t")).then_inc(load, 16)
            sp.dma_start(v[:, :, :], scratch["v"][:, FOX_H * HD:].rearrange("(b p) d -> p b d", p=P)).then_inc(load, 16)
            sp.dma_start(bias[:, :, :], dram["swa_bias"]).then_inc(load, 16)
            sp.dma_start(sink[:, :], dram["swa_sinks"][0:1, :].broadcast_to([P, SWA_H])).then_inc(load, 16)
            sp.wait_ge(mix_kept, NU)
            sp.dma_start(scratch["mix"][:, FOX_H * HD:].rearrange("(b p) d -> p b d", p=P),
                         out[:, :, :, :].rearrange("p b h d -> p b (h d)")).then_inc(stored, 16)
            sp.wait_ge(stored, 16)

        @block.tensor
        def _(pe):
            pe.wait_ge(load, 80)

            def scores(u):
                g, i = units[u]
                if u >= 2:
                    pe.wait_ge(probed, (G + 1) * (u - 1))
                for n in range(G):
                    for place, b in spans(i):
                        mm = nc.tensor.matmul(score[u % 2][:, n, place * P:(place + 1) * P],
                                              q[:, g * G + n, i * P:(i + 1) * P], k[:, g, b * P:(b + 1) * P],
                                              start=True, stop=True)
                mm.then_inc(scored, 1)

            scores(0)
            for u, (g, i) in enumerate(units):
                if u + 1 < NU:
                    scores(u + 1)
                pe.wait_ge(probed, (G + 1) * (u + 1))
                if u >= 1:
                    pe.wait_ge(turn_kept, u)
                for n in range(G):
                    for place, b in spans(i):
                        tr = nc.tensor.transpose(turned[:, n, place * P:(place + 1) * P],
                                                 prob[:, u % 2, n, place * P:(place + 1) * P], ident[:, :])
                tr.then_inc(turn_made, 1)
                pe.wait_ge(turn_kept, u + 1)
                if u >= 2:
                    pe.wait_ge(mix_kept, u - 1)
                for n in range(G):
                    sp_ = spans(i)
                    for place, b in sp_:
                        mm = nc.tensor.matmul(mixed[u % 2][:, n, :], prob_t[:, u % 2, n, place * P:(place + 1) * P],
                                              v[:, b, g * HD:(g + 1) * HD],
                                              start=(place == sp_[0][0]), stop=(place == 1))
                mm.then_inc(mix_made, 1)

        @block.vector
        def _(dve):
            dve.wait_ge(load, 80)

            def stats(u):
                g, i = units[u]
                s = score[u % 2][:, :, band(i)]
                dve.wait_ge(scored, u + 1)
                nc.vector.tensor_tensor(s, s, bias[:, g * G:(g + 1) * G, band(i)], ALU.add).then_inc(biased, 1)
                dve.wait_ge(biased, u + 1)
                nc.vector.tensor_reduce(top[:, u, :], s, AX_X, ALU.max).then_inc(tops, 1)
                dve.wait_ge(tops, 2 * u + 1)
                nc.vector.tensor_tensor(top[:, u, :], top[:, u, :], sink[:, g * G:(g + 1) * G], ALU.max).then_inc(tops, 1)
                dve.wait_ge(tops, 2 * u + 2)
                nc.vector.tensor_scalar(n_max[:, u, :], top[:, u, :], -1.0, None, ALU.mult).then_inc(maxed, 1)
                nc.vector.tensor_tensor(less[:, u, :], sink[:, g * G:(g + 1) * G], top[:, u, :], ALU.subtract) \
                    .then_inc(lessed, 1)

            def keep(u):
                g, i = units[u]
                dve.wait_ge(turn_made, u + 1)
                if u >= 2:
                    dve.wait_ge(mix_made, u - 1)
                nc.vector.tensor_copy(prob_t[:, u % 2, :, band(i)], turned[:, :, band(i)]).then_inc(turn_kept, 1)
                nc.vector.tensor_tensor(total[:, u, :], row_sum[:, u, :], sink_exp[:, u, :], ALU.add).then_inc(totaled, 1)
                dve.wait_ge(totaled, u + 1)
                nc.vector.reciprocal(inv[:, u, :], total[:, u, :]).then_inc(inv_made, 1)
                dve.wait_ge(mix_made, u + 1)
                dve.wait_ge(inv_made, u + 1)
                nc.vector.tensor_tensor(out[:, i, g * G:(g + 1) * G, :], mixed[u % 2][:, :, :],
                                        inv[:, u, :, None].broadcast_to([P, G, HD]), ALU.mult).then_inc(mix_kept, 1)

            stats(0)
            for u in range(NU):
                if u + 1 < NU:
                    stats(u + 1)
                keep(u)

        @block.scalar
        def _(act):
            for u, (g, i) in enumerate(units):
                act.wait_ge(maxed, u + 1)
                act.wait_ge(lessed, u + 1)
                if u >= 2:
                    act.wait_ge(turn_made, u - 1)
                for n in range(G):
                    nc.scalar.activation(prob[:, u % 2, n, band(i)], score[u % 2][:, n, band(i)], ACT.Exp,
                                         bias=n_max[:, u, n:n + 1], accum_out=row_sum[:, u, n:n + 1]).then_inc(probed, 1)
                nc.scalar.activation(sink_exp[:, u, :], less[:, u, :], ACT.Exp).then_inc(probed, 1)


def project_out(nc, dram, scratch, kept, y):
    ident = kept["ident"]
    with ExitStack() as ctx:
        sb, ps, sem = ctx_tools(nc, ctx)
        w = sb("wo", [P, KD, D])
        m = sb("wo_m", [P, TT, D])
        m_t = sb("wo_mt", [P, 2, D])
        turned = ps("wo_t", [P, 2 * BANK])
        acc = [ps(f"wo_y{i}", [P, 2 * BANK]) for i in range(2)]
        load, turn_made, turn_kept, y_made, y_kept = (sem(f"wo_{n}") for n in ("ld", "tm", "tk", "ym", "yk"))
        block = ctx.enter_context(nc.Block())

        @block.sync
        def _(sp):
            sp.dma_start(m[:, :, :], scratch["mix"].rearrange("(b p) d -> p b d", p=P)).then_inc(load, 16)
            sp.dma_start(w[:, :, :], dram["w_out"][0].rearrange("(k p) n -> p k n", p=P)).then_inc(load, 16)

        @block.tensor
        def _(pe):
            pe.wait_ge(load, 32)

            def turn(t):
                if t >= 1:
                    pe.wait_ge(turn_kept, t)
                for k in range(KD):
                    tr = nc.tensor.transpose(turned[:, k * P:(k + 1) * P], m[:, t, k * P:(k + 1) * P], ident[:, :])
                tr.then_inc(turn_made, 1)

            turn(0)
            for t in range(TT):
                if t + 1 < TT:
                    turn(t + 1)
                pe.wait_ge(turn_kept, t + 1)
                if t >= 2:
                    pe.wait_ge(y_kept, t - 1)
                for half in range(2):
                    for k in range(KD):
                        mm = nc.tensor.matmul(acc[t % 2][:, half * BANK:(half + 1) * BANK],
                                              m_t[:, t % 2, k * P:(k + 1) * P], w[:, k, half * BANK:(half + 1) * BANK],
                                              start=(k == 0), stop=(k == KD - 1))
                mm.then_inc(y_made, 1)

        @block.vector
        def _(dve):
            for t in range(TT):
                dve.wait_ge(turn_made, t + 1)
                if t >= 2:
                    dve.wait_ge(y_made, t - 1)
                nc.vector.tensor_copy(m_t[:, t % 2, :], turned[:, :]).then_inc(turn_kept, 1)

        @block.scalar
        def _(act):
            for t in range(TT):
                act.wait_ge(y_made, t + 1)
                nc.scalar.copy(y[:, t, :], acc[t % 2][:, :]).then_inc(y_kept, 1)


def add_normed(nc, tag, x, y, gate_row, eps, store_to):
    with ExitStack() as ctx:
        sb, ps, sem = ctx_tools(nc, ctx)
        squares = sb(f"{tag}_sq", [P, D])
        sums, var, root, inv, tmp = (sb(f"{tag}_{n}", [P, TT]) for n in ("sum", "var", "root", "inv", "tmp"))
        squared, var_made, root_made, steps, added, stored = (
            sem(f"{tag}_{n}") for n in ("s_sq", "s_var", "s_root", "s_step", "s_add", "s_st"))
        block = ctx.enter_context(nc.Block())

        @block.scalar
        def _(act):
            for t in range(TT):
                if t:
                    act.wait_ge(squared, t)
                nc.scalar.activation(squares[:, :], y[:, t, :], ACT.Square,
                                     accum_out=sums[:, t:t + 1]).then_inc(squared, 1)
            act.wait_ge(var_made, 1)
            nc.scalar.activation(root[:, :], var[:, :], ACT.Sqrt).then_inc(root_made, 1)

        @block.vector
        def _(dve):
            ch = Chain(dve, steps)
            dve.wait_ge(squared, TT)
            nc.vector.tensor_scalar(var[:, :], sums[:, :], 1.0 / D, eps, ALU.mult, ALU.add).then_inc(var_made, 1)
            dve.wait_ge(root_made, 1)
            ch.wait(nc.vector.reciprocal(inv[:, :], root[:, :]))
            dve.wait_ge(var_made, 1)
            ch.wait(nc.vector.tensor_tensor(tmp[:, :], inv[:, :], inv[:, :], ALU.mult))
            ch.wait(nc.vector.tensor_tensor(tmp[:, :], tmp[:, :], var[:, :], ALU.mult))
            ch.wait(nc.vector.tensor_scalar(tmp[:, :], tmp[:, :], -0.5, 1.5, ALU.mult, ALU.add))
            ch.wait(nc.vector.tensor_tensor(inv[:, :], inv[:, :], tmp[:, :], ALU.mult))
            for t in range(TT):
                ch.wait(nc.vector.scalar_tensor_tensor(y[:, t, :], y[:, t, :], inv[:, t:t + 1], gate_row,
                                                       ALU.mult, ALU.mult))
                nc.vector.tensor_tensor(x[:, t, :], x[:, t, :], y[:, t, :], ALU.add).then_inc(added, 1)
            dve.wait_ge(added, TT)

        @block.sync
        def _(sp):
            for t in range(TT):
                sp.wait_ge(added, t + 1)
                sp.dma_start(store_to[t * P:(t + 1) * P, :], x[:, t, :]).then_inc(stored, 16)
            sp.wait_ge(stored, 16 * TT)


def peer_queries(nc, dram, scratch, h_t):
    with ExitStack() as ctx:
        sb, ps, sem = ctx_tools(nc, ctx)
        RING = 2
        w = sb("wq_ring", [P, RING, KD, P])
        rows = sb("pq_rows", [P, 2, T])
        acc = [ps(f"pq_ps{i}", [P, 2 * BANK]) for i in range(2)]
        w_in = [sem(f"pq_w{i}") for i in range(RING)]
        made, taken = sem("pq_made"), sem("pq_taken")
        stored = [sem(f"pq_st{i}") for i in range(2)]
        block = ctx.enter_context(nc.Block())
        w_view = dram["w_query"][0].rearrange("(k p) n -> p k n", p=P)

        @block.sync
        def _(sp):
            def turn(it):
                for s in range(2):
                    sp.wait_ge(made, it * 2 + s + 1)
                    sp.dma_start(w[:, s], w_view[:, :, bass.ds((it * 2 + s) * P, P)]).then_inc(w_in[s], 16)

            turns(sp, NG // 2, turn)

        @block.tensor
        def _(pe):
            pe.sem_inc(made, 2)
            def turn(it):
                for s in range(2):
                    pe.wait_ge(w_in[s], 16 * it + 16)
                    pe.wait_ge(taken, it * 2 + s + 1)
                    for half in range(2):
                        for k in range(KD):
                            mm = nc.tensor.matmul(acc[s][:, half * BANK:(half + 1) * BANK], w[:, s, k, :],
                                                  h_t[:, k, half * BANK:(half + 1) * BANK],
                                                  start=(k == 0), stop=(k == KD - 1))
                    mm.then_inc(made, 1)

            turns(pe, NG // 2, turn)

        @block.scalar
        def _(act):
            act.sem_inc(taken, 2)
            def turn(it):
                for s in range(2):
                    act.wait_ge(made, it * 2 + s + 1 + 2)
                    behind(act, stored[s], it * 16)
                    nc.scalar.copy(rows[:, s, :], acc[s][:, :]).then_inc(taken, 1)

            turns(act, NG // 2, turn)

        @block.gpsimd
        def _(pool):
            def turn(it):
                for s in range(2):
                    pool.wait_ge(taken, it * 2 + s + 1 + 2)
                    pool.dma_start(scratch["pq"][:, bass.ds(it * 2 + s, 1), :].rearrange("p g t -> p (g t)"),
                                   rows[:, s, :]).then_inc(stored[s], 16)

            turns(pool, NG // 2, turn)
            for s in range(2):
                pool.wait_ge(stored[s], 16 * NG // 2)


def peer_pick(nc, dram, scratch, kept, slots):
    ident, iota = kept["ident"], kept["iota"]
    i1_t, i2_t, gate_t = slots
    with ExitStack() as ctx:
        sb, ps, sem = ctx_tools(nc, ctx)
        keys = sb("pk_keys", [P, NG, P])
        keys_t = sb("pk_keys_t", [P, NG, NK])
        q = sb("pk_q", [P, 2, NG, P])
        sc = sb("pk_sc", [P, 2, NG, NK])
        rest = sb("pk_rest", [P, NG, NK])
        val = sb("pk_val", [P, PH, 2, TOPK])
        idx, idx_f = sb("pk_idx", [P, PH, 2, TOPK], U32), sb("pk_idx_f", [P, PH, 2, TOPK])
        cand, cand_rest = sb("pk_cand", [P, PH, TOPK, TOPK]), sb("pk_cand_rest", [P, PH, TOPK, TOPK])
        best, best_i = sb("pk_best", [P, PH, TOPK]), sb("pk_best_i", [P, PH, TOPK], U32)
        part_i = sb("pk_part_i", [P, 2, PH, TOPK], U32)
        part = sb("pk_part", [P, 2, PH, TOPK])
        found = sb("pk_found", [P, 3, SLOTS])
        expo = sb("pk_exp", [P, PH, TOPK])
        norm = sb("pk_norm", [P, 2, PH])
        sc_ps = ps("pk_ps", [P, NG, NK])
        turned = ps("pk_t", [P, 4 * P])
        load, keys_turned, keys_kept = sem("pk_ld"), sem("pk_kt"), sem("pk_kk")
        q_in = [sem(f"pk_q{i}") for i in range(2)]
        scored, sc_kept, steps, shifted, expd, slot_made, slot_turned, slot_kept, waited = (
            sem(f"pk_{n}") for n in ("scored", "sck", "step", "shift", "expd", "sm", "st", "sk", "waited"))
        block = ctx.enter_context(nc.Block())
        STEPS = 16

        @block.sync
        def _(sp):
            sp.dma_start(keys[:, :, :], dram["sub_keys"][0].rearrange("h c k d -> k (h c) d")).then_inc(load, 16)
            def turn(it):
                for s in range(2):
                    sp.wait_ge(scored, it * 2 + s + 1)
                    sp.dma_start(q[:, s], scratch["pq"][:, :, bass.ds((it * 2 + s) * P, P)]).then_inc(q_in[s], 16)

            turns(sp, TT // 2, turn)

        @block.tensor
        def _(pe):
            pe.sem_inc(scored, 2)
            pe.wait_ge(load, 16)
            for g in range(NG):
                tr = nc.tensor.transpose(sc_ps[:, g, :], keys[:, g, :], ident[:, :])
            tr.then_inc(keys_turned, 1)
            pe.wait_ge(keys_kept, 1)
            def turn(it):
                for s in range(2):
                    pe.wait_ge(q_in[s], 16 * it + 16)
                    pe.wait_ge(sc_kept, it * 2 + s + 1)
                    for g in range(NG):
                        mm = nc.tensor.matmul(sc_ps[:, g, :], q[:, s, g, :], keys_t[:, g, :], start=True, stop=True)
                    mm.then_inc(scored, 1)
                    pe.wait_ge(slot_made, it * 2 + s + 1)
                    pe.wait_ge(slot_kept, it * 2 + s + 1)
                    for n in range(3):
                        tr = nc.tensor.transpose(turned[:, n * P:(n + 1) * P], found[:, n, :], ident[:, :])
                    tr.then_inc(slot_turned, 1)

            turns(pe, TT // 2, turn)

        @block.scalar
        def _(act):
            act.wait_ge(keys_turned, 1)
            nc.scalar.copy(keys_t[:, :, :], sc_ps[:, :, :]).then_inc(keys_kept, 1)
            act.sem_inc(sc_kept, 1)
            def turn(it):
                for s in range(2):
                    act.wait_ge(scored, it * 2 + s + 1 + 2)
                    nc.scalar.copy(sc[:, s], sc_ps[:, :, :]).then_inc(sc_kept, 1)
                    act.wait_ge(shifted, it * 2 + s + 1)
                    nc.scalar.activation(expo[:, :, :], expo[:, :, :], ACT.Exp).then_inc(expd, 1)

            turns(act, TT // 2, turn)

        @block.vector
        def _(dve):
            dve.sem_inc(slot_kept, 1)
            def turn(it):
                for s in range(2):
                    ch = Chain(dve, steps, (it * 2 + s) * STEPS, waited)
                    dve.wait_ge(sc_kept, it * 2 + s + 1 + 1)
                    dve.sem_inc(waited, 1)
                    v = val[:, :, :, :].rearrange("p h c k -> p (h c) k")
                    ix = idx[:, :, :, :].rearrange("p h c k -> p (h c) k")
                    for g in range(NG):
                        op = nc.vector.max(v[:, g, 0:8], sc[:, s, g, :])
                    ch.wait_alone(op)
                    for g in range(NG):
                        nc.vector.max_index(ix[:, g, 0:8], v[:, g, 0:8], sc[:, s, g, :])
                        op = nc.vector.match_replace(rest[:, g, :], v[:, g, 0:8], sc[:, s, g, :], TAKEN)
                    ch.wait_alone(op)
                    for g in range(NG):
                        op = nc.vector.max(v[:, g, 8:16], rest[:, g, :])
                    ch.wait_alone(op)
                    for g in range(NG):
                        op = nc.vector.max_index(ix[:, g, 8:16], v[:, g, 8:16], rest[:, g, :])
                    ch.wait_alone(op)
                    nc.vector.tensor_copy(idx_f[:, :, :, :], idx[:, :, :, :])
                    ch.wait_alone(nc.vector.tensor_tensor(cand[:, :, :, :],
                                                    val[:, :, 0, :, None].broadcast_to([P, PH, TOPK, TOPK]),
                                                    val[:, :, 1, None, :].broadcast_to([P, PH, TOPK, TOPK]), ALU.add))
                    c = cand[:, :, :, :].rearrange("p h a b -> p h (a b)")
                    cr = cand_rest[:, :, :, :].rearrange("p h a b -> p h (a b)")
                    for h in range(PH):
                        op = nc.vector.max(best[:, h, 0:8], c[:, h, :])
                    ch.wait_alone(op)
                    for h in range(PH):
                        nc.vector.max_index(best_i[:, h, 0:8], best[:, h, 0:8], c[:, h, :])
                        op = nc.vector.match_replace(cr[:, h, :], best[:, h, 0:8], c[:, h, :], TAKEN)
                    ch.wait_alone(op)
                    for h in range(PH):
                        op = nc.vector.max(best[:, h, 8:16], cr[:, h, :])
                    ch.wait_alone(op)
                    for h in range(PH):
                        nc.vector.max_index(best_i[:, h, 8:16], best[:, h, 8:16], cr[:, h, :])
                    nc.vector.tensor_tensor(expo[:, :, :], best[:, :, :],
                                            best[:, :, 0:1].broadcast_to([P, PH, TOPK]), ALU.subtract) \
                        .then_inc(shifted, 1)
                    dve.wait_ge(shifted, it * 2 + s + 1)
                    nc.vector.tensor_scalar(part_i[:, 0], best_i[:, :, :], 4, None, ALU.logical_shift_right)
                    ch.wait(nc.vector.tensor_scalar(part_i[:, 1], best_i[:, :, :], TOPK - 1, None, ALU.bitwise_and))
                    ch.wait(nc.vector.tensor_copy(part[:, :, :, :], part_i[:, :, :, :]))
                    behind(dve, slot_turned, it * 2 + s)
                    for n, eq in ((0, cand), (1, cand_rest)):
                        op = nc.vector.tensor_tensor(
                            eq[:, :, :, :].rearrange("p h a b -> p (h a) b"),
                            part[:, n].rearrange("p h k -> p (h k)")[:, :, None].broadcast_to([P, SLOTS, TOPK]),
                            iota[:, None, 0:TOPK].broadcast_to([P, SLOTS, TOPK]), ALU.is_equal)
                    ch.wait(op)
                    for n, eq in ((0, cand), (1, cand_rest)):
                        op = nc.vector.tensor_tensor(eq[:, :, :, :], eq[:, :, :, :],
                                                     idx_f[:, :, n, None, :].broadcast_to([P, PH, TOPK, TOPK]), ALU.mult)
                    ch.wait(op)
                    for n, eq in ((0, cand), (1, cand_rest)):
                        op = nc.vector.tensor_reduce(found[:, n, :], eq[:, :, :, :].rearrange("p h a b -> p (h a) b"),
                                                     AX_X, ALU.add)
                    ch.wait(op)
                    dve.wait_ge(expd, it * 2 + s + 1)
                    ch.wait(nc.vector.tensor_reduce(norm[:, 0, :], expo[:, :, :], AX_X, ALU.add))
                    ch.wait(nc.vector.reciprocal(norm[:, 1, :], norm[:, 0, :]))
                    nc.vector.tensor_tensor(found[:, 2, :].rearrange("p (h k) -> p h k", h=PH), expo[:, :, :],
                                            norm[:, 1, :, None].broadcast_to([P, PH, TOPK]), ALU.mult) \
                        .then_inc(slot_made, 1)
                    dve.wait_ge(slot_turned, it * 2 + s + 1)
                    for n, dst in enumerate((i1_t, i2_t, gate_t)):
                        op = nc.vector.tensor_copy(dst[:, bass.ds((it * 2 + s) * P, P)], turned[:, n * P:(n + 1) * P])
                    op.then_inc(slot_kept, 1)
                    dve.wait_ge(slot_kept, it * 2 + s + 1 + 1)
                    assert ch.n <= STEPS
                    dve.sem_inc(steps, STEPS - ch.n)

            turns(dve, TT // 2, turn)


def peer_gates(nc, scratch, kept, slots):
    iota = kept["iota"]
    i1_t, i2_t, gate_t = slots
    HALF = 4
    STEP = 2 * HALF
    TURNS = P // STEP
    with ExitStack() as ctx:
        sb, ps, sem = ctx_tools(nc, ctx)
        second, first = sb("pg_second", [P, STEP, NK]), sb("pg_first", [P, STEP, NK])
        gates = sb("pg_gates", [P, 2, NK, P // 2])
        acc = [ps(f"pg_ps{i}", [P, HALF * NK]) for i in range(2)]
        hot, made, taken = sem("pg_hot"), sem("pg_made"), sem("pg_taken")
        stored = [sem(f"pg_st{i}") for i in range(2)]
        block = ctx.enter_context(nc.Block())

        @block.vector
        def _(dve):
            with dve.Fori(0, T // STEP) as it:
                for j in range(STEP):
                    if j % HALF == 0:
                        dve.wait_ge(made, it * 2 + j // HALF + 1)
                    tok = bass.ds(it * STEP + j, 1)
                    nc.vector.tensor_scalar(second[:, j, :], iota[:, :], i2_t[:, tok], None, ALU.is_equal)
                    op = nc.vector.tensor_scalar(first[:, j, :], iota[:, :], i1_t[:, tok], gate_t[:, tok],
                                                 ALU.is_equal, ALU.mult)
                    if j % HALF == HALF - 1:
                        op.then_inc(hot, 1)

        @block.tensor
        def _(pe):
            pe.sem_inc(made, 2)
            with pe.Fori(0, T // STEP) as it:
                for s in range(2):
                    pe.wait_ge(hot, it * 2 + s + 1)
                    pe.wait_ge(taken, it * 2 + s + 1)
                    for j in range(HALF):
                        mm = nc.tensor.matmul(acc[s][:, j * NK:(j + 1) * NK], second[:, s * HALF + j, :],
                                              first[:, s * HALF + j, :], start=True, stop=True)
                    mm.then_inc(made, 1)

        W = P // 2
        PT = W // STEP

        @block.scalar
        def _(act):
            act.sem_inc(taken, 2)
            def turn(tile):
                for piece in range(2):
                    behind(act, stored[piece], tile * 16)
                    with act.Fori(0, PT) as it:
                        for s in range(2):
                            act.wait_ge(made, (tile * 2 + piece) * PT * 2 + it * 2 + s + 1 + 2)
                            nc.scalar.copy(
                                gates[:, piece, :, bass.ds(it * STEP + s * HALF, HALF)].rearrange("p a t -> p t a"),
                                acc[s][:, :].rearrange("p (t a) -> p t a", t=HALF)).then_inc(taken, 1)

            turns(act, T // P, turn)

        @block.sync
        def _(sp):
            def turn(tile):
                for piece in range(2):
                    sp.wait_ge(taken, (tile * 2 + piece + 1) * PT * 2 + 2)
                    sp.dma_start(scratch["gates"][:, :, bass.ds((tile * 2 + piece) * W, W)].rearrange("a p t -> p a t"),
                                 gates[:, piece, :, :]).then_inc(stored[piece], 16)

            turns(sp, T // P, turn)
            for piece in range(2):
                sp.wait_ge(stored[piece], 16 * TT)


def peer_experts(nc, dram, scratch, kept, h_hi, h_lo, y):
    ident = kept["ident"]
    NB = 4
    NBLK = N_EXP // P
    NGRP = NBLK // NB
    with ExitStack() as ctx:
        sb, ps, sem = ctx_tools(nc, ctx)
        u_raw, v_raw = sb("ex_u", [P, 2, D]), sb("ex_v", [P, 2, D])
        u_hi, u_lo = sb("ex_uhi", [P, 2, KD, P], F16), sb("ex_ulo", [P, 2, KD, P], F16)
        v_hi, v_lo = sb("ex_vhi", [P, 2, NB, D], F16), sb("ex_vlo", [P, 2, NB, D], F16)
        gate, act_g = sb("ex_gate", [P, 2, T]), sb("ex_act", [P, 2, T])
        a_hi, a_lo = sb("ex_ahi", [P, 2, NB, T], F16), sb("ex_alo", [P, 2, NB, T], F16)
        u_turned = ps("ex_ut", [P, KD, P])
        score = [ps(f"ex_s{i}", [P, BANK]) for i in range(2)]
        out = [ps(f"ex_o{i}", [P, BANK]) for i in range(4)]
        u_in, v_in, g_in = ([sem(f"ex_{n}in{i}") for i in range(2)] for n in "uvg")
        turned, uhi_made, ulo_made, scored, gelued, gated, ahi_made, alo_made, vhi_made, vlo_made, mixed, added = (
            sem(f"ex_{n}") for n in ("turned", "uhi", "ulo", "scored", "gelued", "gated", "ahi", "alo", "vhi", "vlo",
                                     "mixed", "added"))
        block = ctx.enter_context(nc.Block())

        def steps(eng, body):
            for n in range(NB):
                body(n, n // 2, 0, n)
            with eng.Fori(0, NGRP // 2 - 1) as it:
                for j in range(2 * NB):
                    k = (NB + j) % (2 * NB)
                    body(it * (2 * NB) + (NB + j), it * NB + (NB + j) // 2, it * 2 + (1 + j // NB), k)
            for n in range(NBLK - NB, NBLK):
                body(n, n // 2, n // NB, n % (2 * NB))

        @block.sync
        def _(sp):
            def body(n, half, g, k):
                s = k % 2
                lagging = not isinstance(n, int) or n >= 2
                if lagging:
                    sp.wait_ge(turned, n - 1)
                sp.dma_start(u_raw[:, s, :], dram["w_u"][0, bass.ds(n * P, P), :]).then_inc(u_in[s], 16)
                if lagging:
                    sp.wait_ge(vlo_made, n - 1)
                sp.dma_start(v_raw[:, s, :], dram["w_v"][0, bass.ds(n * P, P), :]).then_inc(v_in[s], 16)
                if lagging:
                    sp.wait_ge(gated, n - 1)
                sp.dma_start(gate[:, s, :], scratch["gates"][bass.ds(n, 1)].rearrange("a p t -> (a p) t")) \
                    .then_inc(g_in[s], 16)
            steps(sp, body)

        @block.tensor
        def _(pe):
            def turn(n, half, k):
                pe.wait_ge(u_in[k % 2], 16 * half + 16)
                if not isinstance(n, int) or n >= 1:
                    pe.wait_ge(ulo_made, n)
                for c in range(KD):
                    tr = nc.tensor.transpose(u_turned[:, c, :], u_raw[:, k % 2, c * P:(c + 1) * P], ident[:, :])
                tr.then_inc(turned, 1)

            def scores(n, k):
                s = k % 2
                pe.wait_ge(ulo_made, n + 1)
                if not isinstance(n, int) or n >= 1:
                    pe.wait_ge(gelued, 2 * n)
                for half in range(2):
                    cols = slice(half * BANK, (half + 1) * BANK)
                    for c in range(KD):
                        nc.tensor.matmul(score[half][:, :], u_hi[:, s, c, :], h_hi[:, c, cols], start=(c == 0), stop=False)
                        nc.tensor.matmul(score[half][:, :], u_hi[:, s, c, :], h_lo[:, c, cols], start=False, stop=False)
                        mm = nc.tensor.matmul(score[half][:, :], u_lo[:, s, c, :], h_hi[:, c, cols],
                                              start=False, stop=(c == KD - 1))
                    mm.then_inc(scored, 1)

            def outputs(g, pair, par):
                if pair == 0:
                    pe.wait_ge(alo_made, g * NB + NB)
                    pe.wait_ge(vlo_made, g * NB + NB)
                for i in range(2):
                    t = 2 * pair + i
                    for half in range(2):
                        pe.wait_ge(added, g * 16 + 2 * t + half + 1)
                    rows = slice(t * P, (t + 1) * P)
                    for b in range(NB):
                        for a, v, first, last in ((a_hi, v_hi, True, False), (a_hi, v_lo, False, False),
                                                  (a_lo, v_hi, False, True)):
                            for half in range(2):
                                mm = nc.tensor.matmul(out[2 * i + half][:, :], a[:, par, b, rows],
                                                      v[:, par, b, half * BANK:(half + 1) * BANK],
                                                      start=(b == 0 and first), stop=(b == NB - 1 and last))
                                if b == NB - 1 and last:
                                    mm.then_inc(mixed, 1)

            def body(n, half, g, k):
                if not (isinstance(n, int) and n == NBLK - 1):
                    turn(n + 1, half + k % 2, (k + 1) % (2 * NB))
                scores(n, k)
                if not (isinstance(n, int) and n < NB):
                    outputs(g - 1, k % NB, 1 - k // NB)

            turn(0, 0, 0)
            steps(pe, body)
            for pair in range(TT // 2):
                outputs(NGRP - 1, pair, (NGRP - 1) % 2)

        @block.scalar
        def _(act):
            def split_u(n, k):
                act.wait_ge(turned, n + 1)
                if not isinstance(n, int) or n >= 2:
                    act.wait_ge(scored, 2 * n - 2)
                nc.scalar.activation(u_hi[:, k % 2], u_turned[:, :, :], ACT.Copy, scale=S_U).then_inc(uhi_made, 1)

            def body(n, half, g, k):
                s, b, par = k % 2, k % NB, k // NB
                first = isinstance(n, int) and n < NB
                if not (isinstance(n, int) and n == NBLK - 1):
                    split_u(n + 1, (k + 1) % (2 * NB))
                if not first and b == 0:
                    act.wait_ge(mixed, g * 16 - 16)
                act.wait_ge(v_in[s], 16 * half + 16)
                nc.scalar.activation(v_hi[:, par, b, :], v_raw[:, s, :], ACT.Copy, scale=S_V).then_inc(vhi_made, 1)
                if not isinstance(n, int) or n >= 2:
                    act.wait_ge(alo_made, n - 1)
                for hf in range(2):
                    act.wait_ge(scored, 2 * n + (hf + 1))
                    nc.scalar.activation(act_g[:, s, hf * BANK:(hf + 1) * BANK], score[hf][:, :], ACT.Gelu_apprx_tanh,
                                         scale=1.0 / (S_H * S_U)).then_inc(gelued, 1)
                act.wait_ge(gated, n + 1)
                nc.scalar.activation(a_hi[:, par, b, :], act_g[:, s, :], ACT.Copy, scale=S_A).then_inc(ahi_made, 1)

            split_u(0, 0)
            steps(act, body)

        @block.vector
        def _(dve):
            def split_u(n, k):
                dve.wait_ge(uhi_made, n + 1)
                nc.vector.scalar_tensor_tensor(u_lo[:, k % 2], u_turned[:, :, :], S_U, u_hi[:, k % 2],
                                               ALU.mult, ALU.subtract).then_inc(ulo_made, 1)

            def add(g, pair):
                for i in range(2):
                    t = 2 * pair + i
                    for half in range(2):
                        cols = slice(half * BANK, (half + 1) * BANK)
                        dve.wait_ge(mixed, g * 16 + 2 * t + half + 1)
                        dve.wait_ge(added, g * 16 + 4)
                        nc.vector.tensor_tensor(y[:, t, cols], out[2 * i + half][:, :], y[:, t, cols], ALU.add) \
                            .then_inc(added, 1)

            def body(n, half, g, k):
                s, b, par = k % 2, k % NB, k // NB
                if not (isinstance(n, int) and n == NBLK - 1):
                    split_u(n + 1, (k + 1) % (2 * NB))
                dve.wait_ge(vhi_made, n + 1)
                nc.vector.scalar_tensor_tensor(v_lo[:, par, b, :], v_raw[:, s, :], S_V, v_hi[:, par, b, :],
                                               ALU.mult, ALU.subtract).then_inc(vlo_made, 1)
                dve.wait_ge(gelued, 2 * n + 2)
                dve.wait_ge(g_in[s], 16 * half + 16)
                nc.vector.tensor_tensor(act_g[:, s, :], act_g[:, s, :], gate[:, s, :], ALU.mult).then_inc(gated, 1)
                dve.wait_ge(ahi_made, n + 1)
                nc.vector.scalar_tensor_tensor(a_lo[:, par, b, :], act_g[:, s, :], S_A, a_hi[:, par, b, :],
                                               ALU.mult, ALU.subtract).then_inc(alo_made, 1)
                if not (isinstance(n, int) and n < NB):
                    add(g - 1, b)

            for t in range(0, TT, 2):
                nc.vector.memset(y[:, t:t + 2, :], 0.0).then_inc(added, 1)
            split_u(0, 0)
            steps(dve, body)
            for pair in range(TT // 2):
                add(NGRP - 1, pair)


def reload(nc, tag, dst, src):
    with ExitStack() as ctx:
        load = ctx.enter_context(nc.semaphore(f"{tag}_in"))
        block = ctx.enter_context(nc.Block())

        @block.sync
        def _(sp):
            sp.dma_start(dst[:, :, :], src.rearrange("(b p) d -> p b d", p=P)).then_inc(load, 16)
            sp.wait_ge(load, 16)


def build(nc, dram, out):
    scratch = {
        "qk_fox": nc.dram_tensor("qk_fox", [2 * FOX_H, AUG, T], F32, kind="Internal").ap(),
        "qk_swa": nc.dram_tensor("qk_swa", [SWA_H + SWA_KV, HD, T], F32, kind="Internal").ap(),
        "v": nc.dram_tensor("v_all", [T, V_W], F32, kind="Internal").ap(),
        "mix": nc.dram_tensor("mix", [T, D], F32, kind="Internal").ap(),
        "x_mid": nc.dram_tensor("x_mid", [T, D], F32, kind="Internal").ap(),
        "pq": nc.dram_tensor("pq", [P, NG, T], F32, kind="Internal").ap(),
        "gates": nc.dram_tensor("gates", [NK, NK, T], F32, kind="Internal").ap(),
    }
    x_rows = dram["x"][0]
    with ExitStack() as ctx:
        sb, ps, sem = ctx_tools(nc, ctx)
        ident, iota = sb("ident", [P, P]), sb("iota", [P, P])
        gate2 = sb("gate2", [P, D])
        h_hi, h_lo = sb("h_hi", [P, KD, T], F16), sb("h_lo", [P, KD, T], F16)
        kept = {"ident": ident, "iota": iota}
        with ExitStack() as front:
            fsb, _, _ = ctx_tools(nc, front)
            causal, mod, x = fsb("causal", [P, P]), fsb("mod", [P, N_MOD * D]), fsb("x_sb", [P, TT, D])
            kept |= {"causal": causal, "mod": mod, "x": x}
            with ExitStack() as c2:
                load = c2.enter_context(nc.semaphore("const_in"))
                block = c2.enter_context(nc.Block())

                @block.sync
                def _(sp):
                    sp.dma_start(ident[:, :], dram["ident"]).then_inc(load, 16)
                    sp.dma_start(iota[:, :], dram["iota"]).then_inc(load, 16)
                    sp.dma_start(causal[:, :], dram["causal"]).then_inc(load, 16)
                    sp.dma_start(x[:, :, :], x_rows.rearrange("(b p) d -> p b d", p=P)).then_inc(load, 16)
                    sp.wait_ge(load, 64)
            modulation(nc, dram, kept)
            row = [mod[:, i * D:(i + 1) * D] for i in range(N_MOD)]
            with ExitStack() as c3:
                h_t = c3.enter_context(nc.sbuf_tensor("h1_t", [P, KD, T], F32))
                norm_and_turn(nc, kept, "n1", row[1], row[0], (h_t, None, None))
                project_in(nc, dram, scratch, kept, h_t)
            fox_attention(nc, scratch, kept)
            swa_attention(nc, dram, scratch, kept)
            with ExitStack() as c3:
                y = c3.enter_context(nc.sbuf_tensor("y_mix", [P, TT, D], F32))
                project_out(nc, dram, scratch, kept, y)
                add_normed(nc, "am", x, y, row[2], EPS, scratch["x_mid"])
            with ExitStack() as c3:
                h_t = c3.enter_context(nc.sbuf_tensor("h2_t", [P, KD, T], F32))
                norm_and_turn(nc, kept, "n2", row[4], row[3], (h_t, h_hi, h_lo))
                peer_queries(nc, dram, scratch, h_t)
            with ExitStack() as c3:
                copied = c3.enter_context(nc.semaphore("gate2_copied"))
                block = c3.enter_context(nc.Block())

                @block.vector
                def _(dve):
                    nc.vector.tensor_copy(gate2[:, :], row[5]).then_inc(copied, 1)
                    dve.wait_ge(copied, 1)
        with ExitStack() as c3:
            slots = [c3.enter_context(nc.sbuf_tensor(f"slot_{n}", [P, T], F32)) for n in ("i1", "i2", "gate")]
            peer_pick(nc, dram, scratch, kept, slots)
            peer_gates(nc, scratch, kept, slots)
        with ExitStack() as c3:
            y = c3.enter_context(nc.sbuf_tensor("y_ffn", [P, TT, D], F32))
            peer_experts(nc, dram, scratch, kept, h_hi, h_lo, y)
            with ExitStack() as c4:
                x = c4.enter_context(nc.sbuf_tensor("x_again", [P, TT, D], F32))
                reload(nc, "xr", x, scratch["x_mid"])
                add_normed(nc, "af", x, y, gate2[:, :], EPS * (S_A * S_V) ** 2, out[0])


def constants():
    r = np.arange(P)
    dist = r[:, None] + P - np.arange(2 * P)[None, :]
    slopes = 2.0 ** (-8.0 * np.arange(1, SWA_H + 1) / SWA_H)
    bias = np.where(((dist >= 0) & (dist < P))[:, None, :], -slopes[None, :, None] * dist[:, None, :], NEG)
    return {
        "ident": np.eye(P, dtype=np.float32),
        "iota": np.ascontiguousarray(np.broadcast_to(r.astype(np.float32), (P, P))),
        "causal": np.where(r[None, :] <= r[:, None], 0.0, NEG).astype(np.float32),
        "swa_bias": bias.astype(np.float32),
    }


_INS = ["x", "c", "w_ada", "b_ada", "g_pre_mix", "g_post_mix", "g_pre_ffn", "g_post_ffn", "w_in", "b_fgate",
        "swa_sinks", "w_out", "w_query", "sub_keys", "w_u", "w_v"]


def declare(nc, arrays):
    dram = {name: nc.dram_tensor(f"in_{name}", list(a.shape), F32, kind="ExternalInput").ap()
            for name, a in arrays.items()}
    build(nc, dram, nc.dram_tensor("out", [1, T, D], F32, kind="ExternalOutput").ap())


def kernel(**inputs):
    import concourse.bacc as bacc
    from concourse.bass_utils import run_bass_kernel_spmd as run

    arrays = {name: np.ascontiguousarray(inputs[name]) for name in _INS}
    arrays.update(constants())
    nc = bacc.Bacc("TRN2", target_bir_lowering=False, num_devices=1)
    declare(nc, arrays)
    r = run(nc, [{f"in_{name}": a for name, a in arrays.items()}], core_ids=[0])
    return r.results[0]["out"]
```

```python
from contextlib import ExitStack

import numpy as np

import concourse.bass as bass
from concourse import mybir

F32 = mybir.dt.float32
F16 = mybir.dt.float16
U32 = mybir.dt.uint32
ALU = mybir.AluOpType
ACT = mybir.ActivationFunctionType
AX_X = mybir.AxisListType.X

P = 128
BANK = 512
D = 1024
T = 1024
KD = D // P
TT = T // P
N_MOD = 6
HD = 64
FOX_H, SWA_H, SWA_KV = 8, 8, 2
SWA_GROUP = SWA_H // SWA_KV
AUG = HD + 2
COL_FV = 2 * FOX_H * HD
COL_FF = 3 * FOX_H * HD
COL_SQ = COL_FF + FOX_H
COL_SK = COL_SQ + SWA_H * HD
COL_SV = COL_SK + SWA_KV * HD
IN_W = COL_SV + SWA_KV * HD
V_W = (FOX_H + SWA_KV) * HD
PH = 8
NG = 2 * PH
NK = 128
TOPK = 16
SLOTS = PH * TOPK
N_EXP = NK * NK
NBLK = N_EXP // P
GT = 2
TD = T - GT * P
GQ = GT * SLOTS
GRING, GBATCH = 4, 16
PIECE = 64
N_PIECE = TD // PIECE
EPS = 1e-6
NEG = -1e30
TAKEN = -3.0e38
SCALE = HD ** -0.5

S_H = 16.0
S_U = 64.0
S_A = 64.0
S_V = 64.0


def ctx_tools(nc, ctx):
    def sb(name, shape, dt=F32):
        return ctx.enter_context(nc.sbuf_tensor(name, shape, dt))

    def ps(name, shape, dt=F32):
        return ctx.enter_context(nc.psum_tensor(name, shape, dt))

    def sem(name):
        s = ctx.enter_context(nc.semaphore(name))
        ctx.callback(nc.sync.sem_clear, s)
        return s

    return sb, ps, sem


def turns(eng, count, body):
    body(0)
    with eng.Fori(1, count) as i:
        body(i)


def behind(eng, sem, value):
    if not isinstance(value, int) or value > 0:
        eng.wait_ge(sem, value)


class Chain:

    def __init__(self, eng, sem, start=0, waited=None):
        self.eng, self.sem, self.n, self.start, self.waited = eng, sem, 0, start, waited

    def wait(self, ins):
        ins.then_inc(self.sem, 1)
        self.n += 1
        self.eng.wait_ge(self.sem, self.start + self.n)

    def wait_alone(self, ins):
        self.wait(ins)
        self.eng.sem_inc(self.waited, 1)


def modulation(nc, dram, kept):
    SLICE = BANK
    NS = N_MOD * D // SLICE
    RING = 2
    with ExitStack() as ctx:
        sb, ps, sem = ctx_tools(nc, ctx)
        c_raw = sb("c_raw", [P, KD])
        c_silu = sb("c_silu", [P, KD])
        c_wide = sb("c_wide", [P, KD, P])
        w = sb("w_ada_ring", [P, RING, KD, SLICE])
        gains = sb("gains", [P, 4, D])
        mod = kept["mod"]
        out = [ps(f"mod_ps{i}", [P, BANK]) for i in range(RING)]
        small_in, silu_done, wide_done = sem("m_small_in"), sem("m_silu"), sem("m_wide")
        w_in = [sem(f"m_w_in{i}") for i in range(RING)]
        slice_made, slice_kept, rows = sem("m_slice_made"), sem("m_slice_kept"), sem("m_rows")
        block = ctx.enter_context(nc.Block())
        w_view = dram["w_ada"][0].rearrange("(p k) n -> p k n", k=KD)

        @block.sync
        def _(sp):
            sp.dma_start(c_raw[:, :], dram["c"].rearrange("b (p k) -> (b p) k", k=KD)).then_inc(small_in, 16)
            sp.dma_start(mod[:, :], dram["b_ada"][0:1, :].broadcast_to([P, N_MOD * D])).then_inc(small_in, 16)
            for i, name in enumerate(("g_pre_mix", "g_post_mix", "g_pre_ffn", "g_post_ffn")):
                sp.dma_start(gains[:, i, :], dram[name][0:1, :].broadcast_to([P, D])).then_inc(small_in, 16)
            for n in range(RING):
                sp.dma_start(w[:, n], w_view[:, :, n * SLICE:(n + 1) * SLICE]).then_inc(w_in[n], 16)
            with sp.Fori(0, NS // RING - 1) as it:
                for n in range(RING):
                    sp.wait_ge(slice_made, it * RING + n + 1)
                    sp.dma_start(w[:, n], w_view[:, :, bass.ds((it * RING + RING + n) * SLICE, SLICE)]) \
                        .then_inc(w_in[n], 16)

        @block.scalar
        def _(act):
            act.wait_ge(small_in, 96)
            nc.scalar.activation(c_silu[:, :], c_raw[:, :], ACT.Silu).then_inc(silu_done, 1)

        @block.tensor
        def _(pe):
            pe.wait_ge(wide_done, 1)
            with pe.Fori(0, NS // RING) as it:
                for n in range(RING):
                    pe.wait_ge(w_in[n], 16 * it + 16)
                    pe.wait_ge(slice_kept, it * RING + n + 1)
                    for k in range(KD):
                        mm = nc.tensor.matmul(out[n][:, :], c_wide[:, k, :], w[:, n, k, :],
                                              start=(k == 0), stop=(k == KD - 1))
                    mm.then_inc(slice_made, 1)

        @block.vector
        def _(dve):
            dve.wait_ge(silu_done, 1)
            nc.vector.tensor_copy(c_wide[:, :, :], c_silu[:, :, None].broadcast_to([P, KD, P])) \
                .then_inc(wide_done, 1)
            dve.sem_inc(slice_kept, RING)
            dve.wait_ge(small_in, 96)
            with dve.Fori(0, NS // RING) as it:
                for n in range(RING):
                    dve.wait_ge(slice_made, it * RING + n + 1)
                    col = bass.ds((it * RING + n) * SLICE, SLICE)
                    nc.vector.tensor_tensor(mod[:, col], out[n][:, :], mod[:, col], ALU.add) \
                        .then_inc(slice_kept, 1)
            dve.wait_ge(slice_kept, RING + NS)
            for i, (m, g) in enumerate(((1, 0), (4, 2))):
                row = mod[:, m * D:(m + 1) * D]
                nc.vector.scalar_tensor_tensor(row, row, 1.0, gains[:, g, :], ALU.add, ALU.mult).then_inc(rows, 1)
            for i, (m, g) in enumerate(((2, 1), (5, 3))):
                row = mod[:, m * D:(m + 1) * D]
                nc.vector.tensor_tensor(row, row, gains[:, g, :], ALU.mult).then_inc(rows, 1)
            dve.wait_ge(rows, 4)


def norm_and_turn(nc, kept, tag, scale_row, shift_row, outputs):
    x, ident = kept["x"], kept["ident"]
    h_turned, h_hi, h_lo, h_rows = outputs
    with ExitStack() as ctx:
        sb, ps, sem = ctx_tools(nc, ctx)
        squares = sb(f"{tag}_sq", [P, D])
        sums, var, root, inv, tmp = (sb(f"{tag}_{n}", [P, TT]) for n in ("sum", "var", "root", "inv", "tmp"))
        h = sb(f"{tag}_h", [P, 2, D])
        turned = [ps(f"{tag}_ps{i}", [P, 2, BANK]) for i in range(2)]
        squared, var_made, root_made, steps = (sem(f"{tag}_{n}") for n in ("s_sq", "s_var", "s_root", "s_step"))
        h_made, h_turned_sem, hi_made, kept_sem = (sem(f"{tag}_{n}") for n in ("s_h", "s_t", "s_hi", "s_k"))
        block = ctx.enter_context(nc.Block())

        @block.scalar
        def _(act):
            for t in range(TT):
                if t:
                    act.wait_ge(squared, t)
                nc.scalar.activation(squares[:, :], x[:, t, :], ACT.Square,
                                     accum_out=sums[:, t:t + 1]).then_inc(squared, 1)
            act.wait_ge(var_made, 1)
            nc.scalar.activation(root[:, :], var[:, :], ACT.Sqrt).then_inc(root_made, 1)
            for t in range(TT):
                act.wait_ge(h_turned_sem, t + 1)
                src = turned[t % 2][:, :, :].rearrange("p a (k c) -> p (a k) c", c=P)
                if h_hi is None:
                    nc.scalar.copy(h_turned[:, :, t * P:(t + 1) * P], src).then_inc(kept_sem, 1)
                else:
                    nc.scalar.activation(h_hi[:, :, t * P:(t + 1) * P], src, ACT.Copy, scale=S_H) \
                        .then_inc(hi_made, 1)

        @block.vector
        def _(dve):
            ch = Chain(dve, steps)
            dve.wait_ge(squared, TT)
            nc.vector.tensor_scalar(var[:, :], sums[:, :], 1.0 / D, EPS, ALU.mult, ALU.add).then_inc(var_made, 1)
            dve.wait_ge(root_made, 1)
            ch.wait(nc.vector.reciprocal(inv[:, :], root[:, :]))
            dve.wait_ge(var_made, 1)
            ch.wait(nc.vector.tensor_tensor(tmp[:, :], inv[:, :], inv[:, :], ALU.mult))
            ch.wait(nc.vector.tensor_tensor(tmp[:, :], tmp[:, :], var[:, :], ALU.mult))
            ch.wait(nc.vector.tensor_scalar(tmp[:, :], tmp[:, :], -0.5, 1.5, ALU.mult, ALU.add))
            ch.wait(nc.vector.tensor_tensor(inv[:, :], inv[:, :], tmp[:, :], ALU.mult))

            def keep(t):
                src = turned[t % 2][:, :, :].rearrange("p a (k c) -> p (a k) c", c=P)
                if h_hi is not None:
                    dve.wait_ge(hi_made, t + 1)
                    nc.vector.scalar_tensor_tensor(h_lo[:, :, t * P:(t + 1) * P], src, S_H,
                                                   h_hi[:, :, t * P:(t + 1) * P], ALU.mult, ALU.subtract) \
                        .then_inc(kept_sem, 1)

            for t in range(TT):
                if t >= 2:
                    dve.wait_ge(h_turned_sem, t - 1)
                ch.wait(nc.vector.scalar_tensor_tensor(h[:, t % 2, :], x[:, t, :], inv[:, t:t + 1], scale_row,
                                                       ALU.mult, ALU.mult))
                if h_rows is not None and t < GT:
                    nc.vector.tensor_tensor(h_rows[:, t, :], h[:, t % 2, :], shift_row, ALU.add)
                nc.vector.tensor_tensor(h[:, t % 2, :], h[:, t % 2, :], shift_row, ALU.add).then_inc(h_made, 1)
                if t >= 1:
                    keep(t - 1)
            keep(TT - 1)

        @block.tensor
        def _(pe):
            for t in range(TT):
                pe.wait_ge(h_made, t + 1)
                if t >= 2:
                    pe.wait_ge(kept_sem, t - 1)
                for k in range(KD):
                    tr = nc.tensor.transpose(turned[t % 2][:, k // 4, (k % 4) * P:(k % 4 + 1) * P],
                                             h[:, t % 2, k * P:(k + 1) * P], ident[:, :])
                tr.then_inc(h_turned_sem, 1)


def project_in(nc, dram, scratch, kept, h_t):
    with ExitStack() as ctx:
        sb, ps, sem = ctx_tools(nc, ctx)
        RING = 3
        w = sb("w_ring", [P, RING, KD, P])
        w_v = sb("w_v", [P, KD, V_W])
        w_f = sb("w_f", [P, KD, FOX_H])
        wide = sb("qk_rows", [P, 2, T])
        vals = sb("v_rows", [P, 2, V_W])
        bias_f = sb("bias_f", [FOX_H, 1])
        f_logit, f_abs, f_exp, f_min, f_one = (
            sb(f"f_{n}", [FOX_H, T]) for n in ("logit", "abs", "exp", "min", "one"))
        f_sum, f_neg = f_logit, f_exp
        acc = [ps(f"in_ps{i}", [P, 2, BANK]) for i in range(2)]
        acc_v = [ps(f"in_psv{i}", [P, 2, BANK]) for i in range(2)]
        w_in = [sem(f"i_w{i}") for i in range(RING)]
        wv_in, small_in, f_steps = sem("i_wv"), sem("i_small"), sem("i_f")
        made, taken, v_made, v_taken = sem("i_made"), sem("i_taken"), sem("i_vmade"), sem("i_vtaken")
        stored = [sem(f"i_st{i}") for i in range(2)]
        v_stored = [sem(f"i_vst{i}") for i in range(2)]
        f_act, f_stored = sem("i_fact"), sem("i_fst")
        block = ctx.enter_context(nc.Block())
        w_view = dram["w_in"][0].rearrange("(k p) n -> p k n", p=P)
        tiles = [(j * P, SCALE if j < 4 else 1.0, scratch["qk_fox"][2 * j:2 * j + 2, 0:HD, :]) for j in range(8)]
        tiles += [(COL_SQ + j * P, SCALE if j < 4 else 1.0, scratch["qk_swa"][2 * j:2 * j + 2]) for j in range(5)]
        NTL = len(tiles)

        @block.sync
        def _(sp):
            sp.dma_start(w_f[:, :, :], w_view[:, :, COL_FF:COL_SQ]).then_inc(small_in, 16)
            sp.dma_start(bias_f[:, :], dram["b_fgate"].rearrange("a h -> h a")).then_inc(small_in, 16)
            for j in range(NTL):
                if j >= RING:
                    sp.wait_ge(made, j - RING + 1)
                sp.dma_start(w[:, j % RING], w_view[:, :, tiles[j][0]:tiles[j][0] + P]).then_inc(w_in[j % RING], 16)
                if j == 4:
                    sp.dma_start(w_v[:, :, 0:FOX_H * HD], w_view[:, :, COL_FV:COL_FF]).then_inc(wv_in, 16)
                    sp.dma_start(w_v[:, :, FOX_H * HD:], w_view[:, :, COL_SV:IN_W]).then_inc(wv_in, 16)
            for s in range(2):
                sp.wait_ge(stored[s], 16 * 2 * ((NTL - s + 1) // 2))
                sp.wait_ge(v_stored[s], 16 * TT // 2)
            sp.wait_ge(f_stored, 16 * 4)

        @block.tensor
        def _(pe):
            pe.wait_ge(small_in, 32)
            for half in range(2):
                for k in range(KD):
                    mm = nc.tensor.matmul(acc_v[0][0:FOX_H, half, :], w_f[:, k, :], h_t[:, k, half * BANK:(half + 1) * BANK],
                                          start=(k == 0), stop=(k == KD - 1))
            mm.then_inc(v_made, 1)
            for j in range(NTL):
                pe.wait_ge(w_in[j % RING], 16 * (j // RING + 1))
                if j >= 2:
                    pe.wait_ge(taken, j - 1)
                for half in range(2):
                    for k in range(KD):
                        mm = nc.tensor.matmul(acc[j % 2][:, half, :], w[:, j % RING, k, :],
                                              h_t[:, k, half * BANK:(half + 1) * BANK],
                                              start=(k == 0), stop=(k == KD - 1))
                mm.then_inc(made, 1)
            pe.wait_ge(wv_in, 32)
            for t in range(TT):
                pe.wait_ge(v_taken, max(t, 1))
                for lo, hi, half in ((0, BANK, 0), (BANK, V_W, 1)):
                    for k in range(KD):
                        mm = nc.tensor.matmul(acc_v[t % 2][:, half, 0:hi - lo], h_t[:, k, t * P:(t + 1) * P],
                                              w_v[:, k, lo:hi], start=(k == 0), stop=(k == KD - 1))
                mm.then_inc(v_made, 1)

        @block.scalar
        def _(act):
            act.wait_ge(f_steps, 1)
            nc.scalar.activation(f_abs[:, :], f_logit[:, :], ACT.Abs).then_inc(f_act, 1)
            act.wait_ge(f_act, 1)
            nc.scalar.activation(f_exp[:, :], f_abs[:, :], ACT.Exp, scale=-1.0).then_inc(f_act, 1)
            act.wait_ge(f_act, 2)
            nc.scalar.activation(f_abs[:, :], f_exp[:, :], ACT.Ln, bias=1.0).then_inc(f_act, 1)
            for j in range(NTL):
                act.wait_ge(made, j + 1)
                if j >= 2:
                    act.wait_ge(stored[j % 2], 32 * (j // 2))
                nc.scalar.activation(wide[:, j % 2, :], acc[j % 2][:, :, :].rearrange("p a b -> p (a b)"), ACT.Copy,
                                     scale=tiles[j][1]).then_inc(taken, 1)
                act.wait_ge(taken, j + 1)
                for head in range(2):
                    act.dma_start(tiles[j][2][head], wide[head * HD:(head + 1) * HD, j % 2, :]) \
                        .then_inc(stored[j % 2], 16)

        @block.vector
        def _(dve):
            dve.wait_ge(v_made, 1)
            nc.vector.tensor_scalar(f_logit[:, :], acc_v[0][0:FOX_H, :, :].rearrange("p a b -> p (a b)"),
                                    bias_f[:, 0:1], None, ALU.add).then_inc(f_steps, 1)
            dve.wait_ge(f_steps, 1)
            nc.vector.tensor_scalar(f_min[:, :], f_logit[:, :], 0.0, None, ALU.min).then_inc(v_taken, 1)
            nc.vector.memset(f_one[:, :], 1.0).then_inc(f_steps, 1)
            dve.wait_ge(f_act, 3)
            dve.wait_ge(v_taken, 1)
            nc.vector.tensor_tensor(f_min[:, :], f_min[:, :], f_abs[:, :], ALU.subtract).then_inc(f_steps, 1)
            dve.wait_ge(f_steps, 3)
            nc.vector.tensor_tensor_scan(f_sum[:, :], f_one[:, :], f_min[:, :], 0.0, ALU.mult, ALU.add) \
                .then_inc(f_steps, 1)
            dve.wait_ge(f_steps, 4)
            nc.vector.tensor_scalar(f_neg[:, :], f_sum[:, :], -1.0, None, ALU.mult).then_inc(f_steps, 1)
            for t in range(TT):
                dve.wait_ge(v_made, t + 2)
                if t >= 2:
                    dve.wait_ge(v_stored[t % 2], 16 * (t // 2))
                nc.vector.tensor_copy(vals[:, t % 2, :],
                                      acc_v[t % 2][:, :, :].rearrange("p a b -> p (a b)")[:, 0:V_W]).then_inc(v_taken, 1)

        @block.gpsimd
        def _(pool):
            pool.wait_ge(f_steps, 5)
            rows = scratch["qk_fox"]
            pool.dma_start(rows[0:FOX_H, HD, :], f_sum[:, :]).then_inc(f_stored, 16)
            pool.dma_start(rows[0:FOX_H, HD + 1, :], f_one[:, :]).then_inc(f_stored, 16)
            pool.dma_start(rows[FOX_H:, HD, :], f_one[:, :]).then_inc(f_stored, 16)
            pool.dma_start(rows[FOX_H:, HD + 1, :], f_neg[:, :]).then_inc(f_stored, 16)
            for t in range(TT):
                pool.wait_ge(v_taken, t + 2)
                pool.dma_start(scratch["v"][t * P:(t + 1) * P, :], vals[:, t % 2, :]).then_inc(v_stored[t % 2], 16)


def fox_attention(nc, scratch, kept):
    ident, causal = kept["ident"], kept["causal"]
    with ExitStack() as ctx:
        sb, ps, sem = ctx_tools(nc, ctx)
        q, k = sb("fx_q", [AUG, 2, T]), sb("fx_k", [AUG, 2, T])
        v = sb("fx_v", [P, 2, TT, HD])
        prob, prob_t = sb("fx_p", [P, 2, T]), sb("fx_pt", [P, 2, T])
        n_max, row_sum, inv = (sb(f"fx_{n}", [P, 2 * TT]) for n in ("max", "sum", "inv"))
        out = sb("fx_out", [P, 2, TT, HD])
        score = [ps(f"fx_s{i}", [P, 2 * BANK]) for i in range(2)]
        turned = ps("fx_t", [P, 2 * BANK])
        mixed = [ps(f"fx_o{i}", [P, HD]) for i in range(2)]
        head_in = [sem(f"fx_in{i}") for i in range(2)]
        scored, masked, maxed, probed = (sem(f"fx_{n}") for n in ("scored", "masked", "maxed", "probed"))
        turn_made, turn_kept, mix_made, inv_made, mix_kept = (
            sem(f"fx_{n}") for n in ("turned", "tkept", "mixm", "invm", "mixk"))
        stored = [sem(f"fx_st{i}") for i in range(2)]
        block = ctx.enter_context(nc.Block())
        NI = FOX_H // 2
        units = [(h, i) for h in range(2) for i in range(TT)]
        NU = len(units)

        @block.sync
        def _(sp):
            def turn(it):
                for h in range(2):
                    behind(sp, mix_made, it * NU + TT * h)
                    head = it * 2 + h
                    sp.dma_start(q[:, h, :], scratch["qk_fox"][bass.ds(head, 1), :, :].rearrange("h r t -> (h r) t")) \
                        .then_inc(head_in[h], 16)
                    sp.dma_start(k[:, h, :], scratch["qk_fox"][bass.ds(head + FOX_H, 1), :, :]
                                 .rearrange("h r t -> (h r) t")).then_inc(head_in[h], 16)
                    sp.dma_start(v[:, h, :, :], scratch["v"][:, bass.ds(head * HD, HD)]
                                 .rearrange("(b p) d -> p b d", p=P)).then_inc(head_in[h], 16)

            turns(sp, NI, turn)

        @block.tensor
        def _(pe):
            pe.sem_inc(mix_made, TT)
            def turn(it):
                def scores(u):
                    h, i = units[u]
                    if i == 0:
                        pe.wait_ge(head_in[h], 48 * it + 48)
                    pe.wait_ge(probed, it * NU + u + 1)
                    for c in range(0, (i + 1) * P, BANK):
                        w = min(BANK, (i + 1) * P - c)
                        mm = nc.tensor.matmul(score[u % 2][:, c:c + w], q[:, h, i * P:(i + 1) * P],
                                              k[:, h, c:c + w], start=True, stop=True)
                    mm.then_inc(scored, 1)

                def mix(u):
                    h, i = units[u]
                    pe.wait_ge(probed, it * NU + u + 1 + 2)
                    pe.wait_ge(turn_kept, it * NU + u + 1)
                    for b in range(i + 1):
                        tr = nc.tensor.transpose(turned[:, b * P:(b + 1) * P], prob[:, u % 2, b * P:(b + 1) * P],
                                                 ident[:, :])
                    tr.then_inc(turn_made, 1)

                def weigh(u):
                    h, i = units[u]
                    pe.wait_ge(turn_kept, it * NU + u + 1 + 1)
                    pe.wait_ge(mix_kept, it * NU + u + 1)
                    for b in range(i + 1):
                        mm = nc.tensor.matmul(mixed[u % 2][:, :], prob_t[:, u % 2, b * P:(b + 1) * P], v[:, h, b, :],
                                              start=(b == 0), stop=(b == i))
                    mm.then_inc(mix_made, 1)

                scores(0)
                for u in range(NU):
                    if u + 1 < NU:
                        scores(u + 1)
                    mix(u)
                    weigh(u)

            turns(pe, NI, turn)

        @block.vector
        def _(dve):
            dve.sem_inc(turn_kept, 1)
            dve.sem_inc(mix_kept, 2)
            def turn(it):
                def stats(u):
                    h, i = units[u]
                    dve.wait_ge(scored, it * NU + u + 1)
                    diag = score[u % 2][:, i * P:(i + 1) * P]
                    nc.vector.tensor_tensor(diag, diag, causal[:, :], ALU.add).then_inc(masked, 1)
                    dve.wait_ge(masked, it * NU + u + 1)
                    nc.vector.tensor_reduce(n_max[:, u:u + 1], score[u % 2][:, 0:(i + 1) * P], AX_X, ALU.max,
                                            negate=True).then_inc(maxed, 1)

                def keep(u):
                    h, i = units[u]
                    dve.wait_ge(turn_made, it * NU + u + 1)
                    dve.wait_ge(mix_made, it * NU + u - 1 + TT)
                    nc.vector.tensor_copy(prob_t[:, u % 2, 0:(i + 1) * P], turned[:, 0:(i + 1) * P]) \
                        .then_inc(turn_kept, 1)
                    nc.vector.reciprocal(inv[:, u:u + 1], row_sum[:, u:u + 1]).then_inc(inv_made, 1)

                def norm(u):
                    h, i = units[u]
                    dve.wait_ge(mix_made, it * NU + u + 1 + TT)
                    dve.wait_ge(inv_made, it * NU + u + 1)
                    if i == 0:
                        behind(dve, stored[h], it * 16)
                    nc.vector.tensor_scalar(out[:, h, i, :], mixed[u % 2][:, :], inv[:, u:u + 1], None, ALU.mult) \
                        .then_inc(mix_kept, 1)

                stats(0)
                for u in range(NU):
                    if u + 1 < NU:
                        stats(u + 1)
                    keep(u)
                    norm(u)

            turns(dve, NI, turn)

        @block.scalar
        def _(act):
            act.sem_inc(probed, 2)
            def turn(it):
                for u, (h, i) in enumerate(units):
                    act.wait_ge(maxed, it * NU + u + 1)
                    if u >= 2:
                        behind(act, inv_made, it * NU + u - 1)
                    else:
                        behind(act, inv_made, it * NU)
                    nc.scalar.activation(prob[:, u % 2, 0:(i + 1) * P], score[u % 2][:, 0:(i + 1) * P], ACT.Exp,
                                         bias=n_max[:, u:u + 1], accum_out=row_sum[:, u:u + 1]).then_inc(probed, 1)

            turns(act, NI, turn)

        @block.gpsimd
        def _(pool):
            def turn(it):
                for h in range(2):
                    pool.wait_ge(mix_kept, it * NU + TT * (h + 1) + 2)
                    pool.dma_start(scratch["mix"][:, bass.ds((it * 2 + h) * HD, HD)].rearrange("(b p) d -> p b d", p=P),
                                   out[:, h, :, :]).then_inc(stored[h], 16)

            turns(pool, NI, turn)
            for h in range(2):
                pool.wait_ge(stored[h], 16 * NI)


def swa_attention(nc, dram, scratch, kept):
    ident = kept["ident"]
    G = SWA_GROUP
    with ExitStack() as ctx:
        sb, ps, sem = ctx_tools(nc, ctx)
        q, k = sb("sw_q", [HD, SWA_H, T]), sb("sw_k", [HD, SWA_KV, T])
        v = sb("sw_v", [P, TT, SWA_KV * HD])
        bias = sb("sw_bias", [P, SWA_H, 2 * P])
        sink = sb("sw_sink", [P, SWA_H])
        prob, prob_t = sb("sw_p", [P, 2, G, 2 * P]), sb("sw_pt", [P, 2, G, 2 * P])
        out = sb("sw_out", [P, TT, SWA_H, HD])
        NU = SWA_KV * TT
        top, n_max, less, sink_exp, row_sum, total, inv = (
            sb(f"sw_{n}", [P, NU, G]) for n in ("top", "max", "less", "sexp", "sum", "tot", "inv"))
        score = [ps(f"sw_s{i}", [P, G, 2 * P]) for i in range(2)]
        turned = ps("sw_t", [P, G, 2 * P])
        mixed = [ps(f"sw_o{i}", [P, G, HD]) for i in range(2)]
        load, scored, biased, tops, maxed, lessed, probed = (
            sem(f"sw_{n}") for n in ("load", "scored", "biased", "tops", "maxed", "lessed", "probed"))
        turn_made, turn_kept, mix_made, totaled, inv_made, mix_kept, stored = (
            sem(f"sw_{n}") for n in ("turned", "tkept", "mixm", "tot", "invm", "mixk", "stored"))
        block = ctx.enter_context(nc.Block())
        units = [(g, i) for g in range(SWA_KV) for i in range(TT)]

        def spans(i):
            return [(1, 0)] if i == 0 else [(0, i - 1), (1, i)]

        def band(i):
            return slice(P, 2 * P) if i == 0 else slice(0, 2 * P)

        @block.sync
        def _(sp):
            sp.dma_start(q[:, :, :], scratch["qk_swa"][0:SWA_H].rearrange("h r t -> r h t")).then_inc(load, 16)
            sp.dma_start(k[:, :, :], scratch["qk_swa"][SWA_H:].rearrange("h r t -> r h t")).then_inc(load, 16)
            sp.dma_start(v[:, :, :], scratch["v"][:, FOX_H * HD:].rearrange("(b p) d -> p b d", p=P)).then_inc(load, 16)
            sp.dma_start(bias[:, :, :], dram["swa_bias"]).then_inc(load, 16)
            sp.dma_start(sink[:, :], dram["swa_sinks"][0:1, :].broadcast_to([P, SWA_H])).then_inc(load, 16)
            sp.wait_ge(mix_kept, NU)
            sp.dma_start(scratch["mix"][:, FOX_H * HD:].rearrange("(b p) d -> p b d", p=P),
                         out[:, :, :, :].rearrange("p b h d -> p b (h d)")).then_inc(stored, 16)
            sp.wait_ge(stored, 16)

        @block.tensor
        def _(pe):
            pe.wait_ge(load, 80)

            def scores(u):
                g, i = units[u]
                if u >= 2:
                    pe.wait_ge(probed, (G + 1) * (u - 1))
                for n in range(G):
                    for place, b in spans(i):
                        mm = nc.tensor.matmul(score[u % 2][:, n, place * P:(place + 1) * P],
                                              q[:, g * G + n, i * P:(i + 1) * P], k[:, g, b * P:(b + 1) * P],
                                              start=True, stop=True)
                mm.then_inc(scored, 1)

            scores(0)
            for u, (g, i) in enumerate(units):
                if u + 1 < NU:
                    scores(u + 1)
                pe.wait_ge(probed, (G + 1) * (u + 1))
                if u >= 1:
                    pe.wait_ge(turn_kept, u)
                for n in range(G):
                    for place, b in spans(i):
                        tr = nc.tensor.transpose(turned[:, n, place * P:(place + 1) * P],
                                                 prob[:, u % 2, n, place * P:(place + 1) * P], ident[:, :])
                tr.then_inc(turn_made, 1)
                pe.wait_ge(turn_kept, u + 1)
                if u >= 2:
                    pe.wait_ge(mix_kept, u - 1)
                for n in range(G):
                    sp_ = spans(i)
                    for place, b in sp_:
                        mm = nc.tensor.matmul(mixed[u % 2][:, n, :], prob_t[:, u % 2, n, place * P:(place + 1) * P],
                                              v[:, b, g * HD:(g + 1) * HD],
                                              start=(place == sp_[0][0]), stop=(place == 1))
                mm.then_inc(mix_made, 1)

        @block.vector
        def _(dve):
            dve.wait_ge(load, 80)

            def stats(u):
                g, i = units[u]
                s = score[u % 2][:, :, band(i)]
                dve.wait_ge(scored, u + 1)
                nc.vector.tensor_tensor(s, s, bias[:, g * G:(g + 1) * G, band(i)], ALU.add).then_inc(biased, 1)
                dve.wait_ge(biased, u + 1)
                nc.vector.tensor_reduce(top[:, u, :], s, AX_X, ALU.max).then_inc(tops, 1)
                dve.wait_ge(tops, 2 * u + 1)
                nc.vector.tensor_tensor(top[:, u, :], top[:, u, :], sink[:, g * G:(g + 1) * G], ALU.max).then_inc(tops, 1)
                dve.wait_ge(tops, 2 * u + 2)
                nc.vector.tensor_scalar(n_max[:, u, :], top[:, u, :], -1.0, None, ALU.mult).then_inc(maxed, 1)
                nc.vector.tensor_tensor(less[:, u, :], sink[:, g * G:(g + 1) * G], top[:, u, :], ALU.subtract) \
                    .then_inc(lessed, 1)

            def keep(u):
                g, i = units[u]
                dve.wait_ge(turn_made, u + 1)
                if u >= 2:
                    dve.wait_ge(mix_made, u - 1)
                nc.vector.tensor_copy(prob_t[:, u % 2, :, band(i)], turned[:, :, band(i)]).then_inc(turn_kept, 1)
                nc.vector.tensor_tensor(total[:, u, :], row_sum[:, u, :], sink_exp[:, u, :], ALU.add).then_inc(totaled, 1)
                dve.wait_ge(totaled, u + 1)
                nc.vector.reciprocal(inv[:, u, :], total[:, u, :]).then_inc(inv_made, 1)
                dve.wait_ge(mix_made, u + 1)
                dve.wait_ge(inv_made, u + 1)
                nc.vector.tensor_tensor(out[:, i, g * G:(g + 1) * G, :], mixed[u % 2][:, :, :],
                                        inv[:, u, :, None].broadcast_to([P, G, HD]), ALU.mult).then_inc(mix_kept, 1)

            stats(0)
            for u in range(NU):
                if u + 1 < NU:
                    stats(u + 1)
                keep(u)

        @block.scalar
        def _(act):
            for u, (g, i) in enumerate(units):
                act.wait_ge(maxed, u + 1)
                act.wait_ge(lessed, u + 1)
                if u >= 2:
                    act.wait_ge(turn_made, u - 1)
                for n in range(G):
                    nc.scalar.activation(prob[:, u % 2, n, band(i)], score[u % 2][:, n, band(i)], ACT.Exp,
                                         bias=n_max[:, u, n:n + 1], accum_out=row_sum[:, u, n:n + 1]).then_inc(probed, 1)
                nc.scalar.activation(sink_exp[:, u, :], less[:, u, :], ACT.Exp).then_inc(probed, 1)


def project_out(nc, dram, scratch, kept, y):
    ident = kept["ident"]
    with ExitStack() as ctx:
        sb, ps, sem = ctx_tools(nc, ctx)
        w = sb("wo", [P, KD, D])
        m = sb("wo_m", [P, TT, D])
        m_t = sb("wo_mt", [P, 2, D])
        turned = ps("wo_t", [P, 2 * BANK])
        acc = [ps(f"wo_y{i}", [P, 2 * BANK]) for i in range(2)]
        load, turn_made, turn_kept, y_made, y_kept = (sem(f"wo_{n}") for n in ("ld", "tm", "tk", "ym", "yk"))
        block = ctx.enter_context(nc.Block())

        @block.sync
        def _(sp):
            sp.dma_start(m[:, :, :], scratch["mix"].rearrange("(b p) d -> p b d", p=P)).then_inc(load, 16)
            sp.dma_start(w[:, :, :], dram["w_out"][0].rearrange("(k p) n -> p k n", p=P)).then_inc(load, 16)

        @block.tensor
        def _(pe):
            pe.wait_ge(load, 32)

            def turn(t):
                if t >= 1:
                    pe.wait_ge(turn_kept, t)
                for k in range(KD):
                    tr = nc.tensor.transpose(turned[:, k * P:(k + 1) * P], m[:, t, k * P:(k + 1) * P], ident[:, :])
                tr.then_inc(turn_made, 1)

            turn(0)
            for t in range(TT):
                if t + 1 < TT:
                    turn(t + 1)
                pe.wait_ge(turn_kept, t + 1)
                if t >= 2:
                    pe.wait_ge(y_kept, t - 1)
                for half in range(2):
                    for k in range(KD):
                        mm = nc.tensor.matmul(acc[t % 2][:, half * BANK:(half + 1) * BANK],
                                              m_t[:, t % 2, k * P:(k + 1) * P], w[:, k, half * BANK:(half + 1) * BANK],
                                              start=(k == 0), stop=(k == KD - 1))
                mm.then_inc(y_made, 1)

        @block.vector
        def _(dve):
            for t in range(TT):
                dve.wait_ge(turn_made, t + 1)
                if t >= 2:
                    dve.wait_ge(y_made, t - 1)
                nc.vector.tensor_copy(m_t[:, t % 2, :], turned[:, :]).then_inc(turn_kept, 1)

        @block.scalar
        def _(act):
            for t in range(TT):
                act.wait_ge(y_made, t + 1)
                nc.scalar.copy(y[:, t, :], acc[t % 2][:, :]).then_inc(y_kept, 1)


def add_normed(nc, tag, x, y, gate_row, eps, store_to):
    with ExitStack() as ctx:
        sb, ps, sem = ctx_tools(nc, ctx)
        squares = sb(f"{tag}_sq", [P, D])
        sums, var, root, inv, tmp = (sb(f"{tag}_{n}", [P, TT]) for n in ("sum", "var", "root", "inv", "tmp"))
        squared, var_made, root_made, steps, added, stored = (
            sem(f"{tag}_{n}") for n in ("s_sq", "s_var", "s_root", "s_step", "s_add", "s_st"))
        block = ctx.enter_context(nc.Block())

        @block.scalar
        def _(act):
            for t in range(TT):
                if t:
                    act.wait_ge(squared, t)
                nc.scalar.activation(squares[:, :], y[:, t, :], ACT.Square,
                                     accum_out=sums[:, t:t + 1]).then_inc(squared, 1)
            act.wait_ge(var_made, 1)
            nc.scalar.activation(root[:, :], var[:, :], ACT.Sqrt).then_inc(root_made, 1)

        @block.vector
        def _(dve):
            ch = Chain(dve, steps)
            dve.wait_ge(squared, TT)
            nc.vector.tensor_scalar(var[:, :], sums[:, :], 1.0 / D, eps, ALU.mult, ALU.add).then_inc(var_made, 1)
            dve.wait_ge(root_made, 1)
            ch.wait(nc.vector.reciprocal(inv[:, :], root[:, :]))
            dve.wait_ge(var_made, 1)
            ch.wait(nc.vector.tensor_tensor(tmp[:, :], inv[:, :], inv[:, :], ALU.mult))
            ch.wait(nc.vector.tensor_tensor(tmp[:, :], tmp[:, :], var[:, :], ALU.mult))
            ch.wait(nc.vector.tensor_scalar(tmp[:, :], tmp[:, :], -0.5, 1.5, ALU.mult, ALU.add))
            ch.wait(nc.vector.tensor_tensor(inv[:, :], inv[:, :], tmp[:, :], ALU.mult))
            for t in range(TT):
                ch.wait(nc.vector.scalar_tensor_tensor(y[:, t, :], y[:, t, :], inv[:, t:t + 1], gate_row,
                                                       ALU.mult, ALU.mult))
                nc.vector.tensor_tensor(x[:, t, :], x[:, t, :], y[:, t, :], ALU.add).then_inc(added, 1)
            dve.wait_ge(added, TT)

        @block.sync
        def _(sp):
            for t in range(TT):
                sp.wait_ge(added, t + 1)
                sp.dma_start(store_to[t * P:(t + 1) * P, :], x[:, t, :]).then_inc(stored, 16)
            sp.wait_ge(stored, 16 * TT)


def peer_queries(nc, dram, scratch, h_hi, h_lo):
    with ExitStack() as ctx:
        sb, ps, sem = ctx_tools(nc, ctx)
        w = sb("wq_raw", [P, 2, KD, P])
        w_hi, w_lo = sb("wq_hi", [P, 2, KD, P], F16), sb("wq_lo", [P, 2, KD, P], F16)
        rows = sb("pq_rows", [P, 2, T])
        acc = [ps(f"pq_ps{i}", [P, 2 * BANK]) for i in range(2)]
        w_in = [sem(f"pq_w{i}") for i in range(2)]
        hi_made, lo_made, made, taken = sem("pq_hi"), sem("pq_lo"), sem("pq_made"), sem("pq_taken")
        stored = [sem(f"pq_st{i}") for i in range(2)]
        block = ctx.enter_context(nc.Block())
        w_view = dram["w_query"][0].rearrange("(k p) n -> p k n", p=P)
        NP = NG // 2

        @block.sync
        def _(sp):
            def turn(it):
                for s in range(2):
                    behind(sp, lo_made, it * 2 + s - 1)
                    sp.dma_start(w[:, s], w_view[:, :, bass.ds((it * 2 + s) * P, P)]).then_inc(w_in[s], 16)

            turns(sp, NP, turn)

        @block.scalar
        def _(act):
            def turn(it):
                for s in range(2):
                    act.wait_ge(w_in[s], 16 * it + 16)
                    behind(act, made, it * 2 + s - 1)
                    nc.scalar.activation(w_hi[:, s], w[:, s], ACT.Copy, scale=S_U).then_inc(hi_made, 1)
                    if s == 0 and isinstance(it, int):
                        continue
                    g = it * 2 + s - 1
                    act.wait_ge(made, g + 1)
                    behind(act, stored[1 - s], it * 16 - 16 if s == 0 else it * 16)
                    nc.scalar.activation(rows[:, 1 - s, :], acc[1 - s][:, :], ACT.Copy, scale=1.0 / (S_H * S_U)) \
                        .then_inc(taken, 1)

            turns(act, NP, turn)
            act.wait_ge(made, NG)
            act.wait_ge(stored[1], 16 * (NP - 1))
            nc.scalar.activation(rows[:, 1, :], acc[1][:, :], ACT.Copy, scale=1.0 / (S_H * S_U)).then_inc(taken, 1)

        @block.vector
        def _(dve):
            with dve.Fori(0, NP) as it:
                for s in range(2):
                    dve.wait_ge(hi_made, it * 2 + s + 1)
                    nc.vector.scalar_tensor_tensor(w_lo[:, s], w[:, s], S_U, w_hi[:, s],
                                                   ALU.mult, ALU.subtract).then_inc(lo_made, 1)

        @block.tensor
        def _(pe):
            def turn(it):
                for s in range(2):
                    pe.wait_ge(lo_made, it * 2 + s + 1)
                    behind(pe, taken, it * 2 + s - 1)
                    for c in range(KD):
                        for wt, h, first, last in ((w_hi, h_hi, c == 0, False), (w_hi, h_lo, False, False),
                                                   (w_lo, h_hi, False, c == KD - 1)):
                            for half in range(2):
                                cols = slice(half * BANK, (half + 1) * BANK)
                                mm = nc.tensor.matmul(acc[s][:, cols], wt[:, s, c, :], h[:, c, cols],
                                                      start=first, stop=last)
                    mm.then_inc(made, 1)

            turns(pe, NP, turn)

        @block.gpsimd
        def _(pool):
            with pool.Fori(0, NP) as it:
                for s in range(2):
                    pool.wait_ge(taken, it * 2 + s + 1)
                    pool.dma_start(scratch["pq"][:, bass.ds(it * 2 + s, 1), :].rearrange("p g t -> p (g t)"),
                                   rows[:, s, :]).then_inc(stored[s], 16)
            for s in range(2):
                pool.wait_ge(stored[s], 16 * NP)


def peer_scores(nc, dram, scratch, kept, h_hi, h_lo, h_rows, coef, expert):
    ident, iota = kept["ident"], kept["iota"]
    PICK_B = 5
    GATE_STEPS, GATE_TOK = 48, TD // 48
    REST_STEPS = NBLK - TT * PICK_B - GATE_STEPS
    GATE_DOTS, REST_DOTS = 2, 4
    N0_GATE, N0_REST = TT * PICK_B, TT * PICK_B + GATE_STEPS
    assert GATE_STEPS * GATE_DOTS + REST_STEPS * REST_DOTS == GQ
    PIECE_STEPS = PIECE // GATE_TOK
    SUB = 4
    SUBS = GATE_TOK // SUB
    with ExitStack() as ctx:
        sb, ps, sem = ctx_tools(nc, ctx)
        u_raw = sb("xu_raw", [P, 2, D])
        u_hi, u_lo = sb("xu_hi", [P, 2, KD, P], F16), sb("xu_lo", [P, 2, KD, P], F16)
        act_g = sb("x_act", [P, 2, TD])
        arena = sb("x_arena", [P, 8, NG * NK])
        keys_t = arena[:, 0, :].rearrange("p (g k) -> p g k", g=NG)
        q = [arena[:, 1 + i, :].rearrange("p (g k) -> p g k", g=NG) for i in range(2)]
        sc = [arena[:, 3 + i, :].rearrange("p (g k) -> p g k", g=NG) for i in range(2)]
        rest = arena[:, 5, :].rearrange("p (g k) -> p g k", g=NG)
        cand, cand_rest = (arena[:, 6 + i, :].rearrange("p (h a b) -> p h a b", h=PH, a=TOPK) for i in range(2))
        keys = sc[0]
        gates = [arena[:, 4 * i:4 * i + 4, :].rearrange("p a b -> p (a b)").rearrange("p (k t) -> p k t", k=NK)
                 for i in range(2)]
        val = sb("pk_val", [P, PH, 2, TOPK])
        idx, idx_f = sb("pk_idx", [P, PH, 2, TOPK], U32), sb("pk_idx_f", [P, PH, 2, TOPK])
        best, best_i = sb("pk_best", [P, PH, TOPK]), sb("pk_best_i", [P, PH, TOPK], U32)
        part_i, part = sb("pk_part_i", [P, 2, PH, TOPK], U32), sb("pk_part", [P, 2, PH, TOPK])
        found, expo, norm = sb("pk_found", [P, 3, SLOTS]), sb("pk_exp", [P, PH, TOPK]), sb("pk_norm", [P, 2, PH])
        slot = sb("slot_t", [P, 3, T])
        second, first = sb("pg_second", [P, 2 * SUB, NK]), sb("pg_first", [P, 2 * SUB, NK])
        g_gate, dots = sb("g_gate", [P, GQ]), sb("g_dots", [P, GQ])
        row_idx = sb("g_idx", [P, 2, GBATCH], U32)
        dots_now = sb("g_now", [P, 8 * REST_DOTS])
        g_row, junk = sb("g_row", [P, GRING, D]), sb("g_junk", [P, 2, D])

        u_turned = ps("xu_t", [P, KD, P])
        score = [ps(f"x_s{i}", [P, TD // 2]) for i in range(2)]
        sub = ps("x_sub", [P, NG // 2, NK])
        turned = ps("x_turned", [P, 4 * P])
        hot_ps = ps("x_gate", [P, SUB * NK])
        gate_ps = [hot_ps, turned]

        u_in = [sem(f"xu_in{i}") for i in range(2)]
        act_st = [sem(f"x_ast{i}") for i in range(2)]
        u_turn, uhi_made, ulo_made, scored, gelued = (sem(f"x_{n}") for n in ("ut", "uhi", "ulo", "sc", "ge"))
        load, keys_turned, keys_kept = sem("pk_ld"), sem("pk_kt"), sem("pk_kk")
        q_in = [sem(f"pk_q{i}") for i in range(2)]
        sub_made, sub_kept, chain, shifted, expd, slot_made, slot_turned, slot_kept, waited = (
            sem(f"pk_{n}") for n in ("sub", "sck", "step", "shift", "expd", "sm", "st", "sk", "waited"))
        parted, matched, pooled = sem("pk_parted"), sem("pk_matched"), sem("pk_pooled")
        hot, made, taken = sem("pg_hot"), sem("pg_made"), sem("pg_taken")
        gate_st = [sem(f"pg_st{i}") for i in range(2)]
        expert_made, idx_copied, dotted, dots_kept, dots_gelu, coefs, freed = (
            sem(f"g_{n}") for n in ("expert", "idx", "dotted", "kept", "gelu", "coef", "freed"))
        g_in = [sem(f"g_in{i}") for i in range(GRING)]
        block = ctx.enter_context(nc.Block())
        CHAIN = 17

        def pick_blocks(it, s):
            for b in range(PICK_B):
                j = s * PICK_B + b
                yield b, it * (2 * PICK_B) + j, it * PICK_B + j // 2, j % 2

        @block.sync
        def _(sp):
            def load_u(n, half, s):
                if not isinstance(n, int) or n >= 2:
                    sp.wait_ge(u_turn, n - 1)
                sp.dma_start(u_raw[:, s, :], dram["w_u"][0, bass.ds(n * P, P), :]).then_inc(u_in[s], 16)

            def store_act(n, s):
                sp.wait_ge(gelued, 2 * n + 2)
                sp.dma_start(scratch["acts"][bass.ds(n, 1)].rearrange("a p t -> (a p) t"), act_g[:, s, :]) \
                    .then_inc(act_st[s], 16)

            sp.dma_start(keys, dram["sub_keys"][0].rearrange("h c k d -> k (h c) d")).then_inc(load, 16)
            load_u(0, 0, 0)
            load_u(1, 0, 1)
            for s in range(2):
                sp.dma_start(q[s], scratch["pq"][:, :, s * P:(s + 1) * P]).then_inc(q_in[s], 16)

            def pick_turn(it):
                for s in range(2):
                    for b, n, half, k in pick_blocks(it, s):
                        load_u(n + 2, half + 1, k)
                        store_act(n, k)
                    if not (isinstance(it, int) and it == TT // 2 - 1):
                        sp.wait_ge(sub_made, 4 * it + 2 * s + 2)
                        sp.dma_start(q[s], scratch["pq"][:, :, bass.ds((it * 2 + s + 2) * P, P)]).then_inc(q_in[s], 16)

            pick_turn(0)
            with sp.Fori(1, TT // 2 - 1) as it:
                pick_turn(it)
            pick_turn(TT // 2 - 1)

            def gate_turn(it):
                for j in range(8):
                    n = it * 8 + (N0_GATE + j)
                    load_u(n + 2, 0, j % 2)
                    store_act(n, j % 2)
                    if j % PIECE_STEPS == PIECE_STEPS - 1:
                        p = j // PIECE_STEPS
                        sp.wait_ge(taken, it * (8 * SUBS) + (p + 1) * PIECE_STEPS * SUBS)
                        sp.dma_start(scratch["gates"][:, bass.ds(it * 2 + p, 1), :].rearrange("p a n -> p (a n)"),
                                     gates[p].rearrange("p k t -> p (k t)")).then_inc(gate_st[p], 16)

            with sp.Fori(0, GATE_STEPS // 8) as it:
                gate_turn(it)

            def rest_turn(it, last):
                for j in range(8):
                    n = it * 8 + (N0_REST + j)
                    if not (last and j >= 6):
                        load_u(n + 2, 0, j % 2)
                    store_act(n, j % 2)

            with sp.Fori(0, REST_STEPS // 8 - 1) as it:
                rest_turn(it, False)
            rest_turn(REST_STEPS // 8 - 1, True)
            for s in range(2):
                sp.wait_ge(act_st[s], 16 * NBLK // 2)
                sp.wait_ge(gate_st[s], 16 * N_PIECE // 2)

        @block.tensor
        def _(pe):
            def turn_u(n, half, s):
                pe.wait_ge(u_in[s], 16 * half + 16)
                if not isinstance(n, int) or n >= 1:
                    pe.wait_ge(ulo_made, n)
                for c in range(KD):
                    tr = nc.tensor.transpose(u_turned[:, c, :], u_raw[:, s, c * P:(c + 1) * P], ident[:, :])
                tr.then_inc(u_turn, 1)

            def scores(n, s):
                pe.wait_ge(ulo_made, n + 1)
                if not isinstance(n, int) or n >= 1:
                    pe.wait_ge(gelued, 2 * n)
                for half in range(2):
                    cols = slice(GT * P + half * (TD // 2), GT * P + (half + 1) * (TD // 2))
                    for c in range(KD):
                        nc.tensor.matmul(score[half][:, :], u_hi[:, s, c, :], h_hi[:, c, cols], start=(c == 0), stop=False)
                        nc.tensor.matmul(score[half][:, :], u_hi[:, s, c, :], h_lo[:, c, cols], start=False, stop=False)
                        mm = nc.tensor.matmul(score[half][:, :], u_lo[:, s, c, :], h_hi[:, c, cols],
                                              start=False, stop=(c == KD - 1))
                    mm.then_inc(scored, 1)

            def sub_scores(r, s, part_):
                behind(pe, sub_kept, 2 * r + part_)
                for g in range(NG // 2):
                    gg = part_ * (NG // 2) + g
                    mm = nc.tensor.matmul(sub[:, g, :], q[s][:, gg, :], keys_t[:, gg, :], start=True, stop=True)
                mm.then_inc(sub_made, 1)

            def turn_slots(r):
                pe.wait_ge(slot_made, r + 1)
                behind(pe, slot_kept, r)
                for n in range(3):
                    tr = nc.tensor.transpose(turned[:, n * P:(n + 1) * P], found[:, n, :], ident[:, :])
                tr.then_inc(slot_turned, 1)

            pe.wait_ge(load, 16)
            for part_ in range(2):
                if part_:
                    pe.wait_ge(keys_kept, 1)
                for g in range(NG // 2):
                    tr = nc.tensor.transpose(sub[:, g, :], keys[:, part_ * (NG // 2) + g, :], ident[:, :])
                tr.then_inc(keys_turned, 1)
            pe.wait_ge(keys_kept, 2)
            pe.wait_ge(q_in[0], 16)
            for part_ in range(2):
                sub_scores(0, 0, part_)
            turn_u(0, 0, 0)

            def pick_turn(it, last=False):
                for s in range(2):
                    r = it * 2 + s
                    for b, n, half, k in pick_blocks(it, s):
                        if b in (0, 2) and not (last and s == 1):
                            if b == 0:
                                pe.wait_ge(q_in[1 - s], 16 * it + (16 if s == 0 else 32))
                            sub_scores(r + 1, 1 - s, b // 2)
                        turn_u(n + 1, half + k, 1 - k)
                        scores(n, k)
                        if b == 2 and not (s == 0 and isinstance(it, int) and it == 0):
                            turn_slots(r - 1)

            pick_turn(0)
            with pe.Fori(1, TT // 2 - 1) as it:
                pick_turn(it)
            pick_turn(TT // 2 - 1, True)
            turn_slots(TT - 1)

            pe.wait_ge(slot_kept, TT)

            def gate_turn(it):
                for j in range(8):
                    n = it * 8 + (N0_GATE + j)
                    half = it * 4 + (N0_GATE + j) // 2
                    turn_u(n + 1, half + j % 2, 1 - j % 2)
                    scores(n, j % 2)
                    for i in range(SUBS):
                        m = it * (8 * SUBS) + j * SUBS + i
                        pe.wait_ge(hot, m + 1)
                        behind(pe, taken, m - 1)
                        for t in range(SUB):
                            mm = nc.tensor.matmul(gate_ps[i % 2][:, t * NK:(t + 1) * NK], second[:, (i % 2) * SUB + t, :],
                                                  first[:, (i % 2) * SUB + t, :], start=True, stop=True)
                        mm.then_inc(made, 1)

            turns(pe, GATE_STEPS // 8, gate_turn)

            def rest_turn(it, last):
                for j in range(8):
                    n = it * 8 + (N0_REST + j)
                    if not (last and j == 7):
                        turn_u(n + 1, it * 4 + (N0_REST + j) // 2 + j % 2, 1 - j % 2)
                    scores(n, j % 2)

            with pe.Fori(0, REST_STEPS // 8 - 1) as it:
                rest_turn(it, False)
            rest_turn(REST_STEPS // 8 - 1, True)

        @block.scalar
        def _(act):
            def split_u(n, s):
                act.wait_ge(u_turn, n + 1)
                if not isinstance(n, int) or n >= 2:
                    act.wait_ge(scored, 2 * n - 2)
                nc.scalar.activation(u_hi[:, s], u_turned[:, :, :], ACT.Copy, scale=S_U).then_inc(uhi_made, 1)

            def gelu(n, half, s):
                behind(act, act_st[s], half * 16)
                for hf in range(2):
                    act.wait_ge(scored, 2 * n + (hf + 1))
                    nc.scalar.activation(act_g[:, s, hf * (TD // 2):(hf + 1) * (TD // 2)], score[hf][:, :],
                                         ACT.Gelu_apprx_tanh, scale=1.0 / (S_H * S_U)).then_inc(gelued, 1)

            def keep_sub(r, s, part_):
                act.wait_ge(sub_made, 2 * r + part_ + 1)
                behind(act, slot_made, r - 1)
                nc.scalar.copy(sc[s][:, part_ * (NG // 2):(part_ + 1) * (NG // 2), :], sub[:, :, :]) \
                    .then_inc(sub_kept, 1)

            for part_ in range(2):
                act.wait_ge(keys_turned, part_ + 1)
                nc.scalar.copy(keys_t[:, part_ * (NG // 2):(part_ + 1) * (NG // 2), :], sub[:, :, :]).then_inc(keys_kept, 1)
            for part_ in range(2):
                keep_sub(0, 0, part_)
            split_u(0, 0)

            def pick_turn(it, last=False):
                for s in range(2):
                    r = it * 2 + s
                    for b, n, half, k in pick_blocks(it, s):
                        split_u(n + 1, 1 - k)
                        if b in (0, 2) and not (last and s == 1):
                            keep_sub(r + 1, 1 - s, b // 2)
                        if b == 4:
                            act.wait_ge(shifted, r + 1)
                            nc.scalar.activation(expo[:, :, :], expo[:, :, :], ACT.Exp).then_inc(expd, 1)
                        gelu(n, half, k)

            pick_turn(0)
            with act.Fori(1, TT // 2 - 1) as it:
                pick_turn(it)
            pick_turn(TT // 2 - 1, True)

            act.wait_ge(slot_kept, TT)

            def gate_turn(it):
                for j in range(8):
                    n = it * 8 + (N0_GATE + j)
                    split_u(n + 1, 1 - j % 2)
                    gelu(n, it * 4 + (N0_GATE + j) // 2, j % 2)
                    p = j // PIECE_STEPS
                    if j % PIECE_STEPS == 0:
                        behind(act, gate_st[p], it * 16)
                    for i in range(SUBS):
                        act.wait_ge(made, it * (8 * SUBS) + (j * SUBS + i + 1))
                        t = (j % PIECE_STEPS) * GATE_TOK + i * SUB
                        nc.scalar.copy(gates[p][:, :, t:t + SUB].rearrange("p a t -> p t a"),
                                       gate_ps[i % 2][:, :].rearrange("p (t a) -> p t a", t=SUB)).then_inc(taken, 1)

            turns(act, GATE_STEPS // 8, gate_turn)

            def rest_turn(it, last):
                for j in range(8):
                    n = it * 8 + (N0_REST + j)
                    if not (last and j == 7):
                        split_u(n + 1, 1 - j % 2)
                    gelu(n, it * 4 + (N0_REST + j) // 2, j % 2)

            with act.Fori(0, REST_STEPS // 8 - 1) as it:
                rest_turn(it, False)
            rest_turn(REST_STEPS // 8 - 1, True)
            act.wait_ge(dots_kept, NBLK // 8 - TT * PICK_B // 8)
            nc.scalar.activation(dots[:, :], dots[:, :], ACT.Gelu_apprx_tanh).then_inc(dots_gelu, 1)

        @block.gpsimd
        def _(pool):
            for r in range(TT):
                pool.wait_ge(matched, r + 1)
                nc.gpsimd.tensor_tensor(cand_rest[:, :, :, :], cand_rest[:, :, :, :],
                                        idx_f[:, :, 1, None, :].broadcast_to([P, PH, TOPK, TOPK]), ALU.mult) \
                    .then_inc(pooled, 1)
            pool.wait_ge(expert_made, 2)

            def gather_turn(it):
                nc.gpsimd.tensor_copy(row_idx[:, 0, :], expert[:, bass.ds(it * GBATCH, GBATCH)]).then_inc(idx_copied, 1)
                pool.wait_ge(idx_copied, it + 1)
                for j in range(GBATCH):
                    behind(pool, dotted, it * GBATCH + j - GRING + 1)
                    pool.sem_inc(freed, 1)
                    nc.gpsimd.indirect_dma_start(g_row[:, j % GRING, :], None, dram["w_u"][0],
                                                 bass.IndirectOffsetOnAxis(row_idx[:, 0, j:j + 1], 0)) \
                        .then_inc(g_in[j % GRING], 16)
                pool.wait_ge(g_in[GRING - 1], it * (16 * GBATCH // GRING) + 16 * GBATCH // GRING)

            turns(pool, GQ // GBATCH, gather_turn)

        @block.vector
        def _(dve):
            def split_u(n, s):
                dve.wait_ge(uhi_made, n + 1)
                nc.vector.scalar_tensor_tensor(u_lo[:, s], u_turned[:, :, :], S_U, u_hi[:, s],
                                               ALU.mult, ALU.subtract).then_inc(ulo_made, 1)

            def dot(q_, landed, j, tile, turn_):
                if j == 0:
                    behind(dve, dots_kept, turn_)
                dve.wait_ge(g_in[j % GRING], landed)
                behind(dve, dotted, q_ - 1)
                nc.vector.tensor_tensor_reduce(junk[:, j % 2, :], g_row[:, j % GRING, :], h_rows[:, tile, :], 1.0, 0.0,
                                               ALU.mult, ALU.add, dots_now[:, j:j + 1]).then_inc(dotted, 1)

            def keep_dots(q0, count):
                dve.wait_ge(dotted, q0 + count)
                nc.vector.tensor_copy(dots[:, bass.ds(q0, count)], dots_now[:, 0:count]).then_inc(dots_kept, 1)

            split_u(0, 0)

            def pick(it, last=False):
                for s in range(2):
                    r = it * 2 + s
                    ch = Chain(dve, chain, r * CHAIN, waited)
                    blocks = {b: (n + 1, 1 - k) for b, n, half, k in pick_blocks(it, s)}
                    v = val[:, :, :, :].rearrange("p h c k -> p (h c) k")
                    ix = idx[:, :, :, :].rearrange("p h c k -> p (h c) k")
                    dve.wait_ge(sub_kept, 2 * r + 2)
                    dve.sem_inc(waited, 1)
                    for g in range(NG):
                        op = nc.vector.max(v[:, g, 0:8], sc[s][:, g, :])
                    ch.wait_alone(op)
                    split_u(*blocks[0])
                    for g in range(NG):
                        nc.vector.max_index(ix[:, g, 0:8], v[:, g, 0:8], sc[s][:, g, :])
                        op = nc.vector.match_replace(rest[:, g, :], v[:, g, 0:8], sc[s][:, g, :], TAKEN)
                    ch.wait_alone(op)
                    for g in range(NG):
                        op = nc.vector.max(v[:, g, 8:16], rest[:, g, :])
                    ch.wait_alone(op)
                    split_u(*blocks[1])
                    for g in range(NG):
                        op = nc.vector.max_index(ix[:, g, 8:16], v[:, g, 8:16], rest[:, g, :])
                    ch.wait_alone(op)
                    nc.vector.tensor_copy(idx_f[:, :, :, :], idx[:, :, :, :])
                    ch.wait_alone(nc.vector.tensor_tensor(cand[:, :, :, :],
                                                          val[:, :, 0, :, None].broadcast_to([P, PH, TOPK, TOPK]),
                                                          val[:, :, 1, None, :].broadcast_to([P, PH, TOPK, TOPK]),
                                                          ALU.add))
                    c = cand[:, :, :, :].rearrange("p h a b -> p h (a b)")
                    cr = cand_rest[:, :, :, :].rearrange("p h a b -> p h (a b)")
                    for h in range(PH):
                        op = nc.vector.max(best[:, h, 0:8], c[:, h, :])
                    ch.wait_alone(op)
                    split_u(*blocks[2])
                    for h in range(PH):
                        nc.vector.max_index(best_i[:, h, 0:8], best[:, h, 0:8], c[:, h, :])
                        op = nc.vector.match_replace(cr[:, h, :], best[:, h, 0:8], c[:, h, :], TAKEN)
                    ch.wait_alone(op)
                    for h in range(PH):
                        op = nc.vector.max(best[:, h, 8:16], cr[:, h, :])
                    ch.wait_alone(op)
                    for h in range(PH):
                        nc.vector.max_index(best_i[:, h, 8:16], best[:, h, 8:16], cr[:, h, :])
                    nc.vector.tensor_tensor(expo[:, :, :], best[:, :, :],
                                            best[:, :, 0:1].broadcast_to([P, PH, TOPK]), ALU.subtract) \
                        .then_inc(shifted, 1)
                    split_u(*blocks[3])
                    dve.wait_ge(shifted, r + 1)
                    nc.vector.tensor_scalar(part_i[:, 0], best_i[:, :, :], 4, None, ALU.logical_shift_right)
                    ch.wait(nc.vector.tensor_scalar(part_i[:, 1], best_i[:, :, :], TOPK - 1, None, ALU.bitwise_and))
                    nc.vector.tensor_copy(part[:, :, :, :], part_i[:, :, :, :]).then_inc(parted, 1)
                    dve.wait_ge(parted, r + 1)
                    nc.vector.tensor_tensor(
                        cand_rest[:, :, :, :].rearrange("p h a b -> p (h a) b"),
                        part[:, 1].rearrange("p h k -> p (h k)")[:, :, None].broadcast_to([P, SLOTS, TOPK]),
                        iota[:, None, 0:TOPK].broadcast_to([P, SLOTS, TOPK]), ALU.is_equal).then_inc(matched, 1)
                    ch.wait(nc.vector.tensor_tensor(
                        cand[:, :, :, :].rearrange("p h a b -> p (h a) b"),
                        part[:, 0].rearrange("p h k -> p (h k)")[:, :, None].broadcast_to([P, SLOTS, TOPK]),
                        iota[:, None, 0:TOPK].broadcast_to([P, SLOTS, TOPK]), ALU.is_equal))
                    ch.wait(nc.vector.tensor_tensor(cand[:, :, :, :], cand[:, :, :, :],
                                                    idx_f[:, :, 0, None, :].broadcast_to([P, PH, TOPK, TOPK]), ALU.mult))
                    behind(dve, slot_turned, r)
                    nc.vector.tensor_reduce(found[:, 0, :], cand[:, :, :, :].rearrange("p h a b -> p (h a) b"),
                                            AX_X, ALU.add)
                    dve.wait_ge(expd, r + 1)
                    ch.wait(nc.vector.tensor_reduce(norm[:, 0, :], expo[:, :, :], AX_X, ALU.add))
                    ch.wait(nc.vector.reciprocal(norm[:, 1, :], norm[:, 0, :]))
                    gate_now = nc.vector.tensor_tensor(found[:, 2, :].rearrange("p (h k) -> p h k", h=PH), expo[:, :, :],
                                                       norm[:, 1, :, None].broadcast_to([P, PH, TOPK]), ALU.mult)
                    split_u(*blocks[4])
                    dve.wait_ge(pooled, r + 1)
                    op = nc.vector.tensor_reduce(found[:, 1, :], cand_rest[:, :, :, :].rearrange("p h a b -> p (h a) b"),
                                                 AX_X, ALU.add)
                    op.then_inc(slot_made, 1)
                    dve.wait_ge(slot_made, r + 1)
                    if isinstance(it, int) and it == 0:
                        cols = slice(s * SLOTS, (s + 1) * SLOTS)
                        nc.vector.tensor_copy(g_gate[:, cols], found[:, 2, :])
                        nc.vector.scalar_tensor_tensor(expert[:, cols], found[:, 0, :], float(NK), found[:, 1, :],
                                                       ALU.mult, ALU.add).then_inc(expert_made, 1)
                        dve.wait_ge(expert_made, s + 1)
                    if not (s == 0 and isinstance(it, int) and it == 0):
                        keep_slots(r - 1)
                    assert ch.n <= CHAIN
                    dve.sem_inc(chain, CHAIN - ch.n)

            def keep_slots(r):
                dve.wait_ge(slot_turned, r + 1)
                nc.vector.tensor_copy(slot[:, :, bass.ds(r * P, P)],
                                      turned[:, 0:3 * P].rearrange("p (n t) -> p n t", n=3)).then_inc(slot_kept, 1)

            pick(0)
            with dve.Fori(1, TT // 2 - 1) as it:
                pick(it)
            pick(TT // 2 - 1, True)
            keep_slots(TT - 1)
            dve.wait_ge(slot_kept, TT)

            def gate_turn(it):
                for j in range(8):
                    n = it * 8 + (N0_GATE + j)
                    split_u(n + 1, 1 - j % 2)
                    for i in range(SUBS):
                        m = it * (8 * SUBS) + (j * SUBS + i)
                        behind(dve, made, m - 1)
                        for t in range(SUB):
                            tok = bass.ds(it * (8 * GATE_TOK) + (GT * P + j * GATE_TOK + i * SUB + t), 1)
                            at = (i % 2) * SUB + t
                            nc.vector.tensor_scalar(second[:, at, :], iota[:, :], slot[:, 1, tok], None, ALU.is_equal)
                            op = nc.vector.tensor_scalar(first[:, at, :], iota[:, :], slot[:, 0, tok], slot[:, 2, tok],
                                                         ALU.is_equal, ALU.mult)
                        op.then_inc(hot, 1)
                        if i % 2 == 1:
                            e = j * GATE_DOTS + i // 2
                            dot(it * (8 * GATE_DOTS) + e, it * (16 * 8 * GATE_DOTS // GRING) + 16 * (e // GRING + 1), e, 0, it)
                keep_dots(it * (8 * GATE_DOTS), 8 * GATE_DOTS)

            turns(dve, GATE_STEPS // 8, gate_turn)
            Q0 = GATE_STEPS * GATE_DOTS

            def rest_turn(it, tile, last):
                for j in range(8):
                    n = it * 8 + (N0_REST + j)
                    if not (last and j == 7):
                        split_u(n + 1, 1 - j % 2)
                    for i in range(REST_DOTS):
                        e = j * REST_DOTS + i
                        dot(it * (8 * REST_DOTS) + (Q0 + e),
                            it * (16 * 8 * REST_DOTS // GRING) + 16 * ((Q0 + e) // GRING + 1), e, tile,
                            it + GATE_STEPS // 8)
                keep_dots(it * (8 * REST_DOTS) + Q0, 8 * REST_DOTS)

            rest_turn(0, 0, False)
            assert Q0 + 8 * REST_DOTS == SLOTS
            with dve.Fori(1, REST_STEPS // 8 - 1) as it:
                rest_turn(it, 1, False)
            rest_turn(REST_STEPS // 8 - 1, 1, True)
            dve.wait_ge(dots_gelu, 1)
            nc.vector.scalar_tensor_tensor(coef[:, :], dots[:, :], S_A * S_V, g_gate[:, :], ALU.mult, ALU.mult) \
                .then_inc(coefs, 1)
            dve.wait_ge(coefs, 1)


def peer_outputs(nc, dram, scratch, coef, expert, y):
    NB = 4
    TURN = 2 * NB
    N_TURN = NBLK // TURN
    BANKS = 2 * (TT - GT)
    DOTS = GQ // NBLK
    assert TURN * DOTS == GBATCH
    with ExitStack() as ctx:
        sb, ps, sem = ctx_tools(nc, ctx)
        v_raw = sb("xv_raw", [P, 2, D])
        v_hi, v_lo = sb("xv_hi", [P, 2, NB, D], F16), sb("xv_lo", [P, 2, NB, D], F16)
        gate = sb("xv_gate", [P, 2, N_PIECE, 2, PIECE])
        act_g = sb("xv_act", [P, 4, TD])
        a_hi, a_lo = sb("xa_hi", [P, 2, NB, TD], F16), sb("xa_lo", [P, 2, NB, TD], F16)
        row_idx = sb("gv_idx", [P, GBATCH], U32)
        g_row = sb("gv_row", [P, GRING, D])
        out = [ps(f"xo{i}", [P, BANK]) for i in range(8)]
        v_in, gate_in = [sem(f"xv_in{i}") for i in range(2)], [sem(f"xg_in{i}") for i in range(2)]
        act_in = [sem(f"xa_in{i}") for i in range(4)]
        gated, ahi_made, alo_made, vhi_made, vlo_made, mixed, added = (
            sem(f"xo_{n}") for n in ("gated", "ahi", "alo", "vhi", "vlo", "mixed", "added"))
        idx_copied, g_added, freed = sem("gv_idxc"), sem("gv_added"), sem("gv_freed")
        g_in = [sem(f"gv_in{i}") for i in range(GRING)]
        block = ctx.enter_context(nc.Block())

        @block.sync
        def _(sp):
            def turn(it):
                for k in range(TURN):
                    n, s = it * TURN + k, k % 2
                    behind(sp, vlo_made, n - 1)
                    sp.dma_start(v_raw[:, s, :], dram["w_v"][0, bass.ds(n * P, P), :]).then_inc(v_in[s], 16)
                    if s == 0:
                        behind(sp, gated, n - 2)
                        sp.dma_start(gate[:, (k // 2) % 2].rearrange("p a b t -> p a (b t)"),
                                     scratch["gates"][:, :, bass.ds((it * NB + k // 2) * 2 * PIECE, 2 * PIECE)]) \
                            .then_inc(gate_in[(k // 2) % 2], 16)
                    behind(sp, alo_made, n - 3)
                    sp.dma_start(act_g[:, k % 4, :], scratch["acts"][bass.ds(n, 1)].rearrange("a p t -> (a p) t")) \
                        .then_inc(act_in[k % 4], 16)

            turns(sp, N_TURN, turn)

        @block.gpsimd
        def _(pool):
            def turn(it):
                nc.gpsimd.tensor_copy(row_idx[:, :], expert[:, bass.ds(it * GBATCH, GBATCH)]).then_inc(idx_copied, 1)
                for k in range(TURN):
                    n = it * TURN + k
                    pool.wait_ge(act_in[k % 4], it * (16 * TURN // 4) + 16 * (k // 4 + 1))
                    pool.wait_ge(gate_in[(k // 2) % 2], it * (16 * TURN // 4) + 16 * (k // 4 + 1))
                    g = gate[:, (k // 2) % 2, :, k % 2, :]
                    a = act_g[:, k % 4, :].rearrange("p (a t) -> p a t", t=PIECE)
                    nc.gpsimd.tensor_tensor(a, a, g, ALU.mult).then_inc(gated, 1)
                    if k == 0:
                        pool.wait_ge(idx_copied, it + 1)
                    for i in range(DOTS):
                        j = k * DOTS + i
                        behind(pool, g_added, it * GBATCH + j - GRING + 1)
                        pool.sem_inc(freed, 1)
                        nc.gpsimd.indirect_dma_start(g_row[:, j % GRING, :], None, dram["w_v"][0],
                                                     bass.IndirectOffsetOnAxis(row_idx[:, j:j + 1], 0)) \
                            .then_inc(g_in[j % GRING], 16)
                pool.wait_ge(g_in[GRING - 1], it * (16 * GBATCH // GRING) + 16 * GBATCH // GRING)

            turns(pool, N_TURN, turn)

        @block.scalar
        def _(act):
            def turn(it):
                for k in range(TURN):
                    n, s, b, par = it * TURN + k, k % 2, k % NB, k // NB
                    if b == 0:
                        behind(act, mixed, it * (2 * BANKS) + (par - 1) * BANKS)
                    act.wait_ge(v_in[s], it * (16 * NB) + 16 * (k // 2 + 1))
                    nc.scalar.activation(v_hi[:, par, b, :], v_raw[:, s, :], ACT.Copy, scale=S_V).then_inc(vhi_made, 1)
                    act.wait_ge(gated, n + 1)
                    nc.scalar.activation(a_hi[:, par, b, :], act_g[:, k % 4, :], ACT.Copy, scale=S_A).then_inc(ahi_made, 1)

            turns(act, N_TURN, turn)

        @block.tensor
        def _(pe):
            def turn(it):
                for par in range(2):
                    g = it * 2 + par
                    pe.wait_ge(alo_made, g * NB + NB)
                    pe.wait_ge(vlo_made, g * NB + NB)
                    for t in range(TT - GT):
                        tile = par * (TT - GT) + t
                        m = g * BANKS + 2 * t
                        behind(pe, added, m - 6)
                        rows = slice(t * P, (t + 1) * P)
                        for b in range(NB):
                            for a, v, first, last in ((a_hi, v_hi, b == 0, False), (a_hi, v_lo, False, False),
                                                      (a_lo, v_hi, False, b == NB - 1)):
                                for half in range(2):
                                    mm = nc.tensor.matmul(out[2 * (tile % 4) + half][:, :], a[:, par, b, rows],
                                                          v[:, par, b, half * BANK:(half + 1) * BANK],
                                                          start=first, stop=last)
                                    if last:
                                        mm.then_inc(mixed, 1)

            turns(pe, N_TURN, turn)

        @block.vector
        def _(dve):
            def add(g, par, j):
                t, half = j // 2, j % 2
                cols = slice(half * BANK, (half + 1) * BANK)
                dve.wait_ge(mixed, g * BANKS + (j + 1))
                behind(dve, added, g * BANKS + (j + 1 - BANKS))
                nc.vector.tensor_tensor(y[:, GT + t, cols], out[2 * ((par * (TT - GT) + t) % 4) + half][:, :],
                                        y[:, GT + t, cols], ALU.add).then_inc(added, 1)

            def turn(it, tile=0):
                for k in range(TURN):
                    n, s, b, par = it * TURN + k, k % 2, k % NB, k // NB
                    dve.wait_ge(vhi_made, n + 1)
                    nc.vector.scalar_tensor_tensor(v_lo[:, par, b, :], v_raw[:, s, :], S_V, v_hi[:, par, b, :],
                                                   ALU.mult, ALU.subtract).then_inc(vlo_made, 1)
                    dve.wait_ge(ahi_made, n + 1)
                    nc.vector.scalar_tensor_tensor(a_lo[:, par, b, :], act_g[:, k % 4, :], S_A, a_hi[:, par, b, :],
                                                   ALU.mult, ALU.subtract).then_inc(alo_made, 1)
                    for i in range(DOTS):
                        j = k * DOTS + i
                        q_ = it * GBATCH + j
                        dve.wait_ge(g_in[j % GRING], it * (16 * GBATCH // GRING) + 16 * (j // GRING + 1))
                        behind(dve, g_added, q_)
                        nc.vector.scalar_tensor_tensor(y[:, tile, :], g_row[:, j % GRING, :], coef[:, bass.ds(q_, 1)],
                                                       y[:, tile, :], ALU.mult, ALU.add).then_inc(g_added, 1)
                    if not (par == 0 and isinstance(it, int) and it == 0):
                        for j in range(b * BANKS // NB, (b + 1) * BANKS // NB):
                            add(it * 2 + (par - 1), 1 - par, j)

            zeroed = sem("y_zeroed")
            nc.vector.memset(y[:, :, :], 0.0).then_inc(zeroed, 1)
            dve.wait_ge(zeroed, 1)
            turn(0)
            with dve.Fori(1, N_TURN // GT) as it:
                turn(it, 0)
            for tile in range(1, GT):
                with dve.Fori(tile * N_TURN // GT, (tile + 1) * N_TURN // GT) as it:
                    turn(it, tile)
            for j in range(BANKS):
                add(2 * N_TURN - 1, 1, j)


def reload(nc, tag, dst, src):
    with ExitStack() as ctx:
        load = ctx_tools(nc, ctx)[2](f"{tag}_in")
        block = ctx.enter_context(nc.Block())

        @block.sync
        def _(sp):
            sp.dma_start(dst[:, :, :], src.rearrange("(b p) d -> p b d", p=P)).then_inc(load, 16)
            sp.wait_ge(load, 16)


def build(nc, dram, out):
    scratch = {
        "qk_fox": nc.dram_tensor("qk_fox", [2 * FOX_H, AUG, T], F32, kind="Internal").ap(),
        "qk_swa": nc.dram_tensor("qk_swa", [SWA_H + SWA_KV, HD, T], F32, kind="Internal").ap(),
        "v": nc.dram_tensor("v_all", [T, V_W], F32, kind="Internal").ap(),
        "mix": nc.dram_tensor("mix", [T, D], F32, kind="Internal").ap(),
        "x_mid": nc.dram_tensor("x_mid", [T, D], F32, kind="Internal").ap(),
        "pq": nc.dram_tensor("pq", [P, NG, T], F32, kind="Internal").ap(),
        "acts": nc.dram_tensor("acts", [NBLK, P, TD], F32, kind="Internal").ap(),
        "gates": nc.dram_tensor("gates", [NK, N_PIECE, NK * PIECE], F32, kind="Internal").ap(),
    }
    x_rows = dram["x"][0]
    with ExitStack() as ctx:
        sb, ps, sem = ctx_tools(nc, ctx)
        ident, iota = sb("ident", [P, P]), sb("iota", [P, P])
        gate2 = sb("gate2", [P, D])
        h_hi, h_lo = sb("h_hi", [P, KD, T], F16), sb("h_lo", [P, KD, T], F16)
        h_rows = sb("h_rows", [P, GT, D])
        coef, expert = sb("g_coef", [P, GQ]), sb("g_expert", [P, GQ], U32)
        kept = {"ident": ident, "iota": iota}
        with ExitStack() as front:
            fsb, _, _ = ctx_tools(nc, front)
            causal, mod, x = fsb("causal", [P, P]), fsb("mod", [P, N_MOD * D]), fsb("x_sb", [P, TT, D])
            kept |= {"causal": causal, "mod": mod, "x": x}
            with ExitStack() as c2:
                load = ctx_tools(nc, c2)[2]("const_in")
                block = c2.enter_context(nc.Block())

                @block.sync
                def _(sp):
                    sp.dma_start(ident[:, :], dram["ident"]).then_inc(load, 16)
                    sp.dma_start(iota[:, :], dram["iota"]).then_inc(load, 16)
                    sp.dma_start(causal[:, :], dram["causal"]).then_inc(load, 16)
                    sp.dma_start(x[:, :, :], x_rows.rearrange("(b p) d -> p b d", p=P)).then_inc(load, 16)
                    sp.wait_ge(load, 64)
            modulation(nc, dram, kept)
            row = [mod[:, i * D:(i + 1) * D] for i in range(N_MOD)]
            with ExitStack() as c3:
                h_t = c3.enter_context(nc.sbuf_tensor("h1_t", [P, KD, T], F32))
                norm_and_turn(nc, kept, "n1", row[1], row[0], (h_t, None, None, None))
                project_in(nc, dram, scratch, kept, h_t)
            fox_attention(nc, scratch, kept)
            swa_attention(nc, dram, scratch, kept)
            with ExitStack() as c3:
                y = c3.enter_context(nc.sbuf_tensor("y_mix", [P, TT, D], F32))
                project_out(nc, dram, scratch, kept, y)
                add_normed(nc, "am", x, y, row[2], EPS, scratch["x_mid"])
            norm_and_turn(nc, kept, "n2", row[4], row[3], (None, h_hi, h_lo, h_rows))
            peer_queries(nc, dram, scratch, h_hi, h_lo)
            with ExitStack() as c3:
                copied = ctx_tools(nc, c3)[2]("gate2_copied")
                block = c3.enter_context(nc.Block())

                @block.vector
                def _(dve):
                    nc.vector.tensor_copy(gate2[:, :], row[5]).then_inc(copied, 1)
                    dve.wait_ge(copied, 1)
        peer_scores(nc, dram, scratch, kept, h_hi, h_lo, h_rows, coef, expert)
        with ExitStack() as c3:
            y = c3.enter_context(nc.sbuf_tensor("y_ffn", [P, TT, D], F32))
            peer_outputs(nc, dram, scratch, coef, expert, y)
            with ExitStack() as c4:
                x = c4.enter_context(nc.sbuf_tensor("x_again", [P, TT, D], F32))
                reload(nc, "xr", x, scratch["x_mid"])
                add_normed(nc, "af", x, y, gate2[:, :], EPS * (S_A * S_V) ** 2, out[0])


def constants():
    r = np.arange(P)
    dist = r[:, None] + P - np.arange(2 * P)[None, :]
    slopes = 2.0 ** (-8.0 * np.arange(1, SWA_H + 1) / SWA_H)
    bias = np.where(((dist >= 0) & (dist < P))[:, None, :], -slopes[None, :, None] * dist[:, None, :], NEG)
    return {
        "ident": np.eye(P, dtype=np.float32),
        "iota": np.ascontiguousarray(np.broadcast_to(r.astype(np.float32), (P, P))),
        "causal": np.where(r[None, :] <= r[:, None], 0.0, NEG).astype(np.float32),
        "swa_bias": bias.astype(np.float32),
    }


_INS = ["x", "c", "w_ada", "b_ada", "g_pre_mix", "g_post_mix", "g_pre_ffn", "g_post_ffn", "w_in", "b_fgate",
        "swa_sinks", "w_out", "w_query", "sub_keys", "w_u", "w_v"]


def declare(nc, arrays):
    dram = {name: nc.dram_tensor(f"in_{name}", list(a.shape), F32, kind="ExternalInput").ap()
            for name, a in arrays.items()}
    build(nc, dram, nc.dram_tensor("out", [1, T, D], F32, kind="ExternalOutput").ap())


def kernel(**inputs):
    import concourse.bacc as bacc
    from concourse.bass_utils import run_bass_kernel_spmd as run

    arrays = {name: np.ascontiguousarray(inputs[name]) for name in _INS}
    arrays.update(constants())
    nc = bacc.Bacc("TRN2", target_bir_lowering=False, num_devices=1)
    declare(nc, arrays)
    r = run(nc, [{f"in_{name}": a for name, a in arrays.items()}], core_ids=[0])
    return r.results[0]["out"]
```

```python
from contextlib import ExitStack

import numpy as np

import concourse.bass as bass
from concourse import mybir

F32 = mybir.dt.float32
F16 = mybir.dt.float16
U32 = mybir.dt.uint32
ALU = mybir.AluOpType
ACT = mybir.ActivationFunctionType
AX_X = mybir.AxisListType.X

P = 128
BANK = 512
D = 1024
T = 1024
KD = D // P
TT = T // P
N_MOD = 6
HD = 64
FOX_H, SWA_H, SWA_KV = 8, 8, 2
SWA_GROUP = SWA_H // SWA_KV
AUG = HD + 2
COL_FV = 2 * FOX_H * HD
COL_FF = 3 * FOX_H * HD
COL_SQ = COL_FF + FOX_H
COL_SK = COL_SQ + SWA_H * HD
COL_SV = COL_SK + SWA_KV * HD
IN_W = COL_SV + SWA_KV * HD
V_W = (FOX_H + SWA_KV) * HD
PH = 8
NG = 2 * PH
NK = 128
TOPK = 16
SLOTS = PH * TOPK
N_EXP = NK * NK
NBLK = N_EXP // P
GT = 2
TD = T - GT * P
GQ = GT * SLOTS
GRING, GBATCH = 4, 16
PIECE = 64
N_PIECE = TD // PIECE
EPS = 1e-6
NEG = -1e30
TAKEN = -3.0e38
SCALE = HD ** -0.5

S_H = 16.0
S_U = 64.0
S_A = 64.0
S_V = 64.0


def ctx_tools(nc, ctx):
    def sb(name, shape, dt=F32):
        return ctx.enter_context(nc.sbuf_tensor(name, shape, dt))

    def ps(name, shape, dt=F32):
        return ctx.enter_context(nc.psum_tensor(name, shape, dt))

    def sem(name):
        s = ctx.enter_context(nc.semaphore(name))
        ctx.callback(nc.sync.sem_clear, s)
        return s

    return sb, ps, sem


def turns(eng, count, body):
    body(0)
    with eng.Fori(1, count) as i:
        body(i)


def behind(eng, sem, value):
    if not isinstance(value, int) or value > 0:
        eng.wait_ge(sem, value)


class Chain:

    def __init__(self, eng, sem, start=0, waited=None):
        self.eng, self.sem, self.n, self.start, self.waited = eng, sem, 0, start, waited

    def wait(self, ins):
        ins.then_inc(self.sem, 1)
        self.n += 1
        self.eng.wait_ge(self.sem, self.start + self.n)

    def wait_alone(self, ins):
        self.wait(ins)
        self.eng.sem_inc(self.waited, 1)


def modulation(nc, dram, kept):
    SLICE = BANK
    NS = N_MOD * D // SLICE
    RING = 3
    N_TURN = NS // RING
    x, mod = kept["x"], kept["mod"]
    with ExitStack() as ctx:
        sb, ps, sem = ctx_tools(nc, ctx)
        c_raw = sb("c_raw", [P, KD])
        c_silu = sb("c_silu", [P, KD])
        c_wide = sb("c_wide", [P, KD, P])
        w = sb("w_ada_ring", [P, RING, KD, SLICE])
        gains = sb("gains", [P, 4, D])
        squares = sb("m_squares", [P, D])
        sums, var, root, tmp = (sb(f"m_{n}", [P, TT]) for n in ("sum", "var", "root", "tmp"))
        inv = kept["x_inv"]
        out = [ps(f"mod_ps{i}", [P, BANK]) for i in range(RING)]
        c_in, gains_in, const_in = (sem(f"m_{n}") for n in ("cin", "gin", "kin"))
        silu_done, wide_done = sem("m_silu"), sem("m_wide")
        w_in = [sem(f"m_w_in{i}") for i in range(RING)]
        slice_made, slice_kept, rows, gate_rows = (sem(f"m_{n}") for n in ("made", "kept", "rows", "gates"))
        squared, var_made, root_made, steps = (sem(f"m_{n}") for n in ("sq", "var", "root", "step"))
        block = ctx.enter_context(nc.Block())
        w_view = dram["w_ada"][0].rearrange("(p k) n -> p k n", k=KD)
        X_TURN = TT // N_TURN
        loads = [3 if n < X_TURN else 2 for n in range(RING)]

        @block.sync
        def _(sp):
            sp.dma_start(c_raw[:, :], dram["c"].rearrange("b (p k) -> (b p) k", k=KD)).then_inc(c_in, 16)

            def turn(it):
                for n in range(RING):
                    behind(sp, slice_made, (it - 1) * RING + n + 1)
                    col = bass.ds((it * RING + n) * SLICE, SLICE)
                    sp.dma_start(w[:, n], w_view[:, :, col]).then_inc(w_in[n], 16)
                    sp.dma_start(mod[:, col], dram["b_ada"][0:1, col].broadcast_to([P, SLICE])).then_inc(w_in[n], 16)
                    if n < X_TURN:
                        sp.dma_start(x[:, bass.ds(it * X_TURN + n, 1), :].rearrange("p a d -> p (a d)"),
                                     dram["x"][0][bass.ds((it * X_TURN + n) * P, P), :]).then_inc(w_in[n], 16)

            turns(sp, N_TURN, turn)
            for i, name in enumerate(("g_pre_mix", "g_post_mix", "g_pre_ffn", "g_post_ffn")):
                sp.dma_start(gains[:, i, :], dram[name][0:1, :].broadcast_to([P, D])).then_inc(gains_in, 16)
            for name in ("ident", "iota", "causal"):
                sp.dma_start(kept[name][:, :], dram[name]).then_inc(const_in, 16)
            sp.wait_ge(const_in, 48)

        @block.scalar
        def _(act):
            act.wait_ge(c_in, 16)
            nc.scalar.activation(c_silu[:, :], c_raw[:, :], ACT.Silu).then_inc(silu_done, 1)
            for it in range(N_TURN):
                for n in range(X_TURN):
                    t = it * X_TURN + n
                    act.wait_ge(slice_made, it * RING + n + 1)
                    behind(act, squared, t)
                    nc.scalar.activation(squares[:, :], x[:, t, :], ACT.Square,
                                         accum_out=sums[:, t:t + 1]).then_inc(squared, 1)
            act.wait_ge(var_made, 1)
            nc.scalar.activation(root[:, :], var[:, :], ACT.Sqrt).then_inc(root_made, 1)

        @block.tensor
        def _(pe):
            pe.wait_ge(wide_done, 1)

            def turn(it):
                for n in range(RING):
                    pe.wait_ge(w_in[n], it * (16 * loads[n]) + 16 * loads[n])
                    behind(pe, slice_kept, (it - 1) * RING + n + 1)
                    for k in range(KD):
                        mm = nc.tensor.matmul(out[n][:, :], c_wide[:, k, :], w[:, n, k, :],
                                              start=(k == 0), stop=(k == KD - 1))
                    mm.then_inc(slice_made, 1)

            turns(pe, N_TURN, turn)

        @block.vector
        def _(dve):
            dve.wait_ge(silu_done, 1)
            nc.vector.tensor_copy(c_wide[:, :, :], c_silu[:, :, None].broadcast_to([P, KD, P])) \
                .then_inc(wide_done, 1)
            with dve.Fori(0, N_TURN) as it:
                for n in range(RING):
                    dve.wait_ge(slice_made, it * RING + n + 1)
                    col = bass.ds((it * RING + n) * SLICE, SLICE)
                    nc.vector.tensor_tensor(mod[:, col], out[n][:, :], mod[:, col], ALU.add) \
                        .then_inc(slice_kept, 1)
            dve.wait_ge(slice_kept, NS)
            dve.wait_ge(gains_in, 64)
            for m, g in ((1, 0), (4, 2)):
                row = mod[:, m * D:(m + 1) * D]
                nc.vector.scalar_tensor_tensor(row, row, 1.0, gains[:, g, :], ALU.add, ALU.mult).then_inc(rows, 1)
            ch = Chain(dve, steps)
            dve.wait_ge(squared, TT)
            nc.vector.tensor_scalar(var[:, :], sums[:, :], 1.0 / D, EPS, ALU.mult, ALU.add).then_inc(var_made, 1)
            dve.wait_ge(root_made, 1)
            ch.wait(nc.vector.reciprocal(inv[:, :], root[:, :]))
            dve.wait_ge(var_made, 1)
            ch.wait(nc.vector.tensor_tensor(tmp[:, :], inv[:, :], inv[:, :], ALU.mult))
            ch.wait(nc.vector.tensor_tensor(tmp[:, :], tmp[:, :], var[:, :], ALU.mult))
            ch.wait(nc.vector.tensor_scalar(tmp[:, :], tmp[:, :], -0.5, 1.5, ALU.mult, ALU.add))
            ch.wait(nc.vector.tensor_tensor(inv[:, :], inv[:, :], tmp[:, :], ALU.mult))
            dve.wait_ge(rows, 2)

        @block.gpsimd
        def _(pool):
            pool.wait_ge(slice_kept, NS)
            pool.wait_ge(gains_in, 64)
            for m, g in ((2, 1), (5, 3)):
                row = mod[:, m * D:(m + 1) * D]
                nc.gpsimd.tensor_tensor(row, row, gains[:, g, :], ALU.mult).then_inc(gate_rows, 1)
            pool.wait_ge(gate_rows, 2)


def norm_and_turn(nc, kept, scale_row, shift_row, h_hi, h_lo):
    x, inv, ident = kept["x"], kept["x_inv"], kept["ident"]
    with ExitStack() as ctx:
        sb, ps, sem = ctx_tools(nc, ctx)
        h = sb("n1_h", [P, 3, D])
        turned = [ps(f"n1_ps{i}", [P, 2, BANK]) for i in range(2)]
        scaled, h_made, h_turn, hi_made, lo_made = (sem(f"n1_{n}") for n in ("sc", "hm", "ht", "hi", "lo"))
        block = ctx.enter_context(nc.Block())

        @block.scalar
        def _(act):
            for t in range(TT):
                act.wait_ge(h_turn, t + 1)
                src = turned[t % 2][:, :, :].rearrange("p a (k c) -> p (a k) c", c=P)
                nc.scalar.activation(h_hi[:, :, t * P:(t + 1) * P], src, ACT.Copy, scale=S_H).then_inc(hi_made, 1)

        @block.vector
        def _(dve):
            def low(t):
                src = turned[t % 2][:, :, :].rearrange("p a (k c) -> p (a k) c", c=P)
                dve.wait_ge(hi_made, t + 1)
                nc.vector.scalar_tensor_tensor(h_lo[:, :, t * P:(t + 1) * P], src, S_H,
                                               h_hi[:, :, t * P:(t + 1) * P], ALU.mult, ALU.subtract) \
                    .then_inc(lo_made, 1)

            for t in range(TT):
                behind(dve, h_turn, t - 2)
                nc.vector.scalar_tensor_tensor(h[:, t % 3, :], x[:, t, :], inv[:, t:t + 1], scale_row,
                                               ALU.mult, ALU.mult).then_inc(scaled, 1)
                if t >= 2:
                    low(t - 2)
            low(TT - 2)
            low(TT - 1)

        @block.gpsimd
        def _(pool):
            for t in range(TT):
                pool.wait_ge(scaled, t + 1)
                nc.gpsimd.tensor_tensor(h[:, t % 3, :], h[:, t % 3, :], shift_row, ALU.add).then_inc(h_made, 1)

        @block.tensor
        def _(pe):
            for t in range(TT):
                pe.wait_ge(h_made, t + 1)
                behind(pe, lo_made, t - 1)
                for k in range(KD):
                    tr = nc.tensor.transpose(turned[t % 2][:, k // 4, (k % 4) * P:(k % 4 + 1) * P],
                                             h[:, t % 3, k * P:(k + 1) * P], ident[:, :])
                tr.then_inc(h_turn, 1)


def project_in(nc, dram, scratch, kept, h_hi, h_lo):
    DESCALE = 1.0 / (S_H * S_U)
    with ExitStack() as ctx:
        sb, ps, sem = ctx_tools(nc, ctx)
        RING = 2
        w = sb("w_ring", [P, RING, KD, P])
        w_hi, w_lo = sb("w_hi", [P, RING, KD, P], F16), sb("w_lo", [P, RING, KD, P], F16)
        VF_W = V_W + FOX_H
        wv = sb("wv", [P, KD, VF_W])
        wv_hi, wv_lo = sb("wv_hi", [P, KD, VF_W], F16), sb("wv_lo", [P, KD, VF_W], F16)
        wide = sb("qk_rows", [P, 2, T])
        vals = sb("v_rows", [P, 2, V_W])
        bias_f = sb("bias_f", [FOX_H, 1])
        f_logit, f_abs, f_exp, f_min, f_one = (
            sb(f"f_{n}", [FOX_H, T]) for n in ("logit", "abs", "exp", "min", "one"))
        f_sum, f_neg = f_logit, f_exp
        acc = [ps(f"in_ps{i}", [P, 2, BANK]) for i in range(2)]
        acc_v = [ps(f"in_psv{i}", [P, 2, BANK]) for i in range(2)]
        w_in = [sem(f"i_w{i}") for i in range(RING)]
        wv_in, small_in, f_steps = sem("i_wv"), sem("i_small"), sem("i_f")
        hi_made, lo_made, vhi_made, vlo_made = sem("i_hi"), sem("i_lo"), sem("i_vhi"), sem("i_vlo")
        made, taken, v_made, v_taken = sem("i_made"), sem("i_taken"), sem("i_vmade"), sem("i_vtaken")
        stored = [sem(f"i_st{i}") for i in range(2)]
        v_stored = [sem(f"i_vst{i}") for i in range(2)]
        f_act, f_stored = sem("i_fact"), sem("i_fst")
        block = ctx.enter_context(nc.Block())
        w_view = dram["w_in"][0].rearrange("(k p) n -> p k n", p=P)
        tiles = [(j * P, SCALE if j < 4 else 1.0, scratch["qk_fox"][2 * j:2 * j + 2, 0:HD, :]) for j in range(8)]
        tiles += [(COL_SQ + j * P, SCALE if j < 4 else 1.0, scratch["qk_swa"][2 * j:2 * j + 2]) for j in range(5)]
        NTL = len(tiles)

        @block.sync
        def _(sp):
            def load(j):
                sp.dma_start(w[:, j % RING], w_view[:, :, tiles[j][0]:tiles[j][0] + P]).then_inc(w_in[j % RING], 16)

            for j in range(RING):
                load(j)
            sp.dma_start(bias_f[:, :], dram["b_fgate"].rearrange("a h -> h a")).then_inc(small_in, 16)
            sp.dma_start(wv[:, :, V_W:], w_view[:, :, COL_FF:COL_SQ]).then_inc(wv_in, 16)
            sp.dma_start(wv[:, :, 0:FOX_H * HD], w_view[:, :, COL_FV:COL_FF]).then_inc(wv_in, 16)
            sp.dma_start(wv[:, :, FOX_H * HD:V_W], w_view[:, :, COL_SV:IN_W]).then_inc(wv_in, 16)
            for j in range(RING, NTL):
                sp.wait_ge(lo_made, j - RING + 1)
                load(j)
            for s in range(2):
                sp.wait_ge(stored[s], 16 * 2 * ((NTL - s + 1) // 2))
                sp.wait_ge(v_stored[s], 16 * TT // 2)
            sp.wait_ge(f_stored, 16 * 4)

        @block.tensor
        def _(pe):
            def heads(j):
                pe.wait_ge(lo_made, j + 1)
                if j >= 2:
                    pe.wait_ge(taken, j - 1)
                for k in range(KD):
                    for wt, h, first, last in ((w_hi, h_hi, k == 0, False), (w_hi, h_lo, False, False),
                                               (w_lo, h_hi, False, k == KD - 1)):
                        for half in range(2):
                            mm = nc.tensor.matmul(acc[j % 2][:, half, :], wt[:, j % RING, k, :],
                                                  h[:, k, half * BANK:(half + 1) * BANK], start=first, stop=last)
                mm.then_inc(made, 1)

            heads(0)
            heads(1)
            pe.wait_ge(vlo_made, 1)
            for half in range(2):
                cols = slice(half * BANK, (half + 1) * BANK)
                for k in range(KD):
                    for wt, h, first, last in ((wv_hi, h_hi, k == 0, False), (wv_hi, h_lo, False, False),
                                               (wv_lo, h_hi, False, k == KD - 1)):
                        mm = nc.tensor.matmul(acc_v[0][0:FOX_H, half, :], wt[:, k, V_W:], h[:, k, cols],
                                              start=first, stop=last)
            mm.then_inc(v_made, 1)
            for t in range(TT):
                pe.wait_ge(v_taken, max(t, 1))
                for lo, hi, half in ((0, BANK, 0), (BANK, V_W, 1)):
                    for k in range(KD):
                        for h, wt, first, last in ((h_hi, wv_hi, k == 0, False), (h_hi, wv_lo, False, False),
                                                   (h_lo, wv_hi, False, k == KD - 1)):
                            mm = nc.tensor.matmul(acc_v[t % 2][:, half, 0:hi - lo], h[:, k, t * P:(t + 1) * P],
                                                  wt[:, k, lo:hi], start=first, stop=last)
                mm.then_inc(v_made, 1)
            for j in range(2, NTL):
                heads(j)

        @block.scalar
        def _(act):
            def split(j):
                act.wait_ge(w_in[j % RING], 16 * (j // RING + 1))
                if j >= RING:
                    act.wait_ge(made, j - RING + 1)
                nc.scalar.activation(w_hi[:, j % RING], w[:, j % RING], ACT.Copy, scale=S_U).then_inc(hi_made, 1)

            split(0)
            split(1)
            act.wait_ge(wv_in, 48)
            nc.scalar.activation(wv_hi[:, :, :], wv[:, :, :], ACT.Copy, scale=S_U).then_inc(vhi_made, 1)
            act.wait_ge(f_steps, 1)
            nc.scalar.activation(f_abs[:, :], f_logit[:, :], ACT.Abs).then_inc(f_act, 1)
            act.wait_ge(f_act, 1)
            nc.scalar.activation(f_exp[:, :], f_abs[:, :], ACT.Exp, scale=-1.0).then_inc(f_act, 1)
            act.wait_ge(f_act, 2)
            nc.scalar.activation(f_abs[:, :], f_exp[:, :], ACT.Ln, bias=1.0).then_inc(f_act, 1)
            for j in range(NTL):
                act.wait_ge(made, j + 1)
                if j >= 2:
                    act.wait_ge(stored[j % 2], 32 * (j // 2))
                nc.scalar.activation(wide[:, j % 2, :], acc[j % 2][:, :, :].rearrange("p a b -> p (a b)"), ACT.Copy,
                                     scale=tiles[j][1] * DESCALE).then_inc(taken, 1)
                if j + 2 < NTL:
                    split(j + 2)

        @block.vector
        def _(dve):
            def split(j):
                dve.wait_ge(hi_made, j + 1)
                nc.vector.scalar_tensor_tensor(w_lo[:, j % RING], w[:, j % RING], S_U, w_hi[:, j % RING],
                                               ALU.mult, ALU.subtract).then_inc(lo_made, 1)

            split(0)
            split(1)
            dve.wait_ge(vhi_made, 1)
            nc.vector.scalar_tensor_tensor(wv_lo[:, :, :], wv[:, :, :], S_U, wv_hi[:, :, :],
                                           ALU.mult, ALU.subtract).then_inc(vlo_made, 1)
            dve.wait_ge(small_in, 16)
            dve.wait_ge(v_made, 1)
            nc.vector.tensor_scalar(f_logit[:, :], acc_v[0][0:FOX_H, :, :].rearrange("p a b -> p (a b)"),
                                    DESCALE, bias_f[:, 0:1], ALU.mult, ALU.add).then_inc(f_steps, 1)
            dve.wait_ge(f_steps, 1)
            nc.vector.tensor_scalar(f_min[:, :], f_logit[:, :], 0.0, None, ALU.min).then_inc(v_taken, 1)
            nc.vector.memset(f_one[:, :], 1.0).then_inc(f_steps, 1)
            dve.wait_ge(f_act, 3)
            dve.wait_ge(v_taken, 1)
            nc.vector.tensor_tensor(f_min[:, :], f_min[:, :], f_abs[:, :], ALU.subtract).then_inc(f_steps, 1)
            dve.wait_ge(f_steps, 3)
            nc.vector.tensor_tensor_scan(f_sum[:, :], f_one[:, :], f_min[:, :], 0.0, ALU.mult, ALU.add) \
                .then_inc(f_steps, 1)
            dve.wait_ge(f_steps, 4)
            nc.vector.tensor_scalar(f_neg[:, :], f_sum[:, :], -1.0, None, ALU.mult).then_inc(f_steps, 1)
            for t in range(TT):
                dve.wait_ge(v_made, t + 2)
                if t >= 2:
                    dve.wait_ge(v_stored[t % 2], 16 * (t // 2))
                nc.vector.tensor_scalar(vals[:, t % 2, :],
                                        acc_v[t % 2][:, :, :].rearrange("p a b -> p (a b)")[:, 0:V_W],
                                        DESCALE, None, ALU.mult).then_inc(v_taken, 1)
            for j in range(2, NTL):
                split(j)

        @block.gpsimd
        def _(pool):
            pool.wait_ge(f_steps, 5)
            rows = scratch["qk_fox"]
            pool.dma_start(rows[0:FOX_H, HD, :], f_sum[:, :]).then_inc(f_stored, 16)
            pool.dma_start(rows[0:FOX_H, HD + 1, :], f_one[:, :]).then_inc(f_stored, 16)
            pool.dma_start(rows[FOX_H:, HD, :], f_one[:, :]).then_inc(f_stored, 16)
            pool.dma_start(rows[FOX_H:, HD + 1, :], f_neg[:, :]).then_inc(f_stored, 16)
            for t in range(TT):
                pool.wait_ge(v_taken, t + 2)
                pool.dma_start(scratch["v"][t * P:(t + 1) * P, :], vals[:, t % 2, :]).then_inc(v_stored[t % 2], 16)
            for j in range(NTL):
                pool.wait_ge(taken, j + 1)
                for head in range(2):
                    pool.dma_start(tiles[j][2][head], wide[head * HD:(head + 1) * HD, j % 2, :]) \
                        .then_inc(stored[j % 2], 16)


def fox_attention(nc, scratch, kept):
    ident, causal = kept["ident"], kept["causal"]
    with ExitStack() as ctx:
        sb, ps, sem = ctx_tools(nc, ctx)
        q, k = sb("fx_q", [AUG, 2, T]), sb("fx_k", [AUG, 2, T])
        v = sb("fx_v", [P, 2, TT, HD])
        prob, prob_t = sb("fx_p", [P, 2, T]), sb("fx_pt", [P, 2, T])
        n_max, row_sum, inv = (sb(f"fx_{n}", [P, 2 * TT]) for n in ("max", "sum", "inv"))
        out = sb("fx_out", [P, 2, TT, HD])
        score = [ps(f"fx_s{i}", [P, 2 * BANK]) for i in range(2)]
        turned = ps("fx_t", [P, 2 * BANK])
        mixed = [ps(f"fx_o{i}", [P, HD]) for i in range(2)]
        head_in = [sem(f"fx_in{i}") for i in range(2)]
        scored, masked, maxed, probed = (sem(f"fx_{n}") for n in ("scored", "masked", "maxed", "probed"))
        turn_made, turn_kept, mix_made, inv_made, mix_kept = (
            sem(f"fx_{n}") for n in ("turned", "tkept", "mixm", "invm", "mixk"))
        stored = [sem(f"fx_st{i}") for i in range(2)]
        block = ctx.enter_context(nc.Block())
        NI = FOX_H // 2
        order = [b for a in range(TT // 2) for b in (TT - 1 - a, a)]
        units = [(h, i) for h in range(2) for i in order]
        NU = len(units)

        @block.sync
        def _(sp):
            def turn(it):
                for h in range(2):
                    behind(sp, mix_made, it * NU + TT * h)
                    head = it * 2 + h
                    sp.dma_start(q[:, h, :], scratch["qk_fox"][bass.ds(head, 1), :, :].rearrange("h r t -> (h r) t")) \
                        .then_inc(head_in[h], 16)
                    sp.dma_start(k[:, h, :], scratch["qk_fox"][bass.ds(head + FOX_H, 1), :, :]
                                 .rearrange("h r t -> (h r) t")).then_inc(head_in[h], 16)
                    sp.dma_start(v[:, h, :, :], scratch["v"][:, bass.ds(head * HD, HD)]
                                 .rearrange("(b p) d -> p b d", p=P)).then_inc(head_in[h], 16)

            turns(sp, NI, turn)

        @block.tensor
        def _(pe):
            pe.sem_inc(mix_made, TT)
            def turn(it):
                def scores(u):
                    h, i = units[u]
                    if u % TT == 0:
                        pe.wait_ge(head_in[h], 48 * it + 48)
                    pe.wait_ge(probed, it * NU + u + 1)
                    for c in range(0, (i + 1) * P, BANK):
                        w = min(BANK, (i + 1) * P - c)
                        mm = nc.tensor.matmul(score[u % 2][:, c:c + w], q[:, h, i * P:(i + 1) * P],
                                              k[:, h, c:c + w], start=True, stop=True)
                    mm.then_inc(scored, 1)

                def mix(u):
                    h, i = units[u]
                    pe.wait_ge(probed, it * NU + u + 1 + 2)
                    pe.wait_ge(turn_kept, it * NU + u + 1)
                    for b in range(i + 1):
                        tr = nc.tensor.transpose(turned[:, b * P:(b + 1) * P], prob[:, u % 2, b * P:(b + 1) * P],
                                                 ident[:, :])
                    tr.then_inc(turn_made, 1)

                def weigh(u):
                    h, i = units[u]
                    pe.wait_ge(turn_kept, it * NU + u + 1 + 1)
                    pe.wait_ge(mix_kept, it * NU + u + 1)
                    for b in range(i + 1):
                        mm = nc.tensor.matmul(mixed[u % 2][:, :], prob_t[:, u % 2, b * P:(b + 1) * P], v[:, h, b, :],
                                              start=(b == 0), stop=(b == i))
                    mm.then_inc(mix_made, 1)

                scores(0)
                scores(1)
                for u in range(NU):
                    if u + 2 < NU:
                        scores(u + 2)
                    mix(u)
                    if u >= 1:
                        weigh(u - 1)
                weigh(NU - 1)

            turns(pe, NI, turn)

        @block.vector
        def _(dve):
            dve.sem_inc(turn_kept, 1)
            dve.sem_inc(mix_kept, 2)
            def turn(it):
                def stats(u):
                    h, i = units[u]
                    dve.wait_ge(scored, it * NU + u + 1)
                    diag = score[u % 2][:, i * P:(i + 1) * P]
                    nc.vector.tensor_tensor(diag, diag, causal[:, :], ALU.add).then_inc(masked, 1)
                    dve.wait_ge(masked, it * NU + u + 1)
                    nc.vector.tensor_reduce(n_max[:, u:u + 1], score[u % 2][:, 0:(i + 1) * P], AX_X, ALU.max,
                                            negate=True).then_inc(maxed, 1)

                def keep(u):
                    h, i = units[u]
                    dve.wait_ge(turn_made, it * NU + u + 1)
                    dve.wait_ge(mix_made, it * NU + u - 1 + TT)
                    nc.vector.tensor_copy(prob_t[:, u % 2, 0:(i + 1) * P], turned[:, 0:(i + 1) * P]) \
                        .then_inc(turn_kept, 1)
                    nc.vector.reciprocal(inv[:, u:u + 1], row_sum[:, u:u + 1]).then_inc(inv_made, 1)

                def norm(u):
                    h, i = units[u]
                    dve.wait_ge(mix_made, it * NU + u + 1 + TT)
                    dve.wait_ge(inv_made, it * NU + u + 1)
                    if u % TT == 0:
                        behind(dve, stored[h], it * 16)
                    nc.vector.tensor_scalar(out[:, h, i, :], mixed[u % 2][:, :], inv[:, u:u + 1], None, ALU.mult) \
                        .then_inc(mix_kept, 1)

                stats(0)
                stats(1)
                for u in range(NU):
                    if u + 2 < NU:
                        stats(u + 2)
                    keep(u)
                    if u >= 1:
                        norm(u - 1)
                norm(NU - 1)

            turns(dve, NI, turn)

        @block.scalar
        def _(act):
            act.sem_inc(probed, 2)
            def turn(it):
                for u, (h, i) in enumerate(units):
                    act.wait_ge(maxed, it * NU + u + 1)
                    if u >= 2:
                        behind(act, inv_made, it * NU + u - 1)
                    else:
                        behind(act, inv_made, it * NU)
                    nc.scalar.activation(prob[:, u % 2, 0:(i + 1) * P], score[u % 2][:, 0:(i + 1) * P], ACT.Exp,
                                         bias=n_max[:, u:u + 1], accum_out=row_sum[:, u:u + 1]).then_inc(probed, 1)

            turns(act, NI, turn)

        @block.gpsimd
        def _(pool):
            def turn(it):
                for h in range(2):
                    pool.wait_ge(mix_kept, it * NU + TT * (h + 1) + 2)
                    pool.dma_start(scratch["mix"][:, bass.ds((it * 2 + h) * HD, HD)].rearrange("(b p) d -> p b d", p=P),
                                   out[:, h, :, :]).then_inc(stored[h], 16)

            turns(pool, NI, turn)
            for h in range(2):
                pool.wait_ge(stored[h], 16 * NI)


def swa_attention(nc, dram, scratch, kept):
    ident = kept["ident"]
    G = SWA_GROUP
    with ExitStack() as ctx:
        sb, ps, sem = ctx_tools(nc, ctx)
        q, k = sb("sw_q", [HD, SWA_H, T]), sb("sw_k", [HD, SWA_KV, T])
        v = sb("sw_v", [P, TT, SWA_KV * HD])
        bias = sb("sw_bias", [P, SWA_H, 2 * P])
        sink = sb("sw_sink", [P, SWA_H])
        prob, prob_t = sb("sw_p", [P, 2, G, 2 * P]), sb("sw_pt", [P, 2, G, 2 * P])
        out = sb("sw_out", [P, TT, SWA_H, HD])
        NU = SWA_KV * TT
        top, n_max, less, sink_exp, row_sum, total, inv = (
            sb(f"sw_{n}", [P, NU, G]) for n in ("top", "max", "less", "sexp", "sum", "tot", "inv"))
        score = [ps(f"sw_s{i}", [P, G, 2 * P]) for i in range(2)]
        turned = ps("sw_t", [P, G, 2 * P])
        mixed = [ps(f"sw_o{i}", [P, G, HD]) for i in range(2)]
        qk_in, bias_in, v_in = [sem(f"sw_qk{i}") for i in range(2)], sem("sw_bin"), sem("sw_vin")
        scored, biased, tops, maxed, lessed, probed = (
            sem(f"sw_{n}") for n in ("scored", "biased", "tops", "maxed", "lessed", "probed"))
        turn_made, turn_kept, mix_made, totaled, inv_made, mix_kept, stored = (
            sem(f"sw_{n}") for n in ("turned", "tkept", "mixm", "tot", "invm", "mixk", "stored"))
        block = ctx.enter_context(nc.Block())
        units = [(g, i) for i in range(TT) for g in range(SWA_KV)]

        def spans(i):
            return [(1, 0)] if i == 0 else [(0, i - 1), (1, i)]

        def band(i):
            return slice(P, 2 * P) if i == 0 else slice(0, 2 * P)

        @block.sync
        def _(sp):
            for half in range(2):
                cols = slice(half * BANK, (half + 1) * BANK)
                sp.dma_start(q[:, :, cols], scratch["qk_swa"][0:SWA_H, :, cols].rearrange("h r t -> r h t")) \
                    .then_inc(qk_in[half], 16)
                sp.dma_start(k[:, :, cols], scratch["qk_swa"][SWA_H:, :, cols].rearrange("h r t -> r h t")) \
                    .then_inc(qk_in[half], 16)
                if half == 0:
                    sp.dma_start(bias[:, :, :], dram["swa_bias"]).then_inc(bias_in, 16)
                    sp.dma_start(sink[:, :], dram["swa_sinks"][0:1, :].broadcast_to([P, SWA_H])).then_inc(bias_in, 16)
                    sp.dma_start(v[:, :, :], scratch["v"][:, FOX_H * HD:].rearrange("(b p) d -> p b d", p=P)) \
                        .then_inc(v_in, 16)
            for i in range(TT):
                sp.wait_ge(mix_kept, SWA_KV * (i + 1))
                sp.dma_start(scratch["mix"][i * P:(i + 1) * P, FOX_H * HD:],
                             out[:, i, :, :].rearrange("p h d -> p (h d)")).then_inc(stored, 16)
            sp.wait_ge(stored, 16 * TT)

        @block.tensor
        def _(pe):
            def scores(u):
                g, i = units[u]
                if u == 0:
                    pe.wait_ge(qk_in[0], 32)
                if g == 0 and i == TT // 2:
                    pe.wait_ge(qk_in[1], 32)
                if u >= 2:
                    pe.wait_ge(probed, (G + 1) * (u - 1))
                for n in range(G):
                    mm = nc.tensor.matmul(score[u % 2][:, n, band(i)], q[:, g * G + n, i * P:(i + 1) * P],
                                          k[:, g, max(i - 1, 0) * P:(i + 1) * P], start=True, stop=True)
                mm.then_inc(scored, 1)

            def turn(u):
                g, i = units[u]
                pe.wait_ge(probed, (G + 1) * (u + 1))
                if u >= 1:
                    pe.wait_ge(turn_kept, u)
                for n in range(G):
                    for place, b in spans(i):
                        tr = nc.tensor.transpose(turned[:, n, place * P:(place + 1) * P],
                                                 prob[:, u % 2, n, place * P:(place + 1) * P], ident[:, :])
                tr.then_inc(turn_made, 1)

            def weigh(u):
                g, i = units[u]
                if u == 0:
                    pe.wait_ge(v_in, 16)
                pe.wait_ge(turn_kept, u + 1)
                if u >= 2:
                    pe.wait_ge(mix_kept, u - 1)
                for n in range(G):
                    for place, b in spans(i):
                        mm = nc.tensor.matmul(mixed[u % 2][:, n, :], prob_t[:, u % 2, n, place * P:(place + 1) * P],
                                              v[:, b, g * HD:(g + 1) * HD],
                                              start=(place == spans(i)[0][0]), stop=(place == 1))
                mm.then_inc(mix_made, 1)

            scores(0)
            scores(1)
            for u in range(NU):
                if u + 2 < NU:
                    scores(u + 2)
                turn(u)
                if u >= 1:
                    weigh(u - 1)
            weigh(NU - 1)

        @block.vector
        def _(dve):
            dve.wait_ge(bias_in, 32)

            def stats(u):
                g, i = units[u]
                s = score[u % 2][:, :, band(i)]
                dve.wait_ge(scored, u + 1)
                nc.vector.tensor_tensor(s, s, bias[:, g * G:(g + 1) * G, band(i)], ALU.add).then_inc(biased, 1)
                dve.wait_ge(biased, u + 1)
                nc.vector.tensor_reduce(top[:, u, :], s, AX_X, ALU.max).then_inc(tops, 1)
                dve.wait_ge(tops, 2 * u + 1)
                nc.vector.tensor_tensor(top[:, u, :], top[:, u, :], sink[:, g * G:(g + 1) * G], ALU.max).then_inc(tops, 1)
                dve.wait_ge(tops, 2 * u + 2)
                nc.vector.tensor_scalar(n_max[:, u, :], top[:, u, :], -1.0, None, ALU.mult).then_inc(maxed, 1)
                nc.vector.tensor_tensor(less[:, u, :], sink[:, g * G:(g + 1) * G], top[:, u, :], ALU.subtract) \
                    .then_inc(lessed, 1)

            def sums(u):
                g, i = units[u]
                dve.wait_ge(probed, (G + 1) * (u + 1))
                nc.vector.tensor_tensor(total[:, u, :], row_sum[:, u, :], sink_exp[:, u, :], ALU.add).then_inc(totaled, 1)
                dve.wait_ge(totaled, u + 1)
                nc.vector.reciprocal(inv[:, u, :], total[:, u, :]).then_inc(inv_made, 1)

            def norm(u):
                g, i = units[u]
                dve.wait_ge(mix_made, u + 1)
                dve.wait_ge(inv_made, u + 1)
                nc.vector.tensor_tensor(out[:, i, g * G:(g + 1) * G, :], mixed[u % 2][:, :, :],
                                        inv[:, u, :, None].broadcast_to([P, G, HD]), ALU.mult).then_inc(mix_kept, 1)

            stats(0)
            stats(1)
            for u in range(NU):
                if u + 2 < NU:
                    stats(u + 2)
                sums(u)
                if u >= 1:
                    norm(u - 1)
            norm(NU - 1)

        @block.scalar
        def _(act):
            def keep(u):
                g, i = units[u]
                act.wait_ge(turn_made, u + 1)
                if u >= 2:
                    act.wait_ge(mix_made, u - 1)
                nc.scalar.copy(prob_t[:, u % 2, :, band(i)], turned[:, :, band(i)]).then_inc(turn_kept, 1)

            for u, (g, i) in enumerate(units):
                act.wait_ge(maxed, u + 1)
                act.wait_ge(lessed, u + 1)
                if u >= 2:
                    act.wait_ge(turn_made, u - 1)
                for n in range(G):
                    nc.scalar.activation(prob[:, u % 2, n, band(i)], score[u % 2][:, n, band(i)], ACT.Exp,
                                         bias=n_max[:, u, n:n + 1], accum_out=row_sum[:, u, n:n + 1]).then_inc(probed, 1)
                nc.scalar.activation(sink_exp[:, u, :], less[:, u, :], ACT.Exp).then_inc(probed, 1)
                if u >= 1:
                    keep(u - 1)
            keep(NU - 1)


def project_out(nc, dram, scratch, kept, rows, gate2, h_hi, h_lo, h_rows):
    ident, x = kept["ident"], kept["x"]
    gate_row, scale_row, shift_row, gate2_row = rows
    STEPS = TT + 3
    with ExitStack() as ctx:
        sb, ps, sem = ctx_tools(nc, ctx)
        w = sb("wo", [P, 2, D])
        w_hi, w_lo = sb("wo_hi", [P, KD, D], F16), sb("wo_lo", [P, KD, D], F16)
        m = sb("wo_m", [P, 2, D])
        m_hi, m_lo = sb("wo_mhi", [P, 2, D], F16), sb("wo_mlo", [P, 2, D], F16)
        y_row, h, squares = sb("wo_y", [P, 2, D]), sb("wo_h", [P, 2, D]), sb("wo_sq", [P, D])
        sums, var, root, inv, tmp = (sb(f"wo_{n}", [P, STEPS, 2]) for n in ("sum", "var", "root", "inv", "tmp"))
        eps = sb("wo_eps", [P, 2])
        turned, h_turned = ps("wo_t", [P, 2 * BANK]), ps("wo_ht", [P, 2 * BANK])
        acc = [ps(f"wo_y{i}", [P, 2 * BANK]) for i in range(2)]
        w_in, m_in = [sem(f"wo_w{i}") for i in range(2)], [sem(f"wo_m{i}") for i in range(2)]
        whi_made, wlo_made, turn_made, mhi_made, mlo_made, y_made = (
            sem(f"wo_{n}") for n in ("whi", "wlo", "tm", "mhi", "mlo", "ym"))
        consts, y_squared, x_squared, var_made, root_made, step, y_normed, x_made, stored = (
            sem(f"wo_{n}") for n in ("consts", "sqy", "sqx", "var", "root", "step", "yn", "xm", "st"))
        h_made, h_turn, hhi_made, hlo_made = (sem(f"wo_{n}") for n in ("hm", "ht", "hhi", "hlo"))
        block = ctx.enter_context(nc.Block())

        @block.sync
        def _(sp):
            def load_m(t):
                if t >= 2:
                    sp.wait_ge(turn_made, t - 1)
                sp.dma_start(m[:, t % 2, :], scratch["mix"][t * P:(t + 1) * P, :]).then_inc(m_in[t % 2], 16)

            load_m(0)
            load_m(1)
            for k in range(KD):
                if k >= 2:
                    sp.wait_ge(wlo_made, k - 1)
                sp.dma_start(w[:, k % 2, :], dram["w_out"][0, k * P:(k + 1) * P, :]).then_inc(w_in[k % 2], 16)
            for t in range(TT):
                if t + 2 < TT:
                    load_m(t + 2)
                sp.wait_ge(x_made, t + 1)
                sp.dma_start(scratch["x_mid"][t * P:(t + 1) * P, :], x[:, t, :]).then_inc(stored, 16)
            sp.wait_ge(stored, 16 * TT)

        @block.tensor
        def _(pe):
            def turn(t):
                pe.wait_ge(m_in[t % 2], 16 * (t // 2 + 1))
                if t >= 1:
                    pe.wait_ge(mlo_made, t)
                for k in range(KD):
                    tr = nc.tensor.transpose(turned[:, k * P:(k + 1) * P], m[:, t % 2, k * P:(k + 1) * P], ident[:, :])
                tr.then_inc(turn_made, 1)

            def product(t):
                pe.wait_ge(mlo_made, t + 1)
                if t >= 2:
                    pe.wait_ge(y_normed, t - 1)
                for k in range(KD):
                    if t == 0:
                        pe.wait_ge(wlo_made, k + 1)
                    for a, wt, first, last in ((m_hi, w_hi, k == 0, False), (m_hi, w_lo, False, False),
                                               (m_lo, w_hi, False, k == KD - 1)):
                        for half in range(2):
                            cols = slice(half * BANK, (half + 1) * BANK)
                            mm = nc.tensor.matmul(acc[t % 2][:, cols], a[:, t % 2, k * P:(k + 1) * P], wt[:, k, cols],
                                                  start=first, stop=last)
                mm.then_inc(y_made, 1)

            def turn_h(t):
                pe.wait_ge(h_made, t + 1)
                if t >= 1:
                    pe.wait_ge(hlo_made, t)
                for k in range(KD):
                    tr = nc.tensor.transpose(h_turned[:, k * P:(k + 1) * P], h[:, t % 2, k * P:(k + 1) * P], ident[:, :])
                tr.then_inc(h_turn, 1)

            turn(0)
            for t in range(TT + 2):
                if t + 1 < TT:
                    turn(t + 1)
                if t < TT:
                    product(t)
                if t >= 2:
                    turn_h(t - 2)

        @block.scalar
        def _(act):
            def split_m(t):
                act.wait_ge(turn_made, t + 1)
                if t >= 2:
                    act.wait_ge(y_made, t - 1)
                nc.scalar.activation(m_hi[:, t % 2, :], turned[:, :], ACT.Copy, scale=S_H).then_inc(mhi_made, 1)

            split_m(0)
            for k in range(KD):
                act.wait_ge(w_in[k % 2], 16 * (k // 2 + 1))
                nc.scalar.activation(w_hi[:, k, :], w[:, k % 2, :], ACT.Copy, scale=S_U).then_inc(whi_made, 1)
            split_m(1)
            act.wait_ge(consts, 2)
            for t in range(1, TT + 3):
                if t - 1 < TT:
                    act.wait_ge(y_made, t)
                    if t >= 3:
                        act.wait_ge(x_squared, t - 2)
                    nc.scalar.activation(squares[:, :], acc[(t - 1) % 2][:, :], ACT.Square,
                                         accum_out=sums[:, t, 0:1]).then_inc(y_squared, 1)
                if 0 <= t - 2 < TT:
                    act.wait_ge(x_made, t - 1)
                    act.wait_ge(y_squared, min(t, TT))
                    if t - 1 >= TT:
                        act.wait_ge(x_squared, t - 2)
                    nc.scalar.activation(squares[:, :], x[:, t - 2, :], ACT.Square,
                                         accum_out=sums[:, t, 1:2]).then_inc(x_squared, 1)
                if t + 1 < TT:
                    split_m(t + 1)
                if t < TT + 2:
                    act.wait_ge(var_made, t)
                    nc.scalar.activation(root[:, t, :], var[:, t, :], ACT.Sqrt).then_inc(root_made, 1)
                if t >= 3:
                    act.wait_ge(h_turn, t - 2)
                    nc.scalar.activation(h_hi[:, :, (t - 3) * P:(t - 2) * P],
                                         h_turned[:, :].rearrange("p (k c) -> p k c", c=P), ACT.Copy,
                                         scale=S_H).then_inc(hhi_made, 1)

        @block.vector
        def _(dve):
            ch = Chain(dve, step)

            def split_m(t):
                dve.wait_ge(mhi_made, t + 1)
                nc.vector.scalar_tensor_tensor(m_lo[:, t % 2, :], turned[:, :], S_H, m_hi[:, t % 2, :],
                                               ALU.mult, ALU.subtract).then_inc(mlo_made, 1)

            nc.vector.memset(sums[:, :, :], 1.0).then_inc(consts, 1)
            nc.vector.memset(eps[:, 0:1], EPS * (S_H * S_U) ** 2)
            nc.vector.memset(eps[:, 1:2], EPS).then_inc(consts, 1)
            nc.vector.tensor_copy(gate2[:, :], gate2_row).then_inc(consts, 1)
            dve.wait_ge(consts, 3)
            split_m(0)
            for k in range(KD):
                dve.wait_ge(whi_made, k + 1)
                nc.vector.scalar_tensor_tensor(w_lo[:, k, :], w[:, k % 2, :], S_U, w_hi[:, k, :],
                                               ALU.mult, ALU.subtract).then_inc(wlo_made, 1)
            split_m(1)
            for t in range(1, TT + 3):
                normed = t < TT + 2
                if normed:
                    dve.wait_ge(y_squared, min(t, TT))
                    if t >= 2:
                        dve.wait_ge(x_squared, t - 1)
                    nc.vector.scalar_tensor_tensor(var[:, t, :], sums[:, t, :], 1.0 / D, eps[:, :],
                                                   ALU.mult, ALU.add).then_inc(var_made, 1)
                if t + 1 < TT:
                    split_m(t + 1)
                if normed:
                    dve.wait_ge(root_made, t)
                    dve.wait_ge(var_made, t)
                    ch.wait(nc.vector.reciprocal(inv[:, t, :], root[:, t, :]))
                    ch.wait(nc.vector.tensor_tensor(tmp[:, t, :], inv[:, t, :], inv[:, t, :], ALU.mult))
                    ch.wait(nc.vector.tensor_tensor(tmp[:, t, :], tmp[:, t, :], var[:, t, :], ALU.mult))
                    ch.wait(nc.vector.tensor_scalar(tmp[:, t, :], tmp[:, t, :], -0.5, 1.5, ALU.mult, ALU.add))
                    ch.wait(nc.vector.tensor_tensor(inv[:, t, :], inv[:, t, :], tmp[:, t, :], ALU.mult))
                if t - 1 < TT:
                    if t >= 3:
                        dve.wait_ge(x_made, t - 2)
                    nc.vector.scalar_tensor_tensor(y_row[:, (t - 1) % 2, :], acc[(t - 1) % 2][:, :], inv[:, t, 0:1],
                                                   gate_row, ALU.mult, ALU.mult).then_inc(y_normed, 1)
                if 0 <= t - 2 < TT:
                    r = t - 2
                    if r >= 2:
                        dve.wait_ge(h_turn, r - 1)
                    dve.wait_ge(x_made, r + 1)
                    ch.wait(nc.vector.scalar_tensor_tensor(h[:, r % 2, :], x[:, r, :], inv[:, t, 1:2], scale_row,
                                                           ALU.mult, ALU.mult))
                    if r < GT:
                        ch.wait(nc.vector.tensor_tensor(h_rows[:, r, :], h[:, r % 2, :], shift_row, ALU.add))
                    nc.vector.tensor_tensor(h[:, r % 2, :], h[:, r % 2, :], shift_row, ALU.add).then_inc(h_made, 1)
                if t >= 3:
                    cols = slice((t - 3) * P, (t - 2) * P)
                    dve.wait_ge(hhi_made, t - 2)
                    nc.vector.scalar_tensor_tensor(h_lo[:, :, cols], h_turned[:, :].rearrange("p (k c) -> p k c", c=P),
                                                   S_H, h_hi[:, :, cols], ALU.mult, ALU.subtract).then_inc(hlo_made, 1)

        @block.gpsimd
        def _(pool):
            for t in range(TT):
                pool.wait_ge(y_normed, t + 1)
                nc.gpsimd.tensor_tensor(x[:, t, :], x[:, t, :], y_row[:, t % 2, :], ALU.add).then_inc(x_made, 1)


def peer_queries(nc, dram, scratch, h_hi, h_lo):
    with ExitStack() as ctx:
        sb, ps, sem = ctx_tools(nc, ctx)
        w = sb("wq_raw", [P, 2, KD, P])
        w_hi, w_lo = sb("wq_hi", [P, 2, KD, P], F16), sb("wq_lo", [P, 2, KD, P], F16)
        rows = sb("pq_rows", [P, 2, T])
        acc = [ps(f"pq_ps{i}", [P, 2 * BANK]) for i in range(2)]
        w_in = [sem(f"pq_w{i}") for i in range(2)]
        hi_made, lo_made, made, taken = sem("pq_hi"), sem("pq_lo"), sem("pq_made"), sem("pq_taken")
        stored = [sem(f"pq_st{i}") for i in range(2)]
        block = ctx.enter_context(nc.Block())
        w_view = dram["w_query"][0].rearrange("(k p) n -> p k n", p=P)
        NP = NG // 2

        @block.sync
        def _(sp):
            def turn(it):
                for s in range(2):
                    behind(sp, lo_made, it * 2 + s - 1)
                    sp.dma_start(w[:, s], w_view[:, :, bass.ds((it * 2 + s) * P, P)]).then_inc(w_in[s], 16)

            turns(sp, NP, turn)

        @block.scalar
        def _(act):
            def turn(it):
                for s in range(2):
                    act.wait_ge(w_in[s], 16 * it + 16)
                    behind(act, made, it * 2 + s - 1)
                    nc.scalar.activation(w_hi[:, s], w[:, s], ACT.Copy, scale=S_U).then_inc(hi_made, 1)
                    if s == 0 and isinstance(it, int):
                        continue
                    g = it * 2 + s - 1
                    act.wait_ge(made, g + 1)
                    behind(act, stored[1 - s], it * 16 - 16 if s == 0 else it * 16)
                    nc.scalar.activation(rows[:, 1 - s, :], acc[1 - s][:, :], ACT.Copy, scale=1.0 / (S_H * S_U)) \
                        .then_inc(taken, 1)

            turns(act, NP, turn)
            act.wait_ge(made, NG)
            act.wait_ge(stored[1], 16 * (NP - 1))
            nc.scalar.activation(rows[:, 1, :], acc[1][:, :], ACT.Copy, scale=1.0 / (S_H * S_U)).then_inc(taken, 1)

        @block.vector
        def _(dve):
            with dve.Fori(0, NP) as it:
                for s in range(2):
                    dve.wait_ge(hi_made, it * 2 + s + 1)
                    nc.vector.scalar_tensor_tensor(w_lo[:, s], w[:, s], S_U, w_hi[:, s],
                                                   ALU.mult, ALU.subtract).then_inc(lo_made, 1)

        @block.tensor
        def _(pe):
            def turn(it):
                for s in range(2):
                    pe.wait_ge(lo_made, it * 2 + s + 1)
                    behind(pe, taken, it * 2 + s - 1)
                    for c in range(KD):
                        for wt, h, first, last in ((w_hi, h_hi, c == 0, False), (w_hi, h_lo, False, False),
                                                   (w_lo, h_hi, False, c == KD - 1)):
                            for half in range(2):
                                cols = slice(half * BANK, (half + 1) * BANK)
                                mm = nc.tensor.matmul(acc[s][:, cols], wt[:, s, c, :], h[:, c, cols],
                                                      start=first, stop=last)
                    mm.then_inc(made, 1)

            turns(pe, NP, turn)

        @block.gpsimd
        def _(pool):
            with pool.Fori(0, NP) as it:
                for s in range(2):
                    pool.wait_ge(taken, it * 2 + s + 1)
                    pool.dma_start(scratch["pq"][:, bass.ds(it * 2 + s, 1), :].rearrange("p g t -> p (g t)"),
                                   rows[:, s, :]).then_inc(stored[s], 16)
            for s in range(2):
                pool.wait_ge(stored[s], 16 * NP)


def peer_scores(nc, dram, scratch, kept, h_hi, h_lo, h_rows, coef, expert):
    ident, iota = kept["ident"], kept["iota"]
    PICK_B = 6
    GATE_STEPS, GATE_TOK = 48, TD // 48
    REST_STEPS = NBLK - TT * PICK_B - GATE_STEPS
    GATE_DOTS, REST_DOTS = 3, (3, 4)
    N0_GATE, N0_REST = TT * PICK_B, TT * PICK_B + GATE_STEPS
    Q0 = GATE_STEPS * GATE_DOTS
    TURN_DOTS = 8 * GATE_DOTS, 4 * sum(REST_DOTS)
    assert Q0 + REST_STEPS * sum(REST_DOTS) // 2 == GQ and all(d % GRING == 0 for d in TURN_DOTS)
    PIECE_STEPS = PIECE // GATE_TOK
    SUB = 4
    SUBS = GATE_TOK // SUB
    assert SUBS == 4
    with ExitStack() as ctx:
        sb, ps, sem = ctx_tools(nc, ctx)
        u_raw = sb("xu_raw", [P, 2, D])
        u_scaled = sb("xu_scaled", [P, D])
        u_hi, u_lo = sb("xu_hi", [P, 2, KD, P], F16), sb("xu_lo", [P, 2, KD, P], F16)
        act_g = sb("x_act", [P, 2, TD])
        arena = sb("x_arena", [P, 8, NG * NK])
        keys_t = arena[:, 0, :].rearrange("p (g k) -> p g k", g=NG)
        q = [arena[:, 1 + i, :].rearrange("p (g k) -> p g k", g=NG) for i in range(2)]
        sc = [arena[:, 3 + i, :].rearrange("p (g k) -> p g k", g=NG) for i in range(2)]
        rest = arena[:, 5, :].rearrange("p (g k) -> p g k", g=NG)
        cand, cand_rest = (arena[:, 6 + i, :].rearrange("p (h a b) -> p h a b", h=PH, a=TOPK) for i in range(2))
        keys = sc[0]
        gates = [arena[:, 4 * i:4 * i + 4, :].rearrange("p a b -> p (a b)").rearrange("p (k t) -> p k t", k=NK)
                 for i in range(2)]
        val = sb("pk_val", [P, PH, 2, TOPK])
        idx, idx_f = sb("pk_idx", [P, PH, 2, TOPK], U32), sb("pk_idx_f", [P, PH, 2, TOPK])
        best, best_i = sb("pk_best", [P, PH, TOPK]), sb("pk_best_i", [P, PH, TOPK], U32)
        part_i, part = sb("pk_part_i", [P, 2, PH, TOPK], U32), sb("pk_part", [P, 2, PH, TOPK])
        found, expo, norm = sb("pk_found", [P, 3, SLOTS]), sb("pk_exp", [P, PH, TOPK]), sb("pk_norm", [P, 2, PH])
        slot = sb("slot_t", [P, 3, T])
        second, first = sb("pg_second", [P, 2 * SUB, NK]), sb("pg_first", [P, 2 * SUB, NK])
        g_gate, dots = sb("g_gate", [P, GQ]), sb("g_dots", [P, GQ])
        row_idx = sb("g_idx", [P, max(TURN_DOTS)], U32)
        dots_now = sb("g_now", [P, max(TURN_DOTS)])
        g_row, junk = sb("g_row", [P, GRING, D]), sb("g_junk", [P, 2, D])

        u_turned = ps("xu_t", [P, KD, P])
        score = [ps(f"x_s{i}", [P, TD // 2]) for i in range(2)]
        sub = ps("x_sub", [P, NG // 2, NK])
        turned = ps("x_turned", [P, 4 * P])
        hot_ps = ps("x_gate", [P, SUB * NK])
        gate_ps = [hot_ps, turned]

        u_in = [sem(f"xu_in{i}") for i in range(2)]
        act_st = [sem(f"x_ast{i}") for i in range(2)]
        u_turn, u_kept, ulo_made, scored, gelued = (sem(f"x_{n}") for n in ("ut", "uk", "ulo", "sc", "ge"))
        load, keys_turned, keys_kept = sem("pk_ld"), sem("pk_kt"), sem("pk_kk")
        q_in = [sem(f"pk_q{i}") for i in range(2)]
        sub_made, sub_kept, chain, shifted, expd, slot_made, slot_turned, slot_kept, waited = (
            sem(f"pk_{n}") for n in ("sub", "sck", "step", "shift", "expd", "sm", "st", "sk", "waited"))
        parted, matched, pooled = sem("pk_parted"), sem("pk_matched"), sem("pk_pooled")
        hot, made, taken = sem("pg_hot"), sem("pg_made"), sem("pg_taken")
        gate_st = [sem(f"pg_st{i}") for i in range(2)]
        expert_made, idx_copied, dotted, dots_kept, dots_gelu, coefs, freed = (
            sem(f"g_{n}") for n in ("expert", "idx", "dotted", "kept", "gelu", "coef", "freed"))
        g_in = [sem(f"g_in{i}") for i in range(GRING)]
        block = ctx.enter_context(nc.Block())
        CHAIN = 17

        def pick_blocks(it, s):
            for b in range(PICK_B):
                j = s * PICK_B + b
                yield b, it * (2 * PICK_B) + j, it * PICK_B + j // 2, j % 2

        @block.sync
        def _(sp):
            def load_u(n, s):
                behind(sp, u_turn, n - 1)
                sp.dma_start(u_raw[:, s, :], dram["w_u"][0, bass.ds(n * P, P), :]).then_inc(u_in[s], 16)

            def store_act(n, s):
                sp.wait_ge(gelued, 2 * n + 2)
                sp.dma_start(scratch["acts"][bass.ds(n, 1)].rearrange("a p t -> (a p) t"), act_g[:, s, :]) \
                    .then_inc(act_st[s], 16)

            sp.dma_start(keys, dram["sub_keys"][0].rearrange("h c k d -> k (h c) d")).then_inc(load, 16)
            load_u(0, 0)
            load_u(1, 1)
            for s in range(2):
                sp.dma_start(q[s], scratch["pq"][:, :, s * P:(s + 1) * P]).then_inc(q_in[s], 16)

            def pick_turn(it):
                for s in range(2):
                    for b, n, half, k in pick_blocks(it, s):
                        load_u(n + 2, k)
                        store_act(n, k)
                        if b == 2 and not (isinstance(it, int) and it == TT // 2 - 1):
                            sp.wait_ge(sub_made, 4 * it + 2 * s + 2)
                            sp.dma_start(q[s], scratch["pq"][:, :, bass.ds((it * 2 + s + 2) * P, P)]) \
                                .then_inc(q_in[s], 16)

            pick_turn(0)
            with sp.Fori(1, TT // 2 - 1) as it:
                pick_turn(it)
            pick_turn(TT // 2 - 1)

            def store_gates(piece, p, part_):
                if part_ == 0:
                    behind(sp, taken, (piece + 1) * (PIECE_STEPS * SUBS))
                keys_ = slice(part_ * NK // PIECE_STEPS, (part_ + 1) * NK // PIECE_STEPS)
                at = piece * (NK * PIECE) + part_ * (NK * PIECE // PIECE_STEPS)
                sp.dma_start(scratch["gates"].rearrange("p a n -> p (a n)")[:, bass.ds(at, NK * PIECE // PIECE_STEPS)],
                             gates[p][:, keys_, :].rearrange("p k t -> p (k t)")).then_inc(gate_st[p], 16)

            def gate_turn(it):
                for j in range(8):
                    n = it * 8 + (N0_GATE + j)
                    load_u(n + 2, j % 2)
                    p = j // PIECE_STEPS
                    if not (isinstance(it, int) and it == 0 and p == 0):
                        store_gates(it * 2 + (p - 1), 1 - p, j % PIECE_STEPS)
                    store_act(n, j % 2)

            turns(sp, GATE_STEPS // 8, gate_turn)

            def rest_turn(it, last):
                for j in range(8):
                    n = it * 8 + (N0_REST + j)
                    if not (last and j >= 6):
                        load_u(n + 2, j % 2)
                    if isinstance(it, int) and it == 0 and j < PIECE_STEPS:
                        store_gates(N_PIECE - 1, 1, j)
                    store_act(n, j % 2)

            rest_turn(0, False)
            with sp.Fori(1, REST_STEPS // 8 - 1) as it:
                rest_turn(it, False)
            rest_turn(REST_STEPS // 8 - 1, True)
            for s in range(2):
                sp.wait_ge(act_st[s], 16 * NBLK // 2)
                sp.wait_ge(gate_st[s], 16 * PIECE_STEPS * N_PIECE // 2)

        @block.tensor
        def _(pe):
            def turn_u(n, half, s):
                pe.wait_ge(u_in[s], 16 * half + 16)
                behind(pe, u_kept, 2 * n)
                for c in range(KD):
                    tr = nc.tensor.transpose(u_turned[:, c, :], u_raw[:, s, c * P:(c + 1) * P], ident[:, :])
                tr.then_inc(u_turn, 1)

            def scores(n, s, between=lambda part_: None):
                pe.wait_ge(u_kept, 2 * n + 2)
                pe.wait_ge(ulo_made, n + 1)
                for half in range(2):
                    behind(pe, gelued, 2 * n - 1 + half)
                    cols = slice(GT * P + half * (TD // 2), GT * P + (half + 1) * (TD // 2))
                    for c in range(KD):
                        nc.tensor.matmul(score[half][:, :], u_hi[:, s, c, :], h_hi[:, c, cols], start=(c == 0), stop=False)
                        nc.tensor.matmul(score[half][:, :], u_hi[:, s, c, :], h_lo[:, c, cols], start=False, stop=False)
                        mm = nc.tensor.matmul(score[half][:, :], u_lo[:, s, c, :], h_hi[:, c, cols],
                                              start=False, stop=(c == KD - 1))
                        if c == KD - 1:
                            mm.then_inc(scored, 1)
                        if c % (KD // 2) == KD // 2 - 1:
                            between(2 * half + c // (KD // 2))

            def sub_scores(r, s, part_):
                behind(pe, sub_kept, 2 * r + part_)
                for g in range(NG // 2):
                    gg = part_ * (NG // 2) + g
                    mm = nc.tensor.matmul(sub[:, g, :], q[s][:, gg, :], keys_t[:, gg, :], start=True, stop=True)
                mm.then_inc(sub_made, 1)

            def turn_slots(r):
                pe.wait_ge(slot_made, r + 1)
                behind(pe, slot_kept, r)
                for n in range(3):
                    tr = nc.tensor.transpose(turned[:, n * P:(n + 1) * P], found[:, n, :], ident[:, :])
                tr.then_inc(slot_turned, 1)

            pe.wait_ge(load, 16)
            for part_ in range(2):
                if part_:
                    pe.wait_ge(keys_kept, 1)
                for g in range(NG // 2):
                    tr = nc.tensor.transpose(sub[:, g, :], keys[:, part_ * (NG // 2) + g, :], ident[:, :])
                tr.then_inc(keys_turned, 1)
            pe.wait_ge(keys_kept, 2)
            pe.wait_ge(q_in[0], 16)
            for part_ in range(2):
                sub_scores(0, 0, part_)
            turn_u(0, 0, 0)

            def pick_turn(it, last=False):
                for s in range(2):
                    r = it * 2 + s
                    for b, n, half, k in pick_blocks(it, s):
                        if b in (0, 2) and not (last and s == 1):
                            if b == 0:
                                pe.wait_ge(q_in[1 - s], 16 * it + (16 if s == 0 else 32))
                            sub_scores(r + 1, 1 - s, b // 2)
                        turn_u(n + 1, half + k, 1 - k)
                        scores(n, k)
                        if b == 2 and not (s == 0 and isinstance(it, int) and it == 0):
                            turn_slots(r - 1)

            pick_turn(0)
            with pe.Fori(1, TT // 2 - 1) as it:
                pick_turn(it)
            pick_turn(TT // 2 - 1, True)
            turn_slots(TT - 1)

            pe.wait_ge(slot_kept, TT)

            def gate_turn(it):
                for j in range(8):
                    def gates_of(i):
                        m = it * (8 * SUBS) + (j * SUBS + i)
                        pe.wait_ge(hot, m + 1)
                        behind(pe, taken, m - 1)
                        for t in range(SUB):
                            mm = nc.tensor.matmul(gate_ps[i % 2][:, t * NK:(t + 1) * NK], second[:, (i % 2) * SUB + t, :],
                                                  first[:, (i % 2) * SUB + t, :], start=True, stop=True)
                        mm.then_inc(made, 1)

                    n = it * 8 + (N0_GATE + j)
                    turn_u(n + 1, it * 4 + (N0_GATE + j) // 2 + j % 2, 1 - j % 2)
                    scores(n, j % 2, gates_of)

            turns(pe, GATE_STEPS // 8, gate_turn)

            def rest_turn(it, last):
                for j in range(8):
                    n = it * 8 + (N0_REST + j)
                    if not (last and j == 7):
                        turn_u(n + 1, it * 4 + (N0_REST + j) // 2 + j % 2, 1 - j % 2)
                    scores(n, j % 2)

            with pe.Fori(0, REST_STEPS // 8 - 1) as it:
                rest_turn(it, False)
            rest_turn(REST_STEPS // 8 - 1, True)

        @block.scalar
        def _(act):
            def split_u(n, s):
                act.wait_ge(u_turn, n + 1)
                behind(act, scored, 2 * n - 2)
                nc.scalar.activation(u_hi[:, s], u_turned[:, :, :], ACT.Copy, scale=S_U).then_inc(u_kept, 1)
                behind(act, ulo_made, n)
                nc.scalar.activation(u_scaled[:, :], u_turned[:, :, :].rearrange("p c n -> p (c n)"), ACT.Copy,
                                     scale=S_U).then_inc(u_kept, 1)

            def gelu(n, half, s, between=lambda part_: None):
                behind(act, act_st[s], half * 16)
                for hf in range(2):
                    between(2 * hf)
                    act.wait_ge(scored, 2 * n + (hf + 1))
                    nc.scalar.activation(act_g[:, s, hf * (TD // 2):(hf + 1) * (TD // 2)], score[hf][:, :],
                                         ACT.Gelu_apprx_tanh, scale=1.0 / (S_H * S_U)).then_inc(gelued, 1)
                    between(2 * hf + 1)

            def keep_sub(r, s, part_):
                act.wait_ge(sub_made, 2 * r + part_ + 1)
                behind(act, shifted, r - 1)
                nc.scalar.copy(sc[s][:, part_ * (NG // 2):(part_ + 1) * (NG // 2), :], sub[:, :, :]) \
                    .then_inc(sub_kept, 1)

            for part_ in range(2):
                act.wait_ge(keys_turned, part_ + 1)
                nc.scalar.copy(keys_t[:, part_ * (NG // 2):(part_ + 1) * (NG // 2), :], sub[:, :, :]).then_inc(keys_kept, 1)
            for part_ in range(2):
                keep_sub(0, 0, part_)
            split_u(0, 0)

            def pick_turn(it, last=False):
                for s in range(2):
                    r = it * 2 + s
                    for b, n, half, k in pick_blocks(it, s):
                        split_u(n + 1, 1 - k)
                        if b in (0, 2) and not (last and s == 1):
                            keep_sub(r + 1, 1 - s, b // 2)
                        if b == 4:
                            act.wait_ge(shifted, r + 1)
                            nc.scalar.activation(expo[:, :, :], expo[:, :, :], ACT.Exp).then_inc(expd, 1)
                        gelu(n, half, k)

            pick_turn(0)
            with act.Fori(1, TT // 2 - 1) as it:
                pick_turn(it)
            pick_turn(TT // 2 - 1, True)

            act.wait_ge(slot_kept, TT)

            def gate_turn(it):
                for j in range(8):
                    p = j // PIECE_STEPS

                    def take(i):
                        act.wait_ge(made, it * (8 * SUBS) + (j * SUBS + i + 1))
                        t = (j % PIECE_STEPS) * GATE_TOK + i * SUB
                        nc.scalar.copy(gates[p][:, :, t:t + SUB].rearrange("p a t -> p t a"),
                                       gate_ps[i % 2][:, :].rearrange("p (t a) -> p t a", t=SUB)).then_inc(taken, 1)

                    n = it * 8 + (N0_GATE + j)
                    split_u(n + 1, 1 - j % 2)
                    if j % PIECE_STEPS == 0:
                        behind(act, gate_st[p], it * (16 * PIECE_STEPS))
                    gelu(n, it * 4 + (N0_GATE + j) // 2, j % 2, take)

            turns(act, GATE_STEPS // 8, gate_turn)

            def rest_turn(it, last):
                for j in range(8):
                    n = it * 8 + (N0_REST + j)
                    if not (last and j == 7):
                        split_u(n + 1, 1 - j % 2)
                    gelu(n, it * 4 + (N0_REST + j) // 2, j % 2)

            with act.Fori(0, REST_STEPS // 8 - 1) as it:
                rest_turn(it, False)
            rest_turn(REST_STEPS // 8 - 1, True)
            act.wait_ge(dots_kept, NBLK // 8 - TT * PICK_B // 8)
            nc.scalar.activation(dots[:, :], dots[:, :], ACT.Gelu_apprx_tanh).then_inc(dots_gelu, 1)

        @block.gpsimd
        def _(pool):
            def low_half(n, s):
                pool.wait_ge(u_kept, 2 * n + 2)
                behind(pool, scored, 2 * n - 2)
                nc.gpsimd.tensor_tensor(u_lo[:, s].rearrange("p c n -> p (c n)"), u_scaled[:, :],
                                        u_hi[:, s].rearrange("p c n -> p (c n)"), ALU.subtract).then_inc(ulo_made, 1)

            low_half(0, 0)

            def pick_turn(it):
                for s in range(2):
                    r = it * 2 + s
                    for b, n, half, k in pick_blocks(it, s):
                        low_half(n + 1, 1 - k)
                        if b == 3:
                            pool.wait_ge(matched, r + 1)
                            nc.gpsimd.tensor_tensor(cand_rest[:, :, :, :], cand_rest[:, :, :, :],
                                                    idx_f[:, :, 1, None, :].broadcast_to([P, PH, TOPK, TOPK]),
                                                    ALU.mult).then_inc(pooled, 1)

            pick_turn(0)
            with pool.Fori(1, TT // 2) as it:
                pick_turn(it)
            pool.wait_ge(expert_made, 2)

            def gather(q0, count, first):
                for i in range(first, first + count):
                    behind(pool, dotted, q0 + (i - GRING + 1))
                    pool.sem_inc(freed, 1)
                    nc.gpsimd.indirect_dma_start(g_row[:, i % GRING, :], None, dram["w_u"][0],
                                                 bass.IndirectOffsetOnAxis(row_idx[:, i:i + 1], 0)) \
                        .then_inc(g_in[i % GRING], 16)

            def next_rows(turn_, q0, count):
                for i in range(GRING):
                    behind(pool, g_in[i], q0 * (16 // GRING))
                nc.gpsimd.tensor_copy(row_idx[:, 0:count], expert[:, bass.ds(q0, count)]).then_inc(idx_copied, 1)
                pool.wait_ge(idx_copied, turn_ + 1)

            def gather_turn(it, n0, q0, dots, last=False):
                at = 0
                for j in range(8):
                    if not (last and j == 7):
                        low_half(n0 + (j + 1), 1 - j % 2)
                    if j == 0:
                        next_rows(it + 1, q0, sum(dots))
                    gather(q0, dots[j], at)
                    at += dots[j]

            next_rows(0, 0, GRING)
            gather(0, GRING, 0)
            turns(pool, GATE_STEPS // 8,
                  lambda it: gather_turn(it, it * 8 + N0_GATE, it * TURN_DOTS[0] + GRING, [GATE_DOTS] * 8))

            def rest_turn(it, dots, last):
                gather_turn(it + GATE_STEPS // 8, it * 8 + N0_REST, it * TURN_DOTS[1] + (Q0 + GRING), dots, last)

            with pool.Fori(0, REST_STEPS // 8 - 1) as it:
                rest_turn(it, REST_DOTS * 4, False)
            assert GRING == REST_DOTS[1]
            rest_turn(REST_STEPS // 8 - 1, (REST_DOTS * 4)[:-1] + (0,), True)

        @block.vector
        def _(dve):
            def dot(q_, landed, j, tile, turn_):
                if j == 0:
                    behind(dve, dots_kept, turn_)
                dve.wait_ge(g_in[j % GRING], landed)
                behind(dve, dotted, q_ - 1)
                nc.vector.tensor_tensor_reduce(junk[:, j % 2, :], g_row[:, j % GRING, :], h_rows[:, tile, :], 1.0, 0.0,
                                               ALU.mult, ALU.add, dots_now[:, j:j + 1]).then_inc(dotted, 1)

            def keep_dots(q0, count):
                dve.wait_ge(dotted, q0 + count)
                nc.vector.tensor_copy(dots[:, bass.ds(q0, count)], dots_now[:, 0:count]).then_inc(dots_kept, 1)


            def pick(it, last=False):
                for s in range(2):
                    r = it * 2 + s
                    ch = Chain(dve, chain, r * CHAIN, waited)
                    v = val[:, :, :, :].rearrange("p h c k -> p (h c) k")
                    ix = idx[:, :, :, :].rearrange("p h c k -> p (h c) k")
                    dve.wait_ge(sub_kept, 2 * r + 2)
                    dve.sem_inc(waited, 1)
                    for g in range(NG):
                        op = nc.vector.max(v[:, g, 0:8], sc[s][:, g, :])
                    ch.wait_alone(op)
                    for g in range(NG):
                        nc.vector.max_index(ix[:, g, 0:8], v[:, g, 0:8], sc[s][:, g, :])
                        op = nc.vector.match_replace(rest[:, g, :], v[:, g, 0:8], sc[s][:, g, :], TAKEN)
                    ch.wait_alone(op)
                    for g in range(NG):
                        op = nc.vector.max(v[:, g, 8:16], rest[:, g, :])
                    ch.wait_alone(op)
                    for g in range(NG):
                        op = nc.vector.max_index(ix[:, g, 8:16], v[:, g, 8:16], rest[:, g, :])
                    ch.wait_alone(op)
                    nc.vector.tensor_copy(idx_f[:, :, :, :], idx[:, :, :, :])
                    ch.wait_alone(nc.vector.tensor_tensor(cand[:, :, :, :],
                                                          val[:, :, 0, :, None].broadcast_to([P, PH, TOPK, TOPK]),
                                                          val[:, :, 1, None, :].broadcast_to([P, PH, TOPK, TOPK]),
                                                          ALU.add))
                    c = cand[:, :, :, :].rearrange("p h a b -> p h (a b)")
                    cr = cand_rest[:, :, :, :].rearrange("p h a b -> p h (a b)")
                    for h in range(PH):
                        op = nc.vector.max(best[:, h, 0:8], c[:, h, :])
                    ch.wait_alone(op)
                    for h in range(PH):
                        nc.vector.max_index(best_i[:, h, 0:8], best[:, h, 0:8], c[:, h, :])
                        op = nc.vector.match_replace(cr[:, h, :], best[:, h, 0:8], c[:, h, :], TAKEN)
                    ch.wait_alone(op)
                    for h in range(PH):
                        op = nc.vector.max(best[:, h, 8:16], cr[:, h, :])
                    ch.wait_alone(op)
                    for h in range(PH):
                        nc.vector.max_index(best_i[:, h, 8:16], best[:, h, 8:16], cr[:, h, :])
                    nc.vector.tensor_tensor(expo[:, :, :], best[:, :, :],
                                            best[:, :, 0:1].broadcast_to([P, PH, TOPK]), ALU.subtract) \
                        .then_inc(shifted, 1)
                    dve.wait_ge(shifted, r + 1)
                    nc.vector.tensor_scalar(part_i[:, 0], best_i[:, :, :], 4, None, ALU.logical_shift_right)
                    ch.wait(nc.vector.tensor_scalar(part_i[:, 1], best_i[:, :, :], TOPK - 1, None, ALU.bitwise_and))
                    nc.vector.tensor_copy(part[:, :, :, :], part_i[:, :, :, :]).then_inc(parted, 1)
                    dve.wait_ge(parted, r + 1)
                    nc.vector.tensor_tensor(
                        cand_rest[:, :, :, :].rearrange("p h a b -> p (h a) b"),
                        part[:, 1].rearrange("p h k -> p (h k)")[:, :, None].broadcast_to([P, SLOTS, TOPK]),
                        iota[:, None, 0:TOPK].broadcast_to([P, SLOTS, TOPK]), ALU.is_equal).then_inc(matched, 1)
                    ch.wait(nc.vector.tensor_tensor(
                        cand[:, :, :, :].rearrange("p h a b -> p (h a) b"),
                        part[:, 0].rearrange("p h k -> p (h k)")[:, :, None].broadcast_to([P, SLOTS, TOPK]),
                        iota[:, None, 0:TOPK].broadcast_to([P, SLOTS, TOPK]), ALU.is_equal))
                    ch.wait(nc.vector.tensor_tensor(cand[:, :, :, :], cand[:, :, :, :],
                                                    idx_f[:, :, 0, None, :].broadcast_to([P, PH, TOPK, TOPK]), ALU.mult))
                    behind(dve, slot_turned, r)
                    nc.vector.tensor_reduce(found[:, 0, :], cand[:, :, :, :].rearrange("p h a b -> p (h a) b"),
                                            AX_X, ALU.add)
                    dve.wait_ge(expd, r + 1)
                    ch.wait(nc.vector.tensor_reduce(norm[:, 0, :], expo[:, :, :], AX_X, ALU.add))
                    ch.wait(nc.vector.reciprocal(norm[:, 1, :], norm[:, 0, :]))
                    nc.vector.tensor_tensor(found[:, 2, :].rearrange("p (h k) -> p h k", h=PH), expo[:, :, :],
                                                       norm[:, 1, :, None].broadcast_to([P, PH, TOPK]), ALU.mult)
                    dve.wait_ge(pooled, r + 1)
                    op = nc.vector.tensor_reduce(found[:, 1, :], cand_rest[:, :, :, :].rearrange("p h a b -> p (h a) b"),
                                                 AX_X, ALU.add)
                    op.then_inc(slot_made, 1)
                    dve.wait_ge(slot_made, r + 1)
                    if isinstance(it, int) and it == 0:
                        cols = slice(s * SLOTS, (s + 1) * SLOTS)
                        nc.vector.tensor_copy(g_gate[:, cols], found[:, 2, :])
                        nc.vector.scalar_tensor_tensor(expert[:, cols], found[:, 0, :], float(NK), found[:, 1, :],
                                                       ALU.mult, ALU.add).then_inc(expert_made, 1)
                        dve.wait_ge(expert_made, s + 1)
                    if not (s == 0 and isinstance(it, int) and it == 0):
                        keep_slots(r - 1)
                    assert ch.n <= CHAIN
                    dve.sem_inc(chain, CHAIN - ch.n)

            def keep_slots(r):
                dve.wait_ge(slot_turned, r + 1)
                nc.vector.tensor_copy(slot[:, :, bass.ds(r * P, P)],
                                      turned[:, 0:3 * P].rearrange("p (n t) -> p n t", n=3)).then_inc(slot_kept, 1)

            pick(0)
            with dve.Fori(1, TT // 2 - 1) as it:
                pick(it)
            pick(TT // 2 - 1, True)
            keep_slots(TT - 1)
            dve.wait_ge(slot_kept, TT)

            def slot_tile(q_):
                return q_ // SLOTS if isinstance(q_, int) else 0

            def gate_turn(it):
                for j in range(8):
                    for i in range(SUBS):
                        m = it * (8 * SUBS) + (j * SUBS + i)
                        behind(dve, made, m - 1)
                        for t in range(SUB):
                            tok = bass.ds(it * (8 * GATE_TOK) + (GT * P + j * GATE_TOK + i * SUB + t), 1)
                            at = (i % 2) * SUB + t
                            nc.vector.tensor_scalar(second[:, at, :], iota[:, :], slot[:, 1, tok], None, ALU.is_equal)
                            op = nc.vector.tensor_scalar(first[:, at, :], iota[:, :], slot[:, 0, tok], slot[:, 2, tok],
                                                         ALU.is_equal, ALU.mult)
                        op.then_inc(hot, 1)
                        if i >= SUBS - GATE_DOTS:
                            e = j * GATE_DOTS + i - (SUBS - GATE_DOTS)
                            q_ = it * TURN_DOTS[0] + e
                            dot(q_, it * (16 * TURN_DOTS[0] // GRING) + 16 * (e // GRING + 1), e, slot_tile(q_), it)
                keep_dots(it * TURN_DOTS[0], TURN_DOTS[0])

            assert GT == 2 and (GATE_STEPS // 8 - 1) * TURN_DOTS[0] <= SLOTS <= Q0
            gate_turn(0)
            with dve.Fori(1, GATE_STEPS // 8 - 1) as it:
                gate_turn(it)
            gate_turn(GATE_STEPS // 8 - 1)

            with dve.Fori(0, REST_STEPS // 8) as it:
                for e in range(TURN_DOTS[1]):
                    dot(it * TURN_DOTS[1] + (Q0 + e),
                        it * (16 * TURN_DOTS[1] // GRING) + 16 * ((Q0 + e) // GRING + 1), e, 1, it + GATE_STEPS // 8)
                keep_dots(it * TURN_DOTS[1] + Q0, TURN_DOTS[1])
            dve.wait_ge(dots_gelu, 1)
            nc.vector.scalar_tensor_tensor(coef[:, :], dots[:, :], S_A * S_V, g_gate[:, :], ALU.mult, ALU.mult) \
                .then_inc(coefs, 1)
            dve.wait_ge(coefs, 1)


def peer_outputs(nc, dram, scratch, coef, expert, gate_row, result):
    NB = 4
    TURN = 2 * NB
    N_TURN = NBLK // TURN
    BANKS = 2 * (TT - GT)
    DOTS = GQ // NBLK

    def rows_of(k):
        return range(k * DOTS, (k + 1) * DOTS)

    assert TURN * DOTS == GBATCH
    with ExitStack() as ctx:
        sb, ps, sem = ctx_tools(nc, ctx)
        x, y = sb("x_again", [P, TT, D]), sb("y_ffn", [P, TT, D])
        squares = sb("fn_sq", [P, D])
        sums, var, root, inv, tmp = (sb(f"fn_{n}", [P, TT]) for n in ("sum", "var", "root", "inv", "tmp"))
        v_raw = sb("xv_raw", [P, 2, D])
        v_hi, v_lo = sb("xv_hi", [P, 2, NB, D], F16), sb("xv_lo", [P, 2, NB, D], F16)
        gate = sb("xv_gate", [P, 2, N_PIECE, 2, PIECE])
        act_g = sb("xv_act", [P, 4, TD])
        a_hi, a_lo = sb("xa_hi", [P, 2, NB, TD], F16), sb("xa_lo", [P, 2, NB, TD], F16)
        row_idx = sb("gv_idx", [P, GBATCH], U32)
        g_row = sb("gv_row", [P, GRING, D])
        out = [ps(f"xo{i}", [P, BANK]) for i in range(8)]
        v_in, gate_in = [sem(f"xv_in{i}") for i in range(2)], [sem(f"xg_in{i}") for i in range(2)]
        act_in = [sem(f"xa_in{i}") for i in range(4)]
        gated, ahi_made, alo_made, vhi_made, vlo_made, mixed, added = (
            sem(f"xo_{n}") for n in ("gated", "ahi", "alo", "vhi", "vlo", "mixed", "added"))
        idx_copied, g_added, freed = sem("gv_idxc"), sem("gv_added"), sem("gv_freed")
        g_in = [sem(f"gv_in{i}") for i in range(GRING)]
        zeroed, x_in, squared, var_made, root_made, step, x_made, stored = (
            sem(f"fn_{n}") for n in ("zero", "xin", "sq", "var", "root", "step", "xm", "st"))
        batches = [slice(0, GT)] + [slice(t, t + 1) for t in range(GT, TT)]
        block = ctx.enter_context(nc.Block())

        @block.sync
        def _(sp):
            def turn(it):
                for k in range(TURN):
                    n, s = it * TURN + k, k % 2
                    behind(sp, vlo_made, n - 1)
                    sp.dma_start(v_raw[:, s, :], dram["w_v"][0, bass.ds(n * P, P), :]).then_inc(v_in[s], 16)
                    if s == 0:
                        behind(sp, gated, n - 2)
                        sp.dma_start(gate[:, (k // 2) % 2].rearrange("p a b t -> p a (b t)"),
                                     scratch["gates"][:, :, bass.ds((it * NB + k // 2) * 2 * PIECE, 2 * PIECE)]) \
                            .then_inc(gate_in[(k // 2) % 2], 16)
                    behind(sp, alo_made, n - 3)
                    sp.dma_start(act_g[:, k % 4, :], scratch["acts"][bass.ds(n, 1)].rearrange("a p t -> (a p) t")) \
                        .then_inc(act_in[k % 4], 16)

            turns(sp, N_TURN, turn)
            sp.dma_start(x[:, :, :], scratch["x_mid"].rearrange("(b p) d -> p b d", p=P)).then_inc(x_in, 16)
            for t in range(TT):
                sp.wait_ge(x_made, t + 1)
                sp.dma_start(result[t * P:(t + 1) * P, :], x[:, t, :]).then_inc(stored, 16)
            sp.wait_ge(stored, 16 * TT)

        @block.gpsimd
        def _(pool):
            def turn(it):
                nc.gpsimd.tensor_copy(row_idx[:, :], expert[:, bass.ds(it * GBATCH, GBATCH)]).then_inc(idx_copied, 1)
                for k in range(TURN):
                    n = it * TURN + k
                    pool.wait_ge(act_in[k % 4], it * (16 * TURN // 4) + 16 * (k // 4 + 1))
                    pool.wait_ge(gate_in[(k // 2) % 2], it * (16 * TURN // 4) + 16 * (k // 4 + 1))
                    g = gate[:, (k // 2) % 2, :, k % 2, :]
                    a = act_g[:, k % 4, :].rearrange("p (a t) -> p a t", t=PIECE)
                    nc.gpsimd.tensor_tensor(a, a, g, ALU.mult).then_inc(gated, 1)
                    if k == 0:
                        pool.wait_ge(idx_copied, it + 1)
                    for j in rows_of(k):
                        behind(pool, g_added, it * GBATCH + j - GRING + 1)
                        pool.sem_inc(freed, 1)
                        nc.gpsimd.indirect_dma_start(g_row[:, j % GRING, :], None, dram["w_v"][0],
                                                     bass.IndirectOffsetOnAxis(row_idx[:, j:j + 1], 0)) \
                            .then_inc(g_in[j % GRING], 16)
                pool.wait_ge(g_in[GRING - 1], it * (16 * GBATCH // GRING) + 16 * GBATCH // GRING)

            turns(pool, N_TURN, turn)

        @block.scalar
        def _(act):
            def turn(it):
                for k in range(TURN):
                    n, s, b, par = it * TURN + k, k % 2, k % NB, k // NB
                    if b == 0:
                        behind(act, mixed, it * (2 * BANKS) + (par - 1) * BANKS)
                    act.wait_ge(v_in[s], it * (16 * NB) + 16 * (k // 2 + 1))
                    nc.scalar.activation(v_hi[:, par, b, :], v_raw[:, s, :], ACT.Copy, scale=S_V).then_inc(vhi_made, 1)
                    act.wait_ge(gated, n + 1)
                    nc.scalar.activation(a_hi[:, par, b, :], act_g[:, k % 4, :], ACT.Copy, scale=S_A).then_inc(ahi_made, 1)

            turns(act, N_TURN, turn)
            for b, tiles in enumerate(batches):
                for t in range(tiles.start, tiles.stop):
                    if t < GT:
                        act.wait_ge(g_added, GQ)
                    else:
                        act.wait_ge(added, BANKS * (2 * N_TURN - 1) + 2 * (t - GT + 1))
                    behind(act, squared, t)
                    nc.scalar.activation(squares[:, :], y[:, t, :], ACT.Square, accum_out=sums[:, t:t + 1]) \
                        .then_inc(squared, 1)
                act.wait_ge(var_made, b + 1)
                nc.scalar.activation(root[:, tiles], var[:, tiles], ACT.Sqrt).then_inc(root_made, 1)

        @block.tensor
        def _(pe):
            def turn(it):
                for par in range(2):
                    g = it * 2 + par
                    pe.wait_ge(alo_made, g * NB + NB)
                    pe.wait_ge(vlo_made, g * NB + NB)
                    for t in range(TT - GT):
                        tile = par * (TT - GT) + t
                        m = g * BANKS + 2 * t
                        behind(pe, added, m - 6)
                        rows = slice(t * P, (t + 1) * P)
                        for b in range(NB):
                            for a, v, first, last in ((a_hi, v_hi, b == 0, False), (a_hi, v_lo, False, False),
                                                      (a_lo, v_hi, False, b == NB - 1)):
                                for half in range(2):
                                    mm = nc.tensor.matmul(out[2 * (tile % 4) + half][:, :], a[:, par, b, rows],
                                                          v[:, par, b, half * BANK:(half + 1) * BANK],
                                                          start=first, stop=last)
                                    if last:
                                        mm.then_inc(mixed, 1)

            turns(pe, N_TURN, turn)

        @block.vector
        def _(dve):
            def add(g, par, j):
                t, half = j // 2, j % 2
                cols = slice(half * BANK, (half + 1) * BANK)
                dve.wait_ge(mixed, g * BANKS + (j + 1))
                behind(dve, added, g * BANKS + (j + 1 - BANKS))
                nc.vector.tensor_tensor(y[:, GT + t, cols], out[2 * ((par * (TT - GT) + t) % 4) + half][:, :],
                                        y[:, GT + t, cols], ALU.add).then_inc(added, 1)

            def turn(it, tile=0):
                for k in range(TURN):
                    n, s, b, par = it * TURN + k, k % 2, k % NB, k // NB
                    if isinstance(it, int) and it == 0 and k == NB:
                        nc.vector.memset(y[:, 1:, :], 0.0).then_inc(zeroed, 1)
                        dve.wait_ge(zeroed, 2)
                    dve.wait_ge(vhi_made, n + 1)
                    nc.vector.scalar_tensor_tensor(v_lo[:, par, b, :], v_raw[:, s, :], S_V, v_hi[:, par, b, :],
                                                   ALU.mult, ALU.subtract).then_inc(vlo_made, 1)
                    dve.wait_ge(ahi_made, n + 1)
                    nc.vector.scalar_tensor_tensor(a_lo[:, par, b, :], act_g[:, k % 4, :], S_A, a_hi[:, par, b, :],
                                                   ALU.mult, ALU.subtract).then_inc(alo_made, 1)
                    for j in rows_of(k):
                        q_ = it * GBATCH + j
                        dve.wait_ge(g_in[j % GRING], it * (16 * GBATCH // GRING) + 16 * (j // GRING + 1))
                        behind(dve, g_added, q_)
                        nc.vector.scalar_tensor_tensor(y[:, tile, :], g_row[:, j % GRING, :], coef[:, bass.ds(q_, 1)],
                                                       y[:, tile, :], ALU.mult, ALU.add).then_inc(g_added, 1)
                    if not (par == 0 and isinstance(it, int) and it == 0):
                        for j in range(b * BANKS // NB, (b + 1) * BANKS // NB):
                            add(it * 2 + (par - 1), 1 - par, j)

            nc.vector.memset(y[:, 0, :], 0.0).then_inc(zeroed, 1)
            dve.wait_ge(zeroed, 1)
            turn(0)
            with dve.Fori(1, N_TURN // GT) as it:
                turn(it, 0)
            for tile in range(1, GT):
                with dve.Fori(tile * N_TURN // GT, (tile + 1) * N_TURN // GT) as it:
                    turn(it, tile)

            ch = Chain(dve, step)

            def mean(b):
                tiles = batches[b]
                dve.wait_ge(squared, tiles.stop)
                nc.vector.tensor_scalar(var[:, tiles], sums[:, tiles], 1.0 / D, EPS * (S_A * S_V) ** 2,
                                        ALU.mult, ALU.add).then_inc(var_made, 1)

            def finish(b):
                tiles = batches[b]
                dve.wait_ge(root_made, b + 1)
                dve.wait_ge(var_made, b + 1)
                ch.wait(nc.vector.reciprocal(inv[:, tiles], root[:, tiles]))
                ch.wait(nc.vector.tensor_tensor(tmp[:, tiles], inv[:, tiles], inv[:, tiles], ALU.mult))
                ch.wait(nc.vector.tensor_tensor(tmp[:, tiles], tmp[:, tiles], var[:, tiles], ALU.mult))
                ch.wait(nc.vector.tensor_scalar(tmp[:, tiles], tmp[:, tiles], -0.5, 1.5, ALU.mult, ALU.add))
                ch.wait(nc.vector.tensor_tensor(inv[:, tiles], inv[:, tiles], tmp[:, tiles], ALU.mult))
                for t in range(tiles.start, tiles.stop):
                    ch.wait(nc.vector.scalar_tensor_tensor(y[:, t, :], y[:, t, :], inv[:, t:t + 1], gate_row[:, :],
                                                           ALU.mult, ALU.mult))
                    dve.wait_ge(x_in, 16)
                    nc.vector.tensor_tensor(x[:, t, :], x[:, t, :], y[:, t, :], ALU.add).then_inc(x_made, 1)

            for b in range(len(batches)):
                mean(b)
                if b + 1 < len(batches):
                    for half in range(2):
                        add(2 * N_TURN - 1, 1, 2 * b + half)
                finish(b)


def build(nc, dram, out):
    scratch = {
        "qk_fox": nc.dram_tensor("qk_fox", [2 * FOX_H, AUG, T], F32, kind="Internal").ap(),
        "qk_swa": nc.dram_tensor("qk_swa", [SWA_H + SWA_KV, HD, T], F32, kind="Internal").ap(),
        "v": nc.dram_tensor("v_all", [T, V_W], F32, kind="Internal").ap(),
        "mix": nc.dram_tensor("mix", [T, D], F32, kind="Internal").ap(),
        "x_mid": nc.dram_tensor("x_mid", [T, D], F32, kind="Internal").ap(),
        "pq": nc.dram_tensor("pq", [P, NG, T], F32, kind="Internal").ap(),
        "acts": nc.dram_tensor("acts", [NBLK, P, TD], F32, kind="Internal").ap(),
        "gates": nc.dram_tensor("gates", [NK, N_PIECE, NK * PIECE], F32, kind="Internal").ap(),
    }
    with ExitStack() as ctx:
        sb, _, _ = ctx_tools(nc, ctx)
        ident, iota = sb("ident", [P, P]), sb("iota", [P, P])
        gate2 = sb("gate2", [P, D])
        coef, expert = sb("g_coef", [P, GQ]), sb("g_expert", [P, GQ], U32)
        turned_h = ctx.enter_context(ExitStack())
        hsb, _, _ = ctx_tools(nc, turned_h)
        h_hi, h_lo = hsb("h_hi", [P, KD, T], F16), hsb("h_lo", [P, KD, T], F16)
        h_rows = hsb("h_rows", [P, GT, D])
        kept = {"ident": ident, "iota": iota}
        with ExitStack() as front:
            fsb, _, _ = ctx_tools(nc, front)
            causal, mod, x = fsb("causal", [P, P]), fsb("mod", [P, N_MOD * D]), fsb("x_sb", [P, TT, D])
            kept |= {"causal": causal, "mod": mod, "x": x, "x_inv": fsb("x_inv", [P, TT])}
            modulation(nc, dram, kept)
            row = [mod[:, i * D:(i + 1) * D] for i in range(N_MOD)]
            norm_and_turn(nc, kept, row[1], row[0], h_hi, h_lo)
            project_in(nc, dram, scratch, kept, h_hi, h_lo)
            fox_attention(nc, scratch, kept)
            swa_attention(nc, dram, scratch, kept)
            project_out(nc, dram, scratch, kept, (row[2], row[4], row[3], row[5]), gate2, h_hi, h_lo, h_rows)
            peer_queries(nc, dram, scratch, h_hi, h_lo)
        peer_scores(nc, dram, scratch, kept, h_hi, h_lo, h_rows, coef, expert)
        turned_h.close()
        peer_outputs(nc, dram, scratch, coef, expert, gate2, out[0])


def constants():
    r = np.arange(P)
    dist = r[:, None] + P - np.arange(2 * P)[None, :]
    slopes = 2.0 ** (-8.0 * np.arange(1, SWA_H + 1) / SWA_H)
    bias = np.where(((dist >= 0) & (dist < P))[:, None, :], -slopes[None, :, None] * dist[:, None, :], NEG)
    return {
        "ident": np.eye(P, dtype=np.float32),
        "iota": np.ascontiguousarray(np.broadcast_to(r.astype(np.float32), (P, P))),
        "causal": np.where(r[None, :] <= r[:, None], 0.0, NEG).astype(np.float32),
        "swa_bias": bias.astype(np.float32),
    }


_INS = ["x", "c", "w_ada", "b_ada", "g_pre_mix", "g_post_mix", "g_pre_ffn", "g_post_ffn", "w_in", "b_fgate",
        "swa_sinks", "w_out", "w_query", "sub_keys", "w_u", "w_v"]


def declare(nc, arrays):
    dram = {name: nc.dram_tensor(f"in_{name}", list(a.shape), F32, kind="ExternalInput").ap()
            for name, a in arrays.items()}
    build(nc, dram, nc.dram_tensor("out", [1, T, D], F32, kind="ExternalOutput").ap())


def kernel(**inputs):
    import concourse.bacc as bacc
    from concourse.bass_utils import run_bass_kernel_spmd as run

    arrays = {name: np.ascontiguousarray(inputs[name]) for name in _INS}
    arrays.update(constants())
    nc = bacc.Bacc("TRN2", target_bir_lowering=False, num_devices=1)
    declare(nc, arrays)
    r = run(nc, [{f"in_{name}": a for name, a in arrays.items()}], core_ids=[0])
    return r.results[0]["out"]
```
